# Optimizing a Trainium2 kernel written in Bass

```python
import math
import jax, jax.numpy as jnp
from jax import lax
import numpy as np

D_MODEL = 1024
BATCH = 1
SEQ = 1024
DEPTH = 1

ATT_HEADS = 16
ATT_HEAD_DIM = 64
KV_LATENT = 128
IDX_HEADS = 8
IDX_DIM = 64
TOPK_MAX = 256
Q_BLOCK = 128
REL_BUCKETS = 32
REL_MAX_DIST = 128
SSM_INNER = 2 * D_MODEL
SSM_HEAD_DIM = 64
SSM_HEADS = SSM_INNER // SSM_HEAD_DIM
SSM_GROUPS = 4
SSM_HEADS_PER_GROUP = SSM_HEADS // SSM_GROUPS
SSM_STATE = 128
SSM_CONV = 4
SSM_CHUNK = 128
SSM_XBC = SSM_INNER + 2 * SSM_GROUPS * SSM_STATE
FFN_DIM = 2816
FFN_CONV = 3
EPS = 1e-6

IN_SPLITS = (
    ATT_HEADS * ATT_HEAD_DIM,
    KV_LATENT,
    IDX_HEADS * IDX_DIM,
    IDX_DIM,
    IDX_HEADS,
    SSM_INNER,
    SSM_XBC,
    SSM_HEADS,
    D_MODEL,
    D_MODEL,
)
IN_COLS = sum(IN_SPLITS)


def split_cols(a, sizes):
    idx, acc = [], 0
    for sz in sizes[:-1]:
        acc += sz
        idx.append(acc)
    return jnp.split(a, idx, axis=-1)

def rmsnorm(x, g):
    x32 = x.astype(jnp.float32)
    y = x32 * lax.rsqrt(jnp.mean(x32 * x32, axis=-1, keepdims=True) + EPS)
    return (y * g.astype(jnp.float32)).astype(x.dtype)

def causal_depthwise_conv(u, w, bias):
    k, ch = w.shape
    out = lax.conv_general_dilated(
        u, w[:, None, :].astype(u.dtype), window_strides=(1,), padding=[(k - 1, 0)],
        dimension_numbers=("NWC", "WIO", "NWC"), feature_group_count=ch)
    return out + bias.astype(u.dtype)

def t5_bucket(dist):
    n = jnp.maximum(dist, 0)
    max_exact = REL_BUCKETS // 2
    large = max_exact + (jnp.log(jnp.maximum(n, 1).astype(jnp.float32) / max_exact)
                         / math.log(REL_MAX_DIST / max_exact)
                         * (REL_BUCKETS - max_exact)).astype(jnp.int32)
    large = jnp.minimum(large, REL_BUCKETS - 1)
    return jnp.where(n < max_exact, n, large)

def dsa_attention(q_lat, c_kv, q_idx, k_idx, w_idx, rel_bias):
    b, s, h, c = q_lat.shape
    n_sel = min(TOPK_MAX, s // 4)
    nblk = s // Q_BLOCK
    scale = ATT_HEAD_DIM ** -0.5
    key_pos = jnp.arange(s)
    gather = jax.vmap(lambda table, idx: table[idx])

    def to_blocks(a):
        return a.reshape(b, nblk, Q_BLOCK, *a.shape[2:]).swapaxes(0, 1)

    def block(args):
        qb, qib, wib, blk = args
        q_pos = blk * Q_BLOCK + jnp.arange(Q_BLOCK)
        causal = key_pos[None, :] <= q_pos[:, None]
        idx_logits = jnp.einsum("bqhd,bsd->bqhs", qib, k_idx,
                                preferred_element_type=jnp.float32)
        score = jnp.einsum("bqhs,bqh->bqs", jax.nn.relu(idx_logits),
                           wib.astype(jnp.float32))
        score = jnp.where(causal[None], score, -jnp.inf)
        _, sel = lax.top_k(score, n_sel)
        c_sel = gather(c_kv, sel)
        logits = jnp.einsum("bqhc,bqkc->bhqk", qb, c_sel,
                            preferred_element_type=jnp.float32) * scale
        dist = q_pos[None, :, None] - sel
        bias = rel_bias[t5_bucket(dist)]
        logits = logits + jnp.moveaxis(bias, -1, 1).astype(jnp.float32)
        logits = jnp.where((dist >= 0)[:, None], logits, -jnp.inf)
        p = jax.nn.softmax(logits, axis=-1).astype(c_sel.dtype)
        return jnp.einsum("bhqk,bqkc->bqhc", p, c_sel)

    out = lax.map(block, (to_blocks(q_lat), to_blocks(q_idx), to_blocks(w_idx),
                          jnp.arange(nblk)))
    return out.swapaxes(0, 1).reshape(b, s, h, c)

def ssd_scan(xh, dt, a, bmat, cmat):
    b, l, g, r, p = xh.shape
    n = bmat.shape[-1]
    q = SSM_CHUNK
    nc = l // q
    f32 = jnp.float32
    x = (xh.astype(f32) * dt[..., None]).reshape(b, nc, q, g, r, p)
    adt = (dt * a).reshape(b, nc, q, g, r)
    bm = bmat.astype(f32).reshape(b, nc, q, g, n)
    cm = cmat.astype(f32).reshape(b, nc, q, g, n)
    a_cum = jnp.cumsum(adt, axis=2)
    tri = jnp.tril(jnp.ones((q, q), dtype=bool))
    seg = a_cum[:, :, :, None] - a_cum[:, :, None, :]
    decay = jnp.exp(jnp.where(tri[None, None, :, :, None, None], seg, -jnp.inf))
    cb = jnp.einsum("bclgn,bcsgn->bclsg", cm, bm)
    y_diag = jnp.einsum("bclsgr,bcsgrp->bclgrp", cb[..., None] * decay, x)
    decay_states = jnp.exp(a_cum[:, :, -1:] - a_cum)
    states = jnp.einsum("bclgn,bclgrp->bcgrpn", bm, x * decay_states[..., None])
    chunk_decay = jnp.exp(a_cum[:, :, -1])

    def step(hstate, inp):
        st, dec = inp
        return hstate * dec[..., None, None] + st, hstate

    h0 = jnp.zeros((b, g, r, p, n), f32)
    _, prev = lax.scan(step, h0, (states.swapaxes(0, 1), chunk_decay.swapaxes(0, 1)))
    prev = prev.swapaxes(0, 1)
    y_off = jnp.einsum("bclgn,bcgrpn->bclgrp", cm, prev) * jnp.exp(a_cum)[..., None]
    return (y_diag + y_off).reshape(b, l, g, r, p)

def gated_group_rmsnorm(y, z, g):
    u = y.astype(jnp.float32) * jax.nn.silu(z.astype(jnp.float32))
    b, l, c = u.shape
    u = u.reshape(b, l, SSM_GROUPS, c // SSM_GROUPS)
    u = u * lax.rsqrt(jnp.mean(u * u, axis=-1, keepdims=True) + EPS)
    return (u.reshape(b, l, c) * g.astype(jnp.float32)).astype(z.dtype)

def first_inputs(seed: int = 0) -> dict:
    key = jax.random.key(seed)
    ks = jax.random.split(key, 24)
    f32 = jnp.float32

    def nrm(k, shape, scale):
        return jax.random.normal(k, shape, f32) * scale

    def gain(k, shape):
        return 1.0 + 0.05 * jax.random.normal(k, shape, f32)

    dt0 = jnp.exp(jax.random.uniform(ks[8], (DEPTH, SSM_HEADS), f32,
                                     math.log(1e-3), math.log(1e-1)))
    dt_bias = dt0 + jnp.log(-jnp.expm1(-dt0))
    return {
        "x": nrm(ks[0], (BATCH, SEQ, D_MODEL), 1.0),
        "rel_bias": nrm(ks[1], (REL_BUCKETS, ATT_HEADS), 0.5),
        "norm_mix": gain(ks[2], (DEPTH, D_MODEL)),
        "w_in": nrm(ks[3], (DEPTH, D_MODEL, IN_COLS), D_MODEL ** -0.5),
        "kv_norm": gain(ks[4], (DEPTH, KV_LATENT)),
        "w_uk": nrm(ks[5], (DEPTH, ATT_HEADS, ATT_HEAD_DIM, KV_LATENT), ATT_HEAD_DIM ** -0.5),
        "w_uv": nrm(ks[6], (DEPTH, ATT_HEADS, ATT_HEAD_DIM, KV_LATENT), KV_LATENT ** -0.5),
        "conv_ssm_w": nrm(ks[7], (DEPTH, SSM_CONV, SSM_XBC), SSM_CONV ** -0.5),
        "conv_ssm_b": nrm(ks[9], (DEPTH, SSM_XBC), 0.01),
        "dt_bias": dt_bias,
        "a_log": jnp.log(jax.random.uniform(ks[10], (DEPTH, SSM_HEADS), f32, 1.0, 16.0)),
        "d_skip": 1.0 + 0.1 * jax.random.normal(ks[11], (DEPTH, SSM_HEADS), f32),
        "ssm_norm": gain(ks[12], (DEPTH, SSM_INNER)),
        "w_att_out": nrm(ks[13], (DEPTH, ATT_HEADS * ATT_HEAD_DIM, D_MODEL),
                         (ATT_HEADS * ATT_HEAD_DIM) ** -0.5),
        "w_ssm_out": nrm(ks[14], (DEPTH, SSM_INNER, D_MODEL), SSM_INNER ** -0.5),
        "w_out": nrm(ks[15], (DEPTH, D_MODEL, D_MODEL), D_MODEL ** -0.5),
        "norm_ffn": gain(ks[16], (DEPTH, D_MODEL)),
        "w_ffn_up": nrm(ks[17], (DEPTH, D_MODEL, 2 * FFN_DIM), D_MODEL ** -0.5),
        "conv_ffn_w": nrm(ks[18], (DEPTH, FFN_CONV, 2 * FFN_DIM), FFN_CONV ** -0.5),
        "conv_ffn_b": nrm(ks[19], (DEPTH, 2 * FFN_DIM), 0.01),
        "w_ffn_down": nrm(ks[20], (DEPTH, FFN_DIM, D_MODEL), FFN_DIM ** -0.5),
        "norm_final": gain(ks[21], (D_MODEL,)),
    }

def first_block(x, rel_bias, norm_mix, w_in, kv_norm, w_uk, w_uv, conv_ssm_w, conv_ssm_b,
              dt_bias, a_log, d_skip, ssm_norm, w_att_out, w_ssm_out, w_out, norm_ffn,
              w_ffn_up, conv_ffn_w, conv_ffn_b, w_ffn_down, norm_final):
    b, s, _ = x.shape
    for layer in range(DEPTH):
        h = rmsnorm(x, norm_mix[layer])
        proj = h @ w_in[layer]
        (q, c_raw, q_idx, k_idx, w_idx, z, xbc, dt_raw, g_att, g_ssm) = split_cols(proj, IN_SPLITS)

        q = q.reshape(b, s, ATT_HEADS, ATT_HEAD_DIM)
        q_lat = jnp.einsum("bshd,hdc->bshc", q, w_uk[layer])
        c_kv = rmsnorm(c_raw, kv_norm[layer])
        att_lat = dsa_attention(q_lat, c_kv,
                                q_idx.reshape(b, s, IDX_HEADS, IDX_DIM), k_idx, w_idx,
                                rel_bias)
        att = jnp.einsum("bshc,hdc->bshd", att_lat, w_uv[layer])
        y_att = att.reshape(b, s, ATT_HEADS * ATT_HEAD_DIM) @ w_att_out[layer]

        xbc = jax.nn.silu(causal_depthwise_conv(xbc, conv_ssm_w[layer], conv_ssm_b[layer]))
        xs, bm, cm = split_cols(xbc, (SSM_INNER, SSM_GROUPS * SSM_STATE, SSM_GROUPS * SSM_STATE))
        dt = jax.nn.softplus(dt_raw.astype(jnp.float32) + dt_bias[layer].astype(jnp.float32))
        a = -jnp.exp(a_log[layer].astype(jnp.float32))
        xh = xs.reshape(b, s, SSM_GROUPS, SSM_HEADS_PER_GROUP, SSM_HEAD_DIM)
        y = ssd_scan(xh,
                     dt.reshape(b, s, SSM_GROUPS, SSM_HEADS_PER_GROUP),
                     a.reshape(SSM_GROUPS, SSM_HEADS_PER_GROUP),
                     bm.reshape(b, s, SSM_GROUPS, SSM_STATE),
                     cm.reshape(b, s, SSM_GROUPS, SSM_STATE))
        y = y + d_skip[layer].astype(jnp.float32).reshape(
            SSM_GROUPS, SSM_HEADS_PER_GROUP)[..., None] * xh.astype(jnp.float32)
        y = gated_group_rmsnorm(y.reshape(b, s, SSM_INNER), z, ssm_norm[layer])
        y_ssm = y @ w_ssm_out[layer]

        merged = jax.nn.sigmoid(g_att) * y_att + jax.nn.sigmoid(g_ssm) * y_ssm
        x = x + merged @ w_out[layer]

        h = rmsnorm(x, norm_ffn[layer])
        u = causal_depthwise_conv(h @ w_ffn_up[layer], conv_ffn_w[layer], conv_ffn_b[layer])
        gate, val = jnp.split(u, 2, axis=-1)
        x = x + (jax.nn.silu(gate) * val) @ w_ffn_down[layer]
    return rmsnorm(x, norm_final)


MEM_TOKENS = 256
ROPE_THETA = 10000.0
RMS_EPS = 1e-6
NEG_INF = -1e30

MLA_HEADS = 8
Q_LORA = 256
KV_LORA = 128
MLA_NOPE = 64
MLA_ROPE = 32
MLA_QK = MLA_NOPE + MLA_ROPE
MLA_V = 64
MLA_W = MLA_HEADS * MLA_V

DIFF_HEADS = 4
DIFF_D = 32
DIFF_V = 2 * DIFF_D
DIFF_W = DIFF_HEADS * DIFF_V

MEM_HEADS = 4
MEM_D = 64
MEM_W = MEM_HEADS * MEM_D

D_MIX = MLA_W + DIFF_W + MEM_W

IN_SPLITS_2 = [
    Q_LORA,
    KV_LORA,
    MLA_ROPE,
    DIFF_HEADS * 2 * DIFF_D,
    DIFF_HEADS * 2 * DIFF_D,
    DIFF_W,
    MEM_W,
    D_MIX,
]
D_IN = int(sum(IN_SPLITS_2))
IN_OFFSETS = [int(v) for v in np.cumsum(IN_SPLITS_2)[:-1]]


def rms_norm(x, g, eps=RMS_EPS):
    xf = x.astype(jnp.float32)
    y = xf * lax.rsqrt(jnp.mean(xf * xf, axis=-1, keepdims=True) + eps)
    return (y * g.astype(jnp.float32)).astype(x.dtype)

def rope(x, pos):
    d = x.shape[-1]
    inv = ROPE_THETA ** (-jnp.arange(0, d, 2, dtype=jnp.float32) / d)
    ang = pos.astype(jnp.float32)[..., None] * inv
    cos = jnp.cos(ang)[:, :, None, :]
    sin = jnp.sin(ang)[:, :, None, :]
    xf = x.astype(jnp.float32)
    x1, x2 = xf[..., : d // 2], xf[..., d // 2:]
    out = jnp.concatenate([x1 * cos - x2 * sin, x2 * cos + x1 * sin], axis=-1)
    return out.astype(x.dtype)

def causal_mask(start, s_len):
    q_idx = start + jnp.arange(Q_BLOCK, dtype=jnp.int32)
    return jnp.arange(s_len, dtype=jnp.int32)[None, :] <= q_idx[:, None]

def causal_block_sweep(block_fn, q):
    b, s = q.shape[0], q.shape[1]
    nb = s // Q_BLOCK
    qb = jnp.moveaxis(q.reshape((b, nb, Q_BLOCK) + q.shape[2:]), 1, 0)
    starts = jnp.arange(nb, dtype=jnp.int32) * Q_BLOCK
    out = lax.map(lambda a: block_fn(a[0], a[1]), (qb, starts))
    return jnp.moveaxis(out, 0, 1).reshape((b, s) + out.shape[3:])

def mla_branch(cq, ckv, kr, pos, q_norm_g, kv_norm_g, w_uq, w_ukv, qn_g, kn_g):
    b, s, _ = cq.shape
    q = (rms_norm(cq, q_norm_g) @ w_uq).reshape(b, s, MLA_HEADS, MLA_QK)
    kv = (rms_norm(ckv, kv_norm_g) @ w_ukv).reshape(b, s, MLA_HEADS, MLA_NOPE + MLA_V)
    k_nope, v = kv[..., :MLA_NOPE], kv[..., MLA_NOPE:]
    k_rope = jnp.broadcast_to(kr.reshape(b, s, 1, MLA_ROPE), (b, s, MLA_HEADS, MLA_ROPE))
    k = jnp.concatenate([k_nope, k_rope], axis=-1)
    q = rms_norm(q, qn_g)
    k = rms_norm(k, kn_g)
    q = jnp.concatenate([q[..., :MLA_NOPE], rope(q[..., MLA_NOPE:], pos)], axis=-1)
    k = jnp.concatenate([k[..., :MLA_NOPE], rope(k[..., MLA_NOPE:], pos)], axis=-1)
    scale = 1.0 / math.sqrt(MLA_QK)

    def block_fn(qblk, start):
        sc = jnp.einsum('bqhd,bkhd->bhqk', qblk, k).astype(jnp.float32) * scale
        sc = jnp.where(causal_mask(start, s)[None, None], sc, NEG_INF)
        p = jax.nn.softmax(sc, axis=-1).astype(v.dtype)
        return jnp.einsum('bhqk,bkhd->bqhd', p, v)

    o = causal_block_sweep(block_fn, q)
    return o.reshape(b, s, MLA_W)

def diff_branch(dq, dk, dv, pos, qn_g, kn_g, lam_vecs, subln_g, lam_init):
    b, s, _ = dq.shape
    q = rms_norm(dq.reshape(b, s, DIFF_HEADS * 2, DIFF_D), qn_g)
    k = rms_norm(dk.reshape(b, s, DIFF_HEADS * 2, DIFF_D), kn_g)
    q = rope(q, pos).reshape(b, s, DIFF_HEADS, 2, DIFF_D)
    k = rope(k, pos).reshape(b, s, DIFF_HEADS, 2, DIFF_D)
    v = dv.reshape(b, s, DIFF_HEADS, DIFF_V)
    lv = lam_vecs.astype(jnp.float32)
    lam = jnp.exp(jnp.sum(lv[0] * lv[1])) - jnp.exp(jnp.sum(lv[2] * lv[3])) + lam_init
    scale = 1.0 / math.sqrt(DIFF_D)

    def block_fn(qblk, start):
        sc = jnp.einsum('bqhmd,bkhmd->bhmqk', qblk, k).astype(jnp.float32) * scale
        sc = jnp.where(causal_mask(start, s)[None, None, None], sc, NEG_INF)
        p = jax.nn.softmax(sc, axis=-1)
        a = (p[:, :, 0] - lam * p[:, :, 1]).astype(v.dtype)
        return jnp.einsum('bhqk,bkhd->bqhd', a, v)

    o = causal_block_sweep(block_fn, q)
    o = rms_norm(o, subln_g) * (1.0 - lam_init)
    return o.reshape(b, s, DIFF_W)

def mem_branch(mq, mem, mem_norm_g, w_mem_kv, qn_g, kn_g):
    b, s, _ = mq.shape
    m = mem.shape[1]
    kv = rms_norm(mem, mem_norm_g) @ w_mem_kv
    k = rms_norm(kv[..., :MEM_W].reshape(b, m, MEM_HEADS, MEM_D), kn_g)
    v = kv[..., MEM_W:].reshape(b, m, MEM_HEADS, MEM_D)
    q = rms_norm(mq.reshape(b, s, MEM_HEADS, MEM_D), qn_g)
    sc = jnp.einsum('bshd,bmhd->bhsm', q, k).astype(jnp.float32) / math.sqrt(MEM_D)
    p = jax.nn.softmax(sc, axis=-1).astype(v.dtype)
    o = jnp.einsum('bhsm,bmhd->bshd', p, v)
    return o.reshape(b, s, MEM_W)

def second_inputs(seed: int = 0) -> dict:
    key = jax.random.key(seed)
    ks = jax.random.split(key, 24)
    f32 = jnp.float32

    def nrm(k, shape, fan_in):
        return jax.random.normal(k, shape, f32) * (fan_in ** -0.5)

    def gain(k, shape):
        return 1.0 + 0.01 * jax.random.normal(k, shape, f32)

    x = jax.random.normal(ks[0], (BATCH, SEQ, D_MODEL), f32)
    mem = jax.random.normal(ks[1], (BATCH, MEM_TOKENS, D_MODEL), f32)
    offsets = jax.random.randint(ks[2], (BATCH, 1), 0, 4096, dtype=jnp.int32)
    positions = offsets + jnp.arange(SEQ, dtype=jnp.int32)[None, :]
    return {
        "x": x,
        "mem": mem,
        "positions": positions,
        "norm_g": gain(ks[3], (DEPTH, D_MODEL)),
        "w_in": nrm(ks[4], (DEPTH, D_MODEL, D_IN), D_MODEL),
        "mla_q_norm_g": gain(ks[5], (DEPTH, Q_LORA)),
        "mla_kv_norm_g": gain(ks[6], (DEPTH, KV_LORA)),
        "w_uq": nrm(ks[7], (DEPTH, Q_LORA, MLA_HEADS * MLA_QK), Q_LORA),
        "w_ukv": nrm(ks[8], (DEPTH, KV_LORA, MLA_HEADS * (MLA_NOPE + MLA_V)), KV_LORA),
        "mla_qn_g": gain(ks[9], (DEPTH, MLA_QK)),
        "mla_kn_g": gain(ks[10], (DEPTH, MLA_QK)),
        "diff_qn_g": gain(ks[11], (DEPTH, DIFF_D)),
        "diff_kn_g": gain(ks[12], (DEPTH, DIFF_D)),
        "diff_lambda": 0.1 * jax.random.normal(ks[13], (DEPTH, 4, DIFF_D), f32),
        "diff_subln_g": gain(ks[14], (DEPTH, DIFF_V)),
        "mem_norm_g": gain(ks[15], (DEPTH, D_MODEL)),
        "w_mem_kv": nrm(ks[16], (DEPTH, D_MODEL, 2 * MEM_W), D_MODEL),
        "mem_qn_g": gain(ks[17], (DEPTH, MEM_D)),
        "mem_kn_g": gain(ks[18], (DEPTH, MEM_D)),
        "w_out": nrm(ks[19], (DEPTH, D_MIX, D_MODEL), D_MIX),
    }

def second_block(x, mem, positions, norm_g, w_in, mla_q_norm_g, mla_kv_norm_g, w_uq, w_ukv,
              mla_qn_g, mla_kn_g, diff_qn_g, diff_kn_g, diff_lambda, diff_subln_g,
              mem_norm_g, w_mem_kv, mem_qn_g, mem_kn_g, w_out):
    for l in range(DEPTH):
        lam_init = 0.8 - 0.6 * math.exp(-0.3 * l)
        h = rms_norm(x, norm_g[l])
        proj = h @ w_in[l]
        cq, ckv, kr, dq, dk, dv, mq, z = jnp.split(proj, IN_OFFSETS, axis=-1)
        y_mla = mla_branch(cq, ckv, kr, positions, mla_q_norm_g[l], mla_kv_norm_g[l],
                           w_uq[l], w_ukv[l], mla_qn_g[l], mla_kn_g[l])
        y_diff = diff_branch(dq, dk, dv, positions, diff_qn_g[l], diff_kn_g[l],
                             diff_lambda[l], diff_subln_g[l], lam_init)
        y_mem = mem_branch(mq, mem, mem_norm_g[l], w_mem_kv[l], mem_qn_g[l], mem_kn_g[l])
        y = jnp.concatenate([y_mla, y_diff, y_mem], axis=-1) * jax.nn.silu(z)
        x = x + y @ w_out[l]
    return x


def setup_inputs(seed=0):
    out = dict(first_inputs(seed))
    for name, value in second_inputs(seed + 1).items():
        if name != "x":
            out[name + "_2"] = value
    return out


def reference(
    x, rel_bias, norm_mix, w_in, kv_norm, w_uk, w_uv, conv_ssm_w, conv_ssm_b, dt_bias, a_log,
    d_skip, ssm_norm, w_att_out, w_ssm_out, w_out, norm_ffn, w_ffn_up, conv_ffn_w, conv_ffn_b,
    w_ffn_down, norm_final, mem_2, positions_2, norm_g_2, w_in_2, mla_q_norm_g_2,
    mla_kv_norm_g_2, w_uq_2, w_ukv_2, mla_qn_g_2, mla_kn_g_2, diff_qn_g_2, diff_kn_g_2,
    diff_lambda_2, diff_subln_g_2, mem_norm_g_2, w_mem_kv_2, mem_qn_g_2, mem_kn_g_2, w_out_2,
):
    x = first_block(
        x, rel_bias, norm_mix, w_in, kv_norm, w_uk, w_uv, conv_ssm_w, conv_ssm_b, dt_bias,
        a_log, d_skip, ssm_norm, w_att_out, w_ssm_out, w_out, norm_ffn, w_ffn_up, conv_ffn_w,
        conv_ffn_b, w_ffn_down, norm_final,
    )
    return second_block(
        x, mem_2, positions_2, norm_g_2, w_in_2, mla_q_norm_g_2, mla_kv_norm_g_2, w_uq_2,
        w_ukv_2, mla_qn_g_2, mla_kn_g_2, diff_qn_g_2, diff_kn_g_2, diff_lambda_2,
        diff_subln_g_2, mem_norm_g_2, w_mem_kv_2, mem_qn_g_2, mem_kn_g_2, w_out_2,
    )


_drawn_inputs = setup_inputs


def setup_inputs(seed=0):
    import zlib

    import numpy as np

    out = dict(_drawn_inputs(seed))
    spreads = {}
    factors = {'kv_norm': 5.002,
     'conv_ssm_b': 6.474,
     'conv_ffn_b': 7.479,
     'norm_g_2': 8.0,
     'mla_q_norm_g_2': 8.0,
     'mla_kv_norm_g_2': 8.0,
     'mla_qn_g_2': 8.0,
     'mla_kn_g_2': 8.0,
     'diff_qn_g_2': 8.0,
     'diff_kn_g_2': 8.0,
     'diff_lambda_2': 3.97,
     'diff_subln_g_2': 8.0,
     'mem_norm_g_2': 8.0,
     'mem_qn_g_2': 8.0,
     'mem_kn_g_2': 8.0}
    for name, (base, spread) in spreads.items():
        noise = np.random.default_rng([zlib.crc32(name.encode()), seed]).standard_normal(out[name].shape)
        drawn = base * np.exp(spread * noise) if base else spread * noise
        out[name] = __import__('jax').numpy.asarray(drawn.astype(out[name].dtype))
    for name, factor in factors.items():
        out[name] = (out[name] * factor).astype(out[name].dtype)
    return out
```

```python
import math
from contextlib import ExitStack

import numpy as np
import concourse.bass as bass
from concourse import mybir

F32 = mybir.dt.float32
BF16 = mybir.dt.bfloat16
I32 = mybir.dt.int32
F32R = mybir.dt.float32r
ALU = mybir.AluOpType
ACT = mybir.ActivationFunctionType
AX = mybir.AxisListType

P = 128
S = 1024
D = 1024
TT = S // P
KT = D // P
EPS = 1e-6
HEADS, HD = 16, 64
LAT = 128
IDXH = 8
TOPK = 256
INNER = 2048
SSMH = 32
GROUPS = 4
HPG = SSMH // GROUPS
CONV = 4
FFN = 2816
FT = FFN // P
XT = (INNER + 2 * GROUPS * 128) // P
O_Q, O_C, O_QI, O_KI, O_WI, O_Z, O_X, O_DT, O_GA, O_GS = (
    0, 1024, 1152, 1664, 1728, 1736, 3784, 6856, 6888, 7912)
BUCKETS, REL_MAX = 32, 128
MEMT = 256
MLAH, NOPE, ROPE, MQK = 8, 64, 32, 96
DH, DD = 8, 32
MEMH = 4
LAM0 = 0.8 - 0.6 * math.exp(-0.3 * 0)
THETA = 10000.0
BIG = 1e30
LOW, TAKEN, SPLIT = -3e38, -3.4e38, -3.2e38
Kf = 1024
W_SLOTS = 8


def bucket_table():
    n = np.maximum(255 - np.arange(384), 0)
    exact = BUCKETS // 2
    large = exact + (np.log(np.maximum(n, 1).astype(np.float32) / exact)
                     / math.log(REL_MAX / exact) * (BUCKETS - exact)).astype(np.int32)
    b = np.where(n < exact, n, np.minimum(large, BUCKETS - 1))
    out = (b[None, :] == np.arange(BUCKETS)[:, None]).astype(np.float32)
    out[BUCKETS - 1] -= 1.0
    return out


def hybrid_two_blocks(nc, t):
    ctx = ExitStack()
    with ctx:
        def sb(name, shape, dt=F32):
            return ctx.enter_context(nc.sbuf_tensor(name, shape, dt))

        def sem(name):
            return ctx.enter_context(nc.semaphore(name))

        arena_at = -(-nc.sbuf_base // 32) * 32
        arena = sb("arena", [P, 49 * Kf])
        rounded_tiles = {}

        def rounded(off):
            if off not in rounded_tiles:
                rounded_tiles[off] = nc.alloc_sbuf_tensor_at(f"rounded{off}", [P, Kf], F32R,
                                                             offset=arena_at + int(off * Kf) * 4)
            return rounded_tiles[off][:, :]

        def at(off, *shape):
            o, n = int(off * Kf), int(np.prod(shape))
            v = arena[:, o:o + n]
            if len(shape) == 2:
                v = v.rearrange("p (a b) -> p a b", b=shape[1])
            if len(shape) == 3:
                v = v.rearrange("p (a b c) -> p a b c", b=shape[1], c=shape[2])
            return v

        ident = sb("ident", [P, P])
        tri = sb("tri", [P, P])
        after = sb("after", [P, P])
        ones = sb("ones", [P, P])
        strip = sb("strip", [P, S], BF16)
        decay_out = sb("decay_out", [P, 2, 2 * SSMH])
        future = decay_out[:, :, :].rearrange("p a b -> p (a b)")
        cols = sb("cols", [P, 4, P])
        rows = sb("rows", [P, 544])
        dtbuf = sb("dtbuf", [P, TT, 2, SSMH])
        dt, adt = dtbuf[:, :, 0, :], dtbuf[:, :, 1, :]
        cosb = dtbuf[:, :, 0, 0:16]
        sinb = dtbuf[:, :, 0, 16:32]
        stat = sb("stat", [P, 256])
        neghalf = sb("neghalf", [P, 1])
        negmax = sb("negmax", [P, 4])
        rsum = sb("rsum", [P, 8])
        rinv = sb("rinv", [P, 8])
        lam = sb("lam", [P, 8])

        r_dtb, r_alog, r_dskip = rows[:, 0:32], rows[:, 32:64], rows[:, 64:96]
        r_qn, r_kn = rows[:, 96:192], rows[:, 192:288]
        r_dqn, r_dkn, r_sub = rows[:, 288:320], rows[:, 320:352], rows[:, 352:416]
        r_mqn, r_mkn = rows[:, 416:480], rows[:, 480:544]
        ROWS = [("dt_bias", r_dtb), ("a_log", r_alog), ("d_skip", r_dskip),
                ("mla_qn_g_2", r_qn), ("mla_kn_g_2", r_kn), ("diff_qn_g_2", r_dqn),
                ("diff_kn_g_2", r_dkn), ("diff_subln_g_2", r_sub), ("mem_qn_g_2", r_mqn),
                ("mem_kn_g_2", r_mkn)]
        COLS = [("conv_ssm_w", 0, 0, CONV * XT), ("conv_ssm_b", 0, 96, XT), ("norm_mix", 0, 120, KT),
                ("ssm_norm", 1, 0, 16), ("norm_ffn", 1, 16, KT), ("norm_g_2", 1, 24, KT),
                ("mem_norm_g_2", 1, 32, KT), ("mla_q_norm_g_2", 1, 40, 2), ("mla_kv_norm_g_2", 1, 42, 1),
                ("kv_norm", 1, 43, 1), ("conv_ffn_b", 1, 44, 2 * FT)]
        COL_ROWS = [128, 88, 88, 44]
        N_CONSTS = len(COLS) + 4

        def dram(name, shape):
            return nc.dram_tensor(name, shape, F32, kind="Internal").ap()

        hT_d = dram("hT_d", [P, KT * S])
        attT_d = dram("attT_d", [P, KT * S])
        z_d = dram("z_d", [S, INNER])
        bias_d = dram("bias_d", [HEADS, P, 384])
        x1_d = dram("x1_d", [P, TT * D])
        x3_d = dram("x3_d", [P, TT * D])

        psum = ctx.enter_context(nc.psum_tensor("psum", [P, 8, 512], F32))
        filled = [sem(f"filled{b}") for b in range(8)]
        evacuated = [sem(f"evacuated{b}") for b in range(8)]
        used = [0] * 8
        owner = [(b, 0) for b in range(8)]
        turn = [0]
        tile_of, before = {}, {}

        def bank(name, n=1):
            b = turn[0] if turn[0] + n <= 8 else 0
            turn[0] = (b + n) % 8
            before[name] = owner[b:b + n]
            used[b] += 1
            owner[b:b + n] = [(b, used[b])] * n
            tile_of[name] = (b, used[b], n)
            return psum_of(name)

        def psum_of(name):
            b, _, n = tile_of[name]
            return psum[:, b, :] if n == 1 else psum[:, b:b + n, :].rearrange("p a b -> p (a b)")

        def full(name):
            return filled[tile_of[name][0]]

        def completed(name):
            return filled[tile_of[name][0]], tile_of[name][1]

        def empty(name):
            return evacuated[tile_of[name][0]]

        def written(name):
            return evacuated[tile_of[name][0]], tile_of[name][1] + 1

        def vacated(name, k=0):
            b, count = before[name][k]
            return evacuated[b], count + 1

        wslot_in = [sem(f"wslot_in{i}") for i in range(W_SLOTS)]
        weights_split = sem("weights_split")
        weights, slot_count = {}, [0] * W_SLOTS
        slot_user, next_slot = [None] * W_SLOTS, [0]
        order = []
        split_order = []
        spent_by = {}

        def weight(name, pieces, gate=0, split=False):
            n = 2 if split else 1
            i = next_slot[0]
            i = (i + i % n) % W_SLOTS
            next_slot[0] = (i + n) % W_SLOTS
            earlier = [u for u in dict.fromkeys(slot_user[i:i + n]) if u is not None]
            slot_user[i:i + n] = [name] * n
            base = arena[:, (41 + i) * Kf:(42 + i) * Kf]
            slot_count[i] += 16 * len(pieces)
            weights[name] = (i, slot_count[i])
            order.append((name, i, earlier, [(base[:, 0:f * g].rearrange("p (a b) -> p a b", b=g)[:, :, lo:hi], src)
                                             for f, g, lo, hi, src in pieces], gate))
            if split:
                split_order.append(name)

        def loaded(name):
            i, count = weights[name]
            return wslot_in[i], count

        def weight_at(name, n):
            base = arena[:, (41 + weights[name][0]) * Kf:(42 + weights[name][0]) * Kf]
            return base[:, 0:(Kf // n) * n].rearrange("p (a b) -> p a b", b=n)

        def split(name):
            return weights_split, split_order.index(name) + 1

        def parts_at(name, n):
            i = weights[name][0]
            return [rounded(41 + s).rearrange("p (a b) -> p a b", b=n) for s in (i + 1, i)]

        def kp(ap):
            return ap.rearrange("(k p) n -> p k n", p=P)

        w_in = kp(t["w_in"][0])
        w_in2 = kp(t["w_in_2"][0])

        def w_cols(name, w, k0, kn, lo, n, gate=0, split=False):
            weight(name, [(kn, n, 0, n, w[:, k0:k0 + kn, lo:lo + n])], gate, split)

        def w_wide(name, w, kn, lo, n, gate=0, split=False):
            for k in range(0, kn, 2):
                w_cols((name, k), w, k, 2, lo, n, gate, split)

        weight("ki", [(8, 128, 0, 64, w_in[:, :, O_KI:O_KI + 64]), (8, 128, 64, 128, w_in[:, :, O_KI:O_KI + 64])])
        for j in range(4):
            w_cols(("qi", j), w_in, 0, 8, O_QI + P * j, P)
        w_cols("c", w_in, 0, 8, O_C, LAT)
        weight("small", [(8, 40, 0, 8, w_in[:, :, O_WI:O_WI + 8]), (8, 40, 8, 40, w_in[:, :, O_DT:O_DT + 32])])
        for n in ("w_uk", "w_uv"):
            w_cols(n, t[n][0].rearrange("h d c -> (h d) c").rearrange("(k p) n -> p k n", p=P), 0, 8, 0, LAT)
        for j in range(8):
            w_cols(("q", j), w_in, 0, 8, O_Q + P * j, P)
        for c in range(4):
            w_wide(("z", c), w_in, 8, O_Z + 512 * c, 512)
        PH_SSM, PH_MERGE, PH_OUT2 = 2, 4, 10
        for j in range(XT):
            w_cols(("x", j), w_in, 0, 8, O_X + P * j, P, PH_SSM)
        w_so, w_ao, w_o = kp(t["w_ssm_out"][0]), kp(t["w_att_out"][0]), kp(t["w_out"][0])
        for j in range(KT):
            w_cols(("so", j, 0), w_so, 0, 8, P * j, P, PH_MERGE)
            w_cols(("so", j, 1), w_so, 8, 8, P * j, P, PH_MERGE)
            w_cols(("gs", j), w_in, 0, 8, O_GS + P * j, P, PH_MERGE)
            w_cols(("ga", j), w_in, 0, 8, O_GA + P * j, P, PH_MERGE)
            w_cols(("ao", j), w_ao, 0, 8, P * j, P, PH_MERGE)
        for c in range(2):
            w_wide(("o", c), w_o, 8, 512 * c, 512)
        w_up, w_dn = kp(t["w_ffn_up"][0]), kp(t["w_ffn_down"][0])
        for j in range(FT):
            w_cols(("up", j, 0), w_up, 0, 8, P * j, P, split=True)
            w_cols(("up", j, 1), w_up, 0, 8, FFN + P * j, P, split=True)
        w_mem = kp(t["w_mem_kv_2"][0])
        w_wide(("dn", 0), w_dn, FT, 0, 512, split=True)
        w_wide("mem", w_mem, 8, 0, 512)
        w_wide(("dn", 1), w_dn, FT, 512, 512, split=True)
        IN2 = [(0, 416), (416, 512), (928, 512), (1440, 512), (1952, 512)]
        for c, (lo, n) in enumerate(IN2):
            w_wide(("in2", c), w_in2, 8, lo, n)
        w_o2 = kp(t["w_out_2"][0])
        for c in range(2):
            w_wide(("o2", c), w_o2, 8, 512 * c, 512, PH_OUT2)

        x_in = [sem(f"x_in{i}") for i in range(TT)]
        consts_in = sem("consts_in")
        rows_in = sem("rows_in")
        consts_made = sem("consts_made")
        squared = sem("squared")
        mean_ready = sem("mean_ready")
        rstd_ready = sem("rstd_ready")
        scaled = sem("scaled")
        relu_ready = sem("relu_ready")
        relu_used = sem("relu_used")
        exp_ready = sem("exp_ready")
        out_ready = sem("out_ready")
        phase_done = sem("phase_done")
        z_out = [sem(f"z_out{i}") for i in range(4)]
        hT_out = sem("hT_out")
        attT_out = sem("attT_out")
        bias_out = sem("bias_out")
        bias_in = sem("bias_in")
        conv_ready = sem("conv_ready")
        conv_used = sem("conv_used")
        u_used = sem("u_used")
        dt_made = sem("dt_made")
        dt_steps = sem("dt_steps")
        z_in = [sem(f"z_in{i}") for i in range(2)]
        step_made = sem("step_made")
        decayed = sem("decayed")
        mixed = sem("mixed")
        xds_ready = sem("xds_ready")
        state_ready = sem("state_ready")
        gated = sem("gated")
        ynorm = sem("ynorm")
        back_in = [sem(f"back_in{i}") for i in range(6)]
        x_again = sem("x_again")
        gate_made = sem("gate_made")
        merged_ready = sem("merged_ready")
        resid = sem("resid")
        x1_out = sem("x1_out")
        silu_made = sem("silu_made")
        high_made = sem("high_made")
        parts_made = sem("parts_made")
        mem_in = sem("mem_in")
        nf_in = sem("nf_in")
        x3_out = sem("x3_out")
        pos_in = sem("pos_in")
        pads = sem("pads")
        dn_spent = sem("dn_spent")
        angle = sem("angle")
        trig = sem("trig")
        w_small_in = sem("w_small_in")
        heads_ready = sem("heads_ready")
        sq_ready = sem("sq_ready")
        gate2 = sem("gate2")
        y_ready = sem("y_ready")
        out_done = sem("out_done")
        lam_steps = sem("lam_steps")

        hT = at(0, KT, S)
        x_tok = at(8, TT, D)
        hs = at(16, 2, D)
        qT = at(8, KT, S)
        attT = qT
        zbuf = at(37.5, 4, 512)
        qiT, kiT = at(18, 4, S), at(22, S)
        ckvT = at(24, LAT * TT)
        score_off = {}
        o = 0
        for i in range(2, TT):
            score_off[i] = o
            o += (i + 1) * P
        scores = at(25, o)
        negmask = arena[:, int(29.25 * Kf):int(29.25 * Kf) + o // 2].bitcast(BF16)
        biasT = at(31.5, HEADS, 256)
        ukT, uvT = at(35.5, D), at(36.5, D)
        row_stage = at(37.5, 4, P)
        onehot, relb = at(38, 384), at(38.5, HEADS)
        bias_row = at(38.75, 384 // 2 * 2)
        craw = at(39.5, TT, 168)
        rel = at(16, 2, S)
        kT, v = at(16, KT, S), at(41, TT, D)
        dtmp = [at(23 + 0.25 * n, TT * SSMH) for n in range(4)]
        def rings(l_off, p_offs, pt_off):
            return ([at(l_off + n, S) for n in range(2)], [at(q, S) for q in p_offs],
                    [at(pt_off + n, S) for n in range(3)])
        A1 = rings(25, (27, 28, 38.5), 35.5)
        att = at(39.5, 1, D)
        uB = [at(8 + 1.25 * n, 3 + S) for n in range(2)]
        accB = [at(11 + n, S) for n in range(2)]
        xsT, bT, cT = at(16, 16, S), at(32, 4, S), at(36, 4, S)
        yT = xsT
        xdt = [at(0 + 2 * n, INNER) for n in range(2)]
        yb = [at(4 + 2 * n, INNER) for n in range(2)]
        state = at(8, INNER)
        zc = [at(10 + 2 * n, INNER) for n in range(2)]
        mix = [at(14 + n, S) for n in range(2)]
        step = [at(40 + n, S) for n in range(2)]
        xds = [at(42 + 0.5 * n, 512) for n in range(2)]
        btok = [at(43 + 0.5 * n, 512) for n in range(2)]
        cbm = [at(44 + 0.5 * n, 512) for n in range(2)]
        yoff = at(45, 512)
        junk = at(45.5, 512)
        hTd, attTd = at(0, KT, S), at(8, KT, S)
        mergedT = at(32, KT, S)
        gate_s = at(40, S)
        x1 = at(0, TT, D)
        hsE, junkE = at(16, 2, D), at(18, D)
        h2T = at(8, KT, S)
        h2hi, h2lo = [[rounded(off + k) for k in range(KT)] for off in (0, 8)]
        accF = [at(38 + n, S) for n in range(2)]
        actT = at(16, FT, S)
        act_parts = [[[rounded(off + n) for n in range(2)] for off in offs]
                     for offs in ((12, 14), (8, 38))]
        memx, memT, memkv, kmT = at(8, 2, D), at(10, KT, MEMT), at(40, 2, 512), at(11.25, 2, MEMT)
        nfb = at(12, D)
        h3T = at(16, KT, S)
        hs3, junkG = at(38, 2, D), at(24, D)
        pA, pB, pZ = at(8, TT, 416), at(24, TT, 1024), at(32, TT, 1024)
        trigT = [at(13 + 0.125 * n, TT, 16) for n in range(5)]
        invf, posf, pos_i = at(13.75, 16), at(13.8125, TT), at(13.875, TT).bitcast(I32)
        lamv = at(14, 4, 32)
        dsq = at(14.5, 768)
        vM = at(12, TT, 512)
        qTm, kTm = at(0, MLAH, S), at(16, MLAH, S)
        cqT, ckv2T = at(41, 2, S), at(43, S)
        wuq, wukv = at(44, 2, 768), at(45.5, D)
        qtok, ktok, htmp = at(46.5, 768), at(47.25, 768), at(48, 768)
        A2 = rings(41, (43, 44, 45), 46)
        od, odsq = at(8, TT, 256), at(12, TT, 256)
        yT2, xo = at(0, KT, S), at(16, TT, D)

        def rings_of(g):
            return A1 if g < N1 else A2

        stat_col, stat_n, stat_at = {}, {}, {}
        squared_n = {}

        def chain(name, col, width, by_act=False):
            stat_n[name] = len(stat_n) + 1
            stat_at[name] = (col, width)

        for i in range(TT):
            chain(("x", i), i, 1)
        chain("ckv", 8, TT)
        for c in range(TT):
            chain(("ssd", c), 16 + 4 * c, 4)
        for i in range(TT):
            chain(("h2", i), 48 + i, 1)
        for i in range(2):
            chain(("mem", i), 72 + i, 1)
        chain("memk", 74, 8)
        for n in range(TT + 2):
            if n < TT:
                chain(("x3", n), 56 + n, 1)
            if n >= 2:
                chain(("h3", n - 2), 64 + n - 2, 1)
        chain("cc", 82, 16)
        chain("dd", 98, 128)
        chain("mqm", 16, 32)
        for i in range(TT):
            chain(("mq", i), 16 * (i % 2), 8)
            chain(("mk", i), 16 * (i % 2) + 8, 8)
        chain("sub", 48, 32)
        sq_order = ([("x", i) for i in range(TT)] + [("ssd", c) for c in range(TT)] + [("h2", i) for i in range(TT)]
                    + [("mem", i) for i in range(2)])
        for n in range(TT + 2):
            sq_order += ([("x3", n)] if n < TT else []) + ([("h3", n - 2)] if n >= 2 else [])
        squared_n = {name: n + 1 for n, name in enumerate(sq_order)}

        part_order = [("h2", k) for k in range(KT)]
        part_order += [("act", c, k) for c in range(2) for k in range(FT)]

        def high(name):
            return high_made, part_order.index(name) + 1

        def parts(name):
            return parts_made, part_order.index(name) + 1

        def down_step(c, k):
            return c * (FT - 1) + k + 1

        def stat_of(name, k=None):
            col, width = stat_at[name]
            return stat[:, col:col + width] if k is None else stat[:, col + k:col + k + 1]

        def rooted(name):
            return rstd_ready, stat_n[name]

        def bc(ap, n, axis=2):
            shape = list(ap.shape)
            return ap.unsqueeze(axis).broadcast_to(shape[:axis] + [n] + shape[axis:])

        block = ctx.enter_context(nc.Block())

        def chunks(n):
            return [(lo, min(n, lo + 512)) for lo in range(0, n, 512)]

        def unit(ph, i, nk, q, k, v, **more):
            return dict(ph=ph, i=i, nk=nk, q=q, k=k, v=v, **more)

        units1 = []
        for i in range(TT):
            for h in range(HEADS):
                r, j = 64 * (h % 2), h // 2
                units1.append(unit(
                    "a", i, i + 1, qT[r:r + 64, j, i * P:(i + 1) * P],
                    lambda lo, hi, r=r, j=j: kT[r:r + 64, j, lo:hi],
                    lambda b, h=h: v[:, b, h * 64:h * 64 + 64], h=h,
                    mask=strip[:, (7 - i) * P:S] if i < 2 else negmask[:, score_off[i]:score_off[i] + (i + 1) * P]))
        units2 = []
        for i in range(TT):
            for h in range(MLAH):
                units2.append(unit(
                    "m", i, i + 1, qTm[0:MQK, h, i * P:(i + 1) * P],
                    lambda lo, hi, h=h: kTm[0:MQK, h, lo:hi],
                    lambda b, h=h: vM[:, b, h * 64:h * 64 + 64], h=h, mask=strip[:, (7 - i) * P:S]))
        for i in range(TT):
            for m in range(2 * DH // 2):
                r, j = 32 * (m % 4), m // 4
                units2.append(unit(
                    "d", i, i + 1, pB[r:r + 32, i, j * P:(j + 1) * P],
                    lambda lo, hi, r=r, j=j: pB[r:r + 32, lo // P:hi // P, 256 + j * P:256 + (j + 1) * P],
                    lambda b, m=m: pB[:, b, 512 + 64 * (m // 2):576 + 64 * (m // 2)], h=m,
                    mask=strip[:, (7 - i) * P:S]))
        for i in range(TT):
            for h in range(MEMH):
                r, j = 64 * (h % 2), h // 2
                units2.append(unit(
                    "e", i, 2, pB[r:r + 64, i, 768 + j * P:768 + (j + 1) * P],
                    lambda lo, hi, r=r, j=j: kmT[r:r + 64, j, lo:hi],
                    lambda b, h=h: memkv[:, b, 256 + h * 64:320 + h * 64], h=h, mask=strip[:, 0:256]))
        N1 = len(units1)

        def last_group(u):
            return (u["nk"] - 1) // 4

        def end_phase(eng):
            eng.drain()
            eng.sem_inc(phase_done, 1)

        @block.tensor
        def _(pe):
            def mm(out, lhsT, rhs, start=True, stop=True):
                return pe.matmul(out, lhsT, rhs, start=start, stop=stop)

            def tr(out, src):
                n = src.shape[0]
                return pe.transpose(out, src, ident[0:n, 0:n])

            def four(name, blocks):
                out = bank(name)
                pe.wait_ge(*vacated(name))
                for n, src in enumerate(blocks):
                    last = tr(out[:, n * P:(n + 1) * P], src)
                last.then_inc(full(name), 1)

            def stationary_weights(name, wnames, xT, both=False):
                for wn in wnames:
                    pe.wait_ge(*loaded(wn))
                if both:
                    out2 = bank(name, 2)
                    pe.wait_ge(*vacated(name))
                    pe.wait_ge(*vacated(name, 1))
                for half in range(2):
                    if both:
                        out = out2[:, half * 512:half * 512 + 512]
                    else:
                        out = bank((*name, half))
                        pe.wait_ge(*vacated((*name, half)))
                    n = 0
                    for wn in wnames:
                        w = weight_at(wn, P)
                        for k in range(8):
                            last = mm(out, w[:, k, :], xT[:, n, half * 512:half * 512 + 512],
                                      n == 0, n == 8 * len(wnames) - 1)
                            n += 1
                    if not both:
                        last.then_inc(full((*name, half)), 1)
                if both:
                    last.then_inc(full(name), 1)
                for wn in wnames:
                    spent_by[wn] = name if both else (*name, 1)

            def three(out, whigh, wlow, xhigh, xlow, first, last):
                mm(out, whigh, xlow, first, False)
                mm(out, whigh, xhigh, False, False)
                return mm(out, wlow, xhigh, False, last)

            def stationary_parts(name, wnames, xhigh, xlow, key=None):
                for wn in wnames:
                    pe.wait_ge(*split(wn))
                out2 = bank(name, 2)
                pe.wait_ge(*vacated(name))
                pe.wait_ge(*vacated(name, 1))
                n = 0
                for wn in wnames:
                    wh, wl = parts_at(wn, P)
                    for k in range(8):
                        if key is not None:
                            pe.wait_ge(*parts((key, n)))
                        for lo in (0, 512):
                            last = three(out2[:, lo:lo + 512], wh[:, k, :], wl[:, k, :], xhigh[n][:, lo:lo + 512],
                                         xlow[n][:, lo:lo + 512], n == 0, n == 8 * len(wnames) - 1)
                        n += 1
                last.then_inc(full(name), 1)
                for wn in wnames:
                    spent_by[wn] = name

            def token_rows(name, n, kn, xT):
                for k in range(0, kn, 2):
                    pe.wait_ge(*loaded((name, k)))
                ws = [weight_at((name, k), n) for k in range(0, kn, 2)]
                for tt in range(TT):
                    out = bank((*name, tt))
                    pe.wait_ge(*vacated((*name, tt)))
                    for k in range(kn):
                        last = mm(out[:, 0:n], xT[:, k, tt * P:(tt + 1) * P], ws[k // 2][:, k % 2, :],
                                  k == 0, k == kn - 1)
                    last.then_inc(full((*name, tt)), 1)
                for k in range(0, kn, 2):
                    spent_by[(name, k)] = (*name, TT - 1)

            def attend(units, base, after_block):
                n = len(units)
                pending = None
                for s in range(n + 4):
                    if s < n:
                        u = units[s]
                        out = bank(("S", base + s), 1 if u["nk"] <= 4 else 2)
                        pe.wait_ge(*vacated(("S", base + s)))
                        pe.wait_ge(*vacated(("S", base + s), -1))
                        for lo, hi in chunks(u["nk"] * P):
                            last = mm(out[:, lo:hi], u["q"], u["k"](lo, hi))
                        last.then_inc(full(("S", base + s)), 1)
                    if pending is not None:
                        after_block(pending)
                        pending = None
                    if 0 <= s - 2 < n:
                        u, g = units[s - 2], base + s - 2
                        probs = rings_of(g)[1][g % 3]
                        pe.wait_ge(exp_ready, g + 1)
                        for grp in range(last_group(u) + 1):
                            out = bank(("T", g, grp))
                            pe.wait_ge(*vacated(("T", g, grp)))
                            for b in range(4 * grp, min(4 * grp + 4, u["nk"])):
                                last = tr(out[:, (b - 4 * grp) * P:(b - 4 * grp + 1) * P], probs[:, b * P:(b + 1) * P])
                            last.then_inc(full(("T", g, grp)), 1)
                    if 0 <= s - 3 < n:
                        u, g = units[s - 3], base + s - 3
                        pT = rings_of(g)[2][g % 3]
                        pe.wait_ge(*written(("T", g, last_group(u))))
                        out = bank(("O", g))
                        pe.wait_ge(*vacated(("O", g)))
                        for b in range(u["nk"]):
                            last = mm(out[:, 0:64], pT[:, b * P:(b + 1) * P], u["v"](b), b == 0, b == u["nk"] - 1)
                        last.then_inc(full(("O", g)), 1)
                        if u["ph"] == "a" and u["h"] == HEADS - 1:
                            pending = u["i"]

            pe.wait_ge(consts_made, 1)
            pe.wait_ge(consts_in, 16 * N_CONSTS)
            out = bank("cols")
            pe.wait_ge(*vacated("cols"))
            for m, r in enumerate(COL_ROWS):
                last = tr(out[:, m * P:m * P + r], row_stage[0:r, m, :])
            last.then_inc(full("cols"), 1)
            out = bank("bias")
            pe.wait_ge(*vacated("bias"))
            mm(out[0:HEADS, 0:384], relb[0:BUCKETS, :], onehot[0:BUCKETS, :]).then_inc(full("bias"), 1)

            def norm_tiles(key, src, n0, tiles, before=None):
                for tt in tiles:
                    pe.wait_ge(scaled, n0 + tt + 1)
                    for half in range(2):
                        four((key, tt, half), [src[:, tt % 2, (4 * half + n) * P:(4 * half + n + 1) * P] for n in range(4)])

            norm_tiles("hx", hs, 0, range(TT))
            for tt in range(TT):
                for half in range(2):
                    pe.wait_ge(*written(("hx", tt, half)))
            stationary_weights(("ki",), ["ki"], hT)
            for j in range(4):
                stationary_weights(("qi", j), [("qi", j)], hT)
            pe.wait_ge(*loaded("c"))
            pe.wait_ge(*loaded("small"))
            wc, wsm = weight_at("c", P), weight_at("small", 40)
            for tt in range(TT):
                out = bank(("c", tt))
                pe.wait_ge(*vacated(("c", tt)))
                for k in range(KT):
                    mm(out[:, 0:LAT], hT[:, k, tt * P:(tt + 1) * P], wc[:, k, :], k == 0, k == KT - 1)
                for k in range(KT):
                    last = mm(out[:, LAT:LAT + 40], hT[:, k, tt * P:(tt + 1) * P], wsm[:, k, :], k == 0, k == KT - 1)
                last.then_inc(full(("c", tt)), 1)
            spent_by["c"] = spent_by["small"] = ("c", TT - 1)
            for half in range(2):
                pe.wait_ge(*written(("ki", half)))
            for j in range(4):
                pe.wait_ge(*written(("qi", j, 1)))
            for i in range(2, TT):
                for h in range(IDXH):
                    r, nk = 64 * (h % 2), (i + 1) * P
                    out = bank(("ix", i, h), 1 if nk <= 512 else 2)
                    pe.wait_ge(*vacated(("ix", i, h)))
                    pe.wait_ge(*vacated(("ix", i, h), -1))
                    for lo, hi in chunks(nk):
                        last = mm(out[:, lo:hi], qiT[r:r + 64, h // 2, i * P:(i + 1) * P], kiT[r:r + 64, lo:hi])
                    last.then_inc(full(("ix", i, h)), 1)
            pe.wait_ge(heads_ready, 1)
            for half in range(2):
                four(("ckvT", half), [craw[:, 4 * half + n, 0:LAT] for n in range(4)])
            for wn, key in (("w_uk", "ukT"), ("w_uv", "uvT")):
                pe.wait_ge(*loaded(wn))
                w = weight_at(wn, P)
                for half in range(2):
                    four((key, half), [w[:, 4 * half + n, :] for n in range(4)])
                spent_by[wn] = (key, 1)
            for j in range(8):
                stationary_weights(("q", j), [("q", j)], hT)
            for c in range(4):
                token_rows(("z", c), 512, 8, hT)
            end_phase(pe)
            pe.wait_ge(phase_done, 4 * 1)

            for j in range(8):
                for half in range(2):
                    out = bank(("kT", j, half))
                    pe.wait_ge(*vacated(("kT", j, half)))
                    mm(out, ukT[:, j * P:(j + 1) * P], ckvT[:, half * 512:half * 512 + 512]).then_inc(full(("kT", j, half)), 1)
            for tt in range(TT):
                for half in range(2):
                    out = bank(("v", tt, half))
                    pe.wait_ge(*vacated(("v", tt, half)))
                    mm(out, ckvT[:, tt * P:(tt + 1) * P], uvT[:, half * 512:half * 512 + 512]).then_inc(full(("v", tt, half)), 1)
            for j in range(8):
                pe.wait_ge(*written(("kT", j, 1)))
            for tt in range(TT):
                pe.wait_ge(*written(("v", tt, 1)))

            def att_transposed(i):
                pe.wait_ge(*written(("O", HEADS * i + HEADS - 1)))
                for half in range(2):
                    four(("aT", i, half), [att[:, 0, (4 * half + n) * P:(4 * half + n + 1) * P] for n in range(4)])

            attend(units1, 0, att_transposed)
            end_phase(pe)
            pe.wait_ge(phase_done, 4 * 2)

            for j in range(XT):
                stationary_weights(("xc", j), [("x", j)], hT)
            end_phase(pe)
            pe.wait_ge(phase_done, 4 * 3)

            def ssd_front(c):
                here = slice(c * P, (c + 1) * P)
                for g in range(GROUPS):
                    four(("xt", c, g), [xsT[:, 4 * g + n, here] for n in range(4)])
                four(("bt", c), [bT[:, n, here] for n in range(GROUPS)])
                out = bank(("cb", c))
                pe.wait_ge(*vacated(("cb", c)))
                for g in range(GROUPS):
                    last = mm(out[:, g * P:(g + 1) * P], bT[:, g, here], cT[:, g, here])
                last.then_inc(full(("cb", c)), 1)
                out = bank(("ea", c))
                pe.wait_ge(*vacated(("ea", c)))
                mm(out[:, 0:SSMH], tri[:, :], adt[:, c, :])
                mm(out[:, SSMH:2 * SSMH], ones[:, :], adt[:, c, :]).then_inc(full(("ea", c)), 1)

            def ssd_tail(n):
                c, g = n // GROUPS, n % GROUPS
                here = slice(c * P, (c + 1) * P)
                pe.wait_ge(mixed, n + 1)
                out = bank(("yd", c, g))
                pe.wait_ge(*vacated(("yd", c, g)))
                for h in range(HPG):
                    lo = (HPG * g + h) * 64
                    last = mm(out[:, h * 64:h * 64 + 64], mix[n % 2][:, h * P:(h + 1) * P], xdt[c % 2][:, lo:lo + 64])
                last.then_inc(full(("yd", c, g)), 1)
                if c:
                    pe.wait_ge(*written(("st", c - 1, g)))
                    out = bank(("yo", c, g))
                    pe.wait_ge(*vacated(("yo", c, g)))
                    mm(out, cT[:, g, here], state[:, g * 512:(g + 1) * 512]).then_inc(full(("yo", c, g)), 1)
                if c < TT - 1:
                    pe.wait_ge(*written(("bt", c)))
                    out = bank(("st", c, g))
                    pe.wait_ge(*vacated(("st", c, g)))
                    mm(out, btok[c % 2][:, g * P:(g + 1) * P], xds[n % 2]).then_inc(full(("st", c, g)), 1)

            NG = TT * GROUPS
            for n in range(NG + 4):
                c, g = n // GROUPS, n % GROUPS
                if n < NG:
                    if g == 0:
                        ssd_front(c)
                    pe.wait_ge(step_made, n + 1)
                    out = bank(("sg", c, g), 2)
                    pe.wait_ge(*vacated(("sg", c, g)))
                    pe.wait_ge(*vacated(("sg", c, g), 1))
                    for lo, hi in chunks(S):
                        last = mm(out[:, lo:hi], after[:, :], step[n % 2][:, lo:hi])
                    last.then_inc(full(("sg", c, g)), 1)
                if 1 <= n <= NG:
                    ssd_tail(n - 1)
                if n >= 4 and (n - 4) % GROUPS == 3:
                    cc = (n - 4) // GROUPS
                    pe.wait_ge(ynorm, cc + 1)
                    for q in range(4):
                        four(("yt", cc, q), [yb[cc % 2][:, (4 * q + m) * P:(4 * q + m + 1) * P] for m in range(4)])
            end_phase(pe)
            pe.wait_ge(phase_done, 4 * 4)

            for j in range(KT):
                stationary_weights(("so", j), [("so", j, 0), ("so", j, 1)], yT, True)
                if j == 0:
                    for s in back_in[0:2]:
                        pe.wait_ge(s, 16)
                stationary_weights(("gs", j), [("gs", j)], hTd, True)
                stationary_weights(("ga", j), [("ga", j)], hTd, True)
                stationary_weights(("ao", j), [("ao", j)], attTd, True)
            end_phase(pe)
            pe.wait_ge(phase_done, 4 * 5)

            pe.wait_ge(merged_ready, KT)
            token_rows(("o", 0), 512, 8, mergedT)
            for k in range(0, 8, 2):
                pe.wait_ge(*loaded((("o", 1), k)))
            ws = [weight_at((("o", 1), k), 512) for k in range(0, 8, 2)]
            for tt in range(TT + 2):
                if tt < TT:
                    out = bank(("o", 1, tt))
                    pe.wait_ge(*vacated(("o", 1, tt)))
                    for k in range(KT):
                        last = mm(out, mergedT[:, k, tt * P:(tt + 1) * P], ws[k // 2][:, k % 2, :], k == 0, k == KT - 1)
                    last.then_inc(full(("o", 1, tt)), 1)
                if tt >= 2:
                    norm_tiles("h2", hsE, TT, [tt - 2])
            for k in range(0, 8, 2):
                spent_by[(("o", 1), k)] = ("o", 1, TT - 1)
            for tt in range(TT):
                for half in range(2):
                    pe.wait_ge(*written(("h2", tt, half)))
            end_phase(pe)
            pe.wait_ge(phase_done, 4 * 6)
            for j in range(FT):
                stationary_parts(("ug", j), [("up", j, 0)], h2hi, h2lo, "h2" if j == 0 else None)
                stationary_parts(("uv", j), [("up", j, 1)], h2hi, h2lo)
            end_phase(pe)
            pe.wait_ge(phase_done, 4 * 7)
            def memory():
                norm_tiles("mx", hs3, 2 * TT, range(2))
                for tt in range(2):
                    for half in range(2):
                        pe.wait_ge(*written(("mx", tt, half)))
                for k in range(0, 8, 2):
                    pe.wait_ge(*loaded(("mem", k)))
                ws = [weight_at(("mem", k), 512) for k in range(0, 8, 2)]
                for tt in range(2):
                    out = bank(("mem", tt))
                    pe.wait_ge(*vacated(("mem", tt)))
                    for k in range(KT):
                        last = mm(out, memT[:, k, tt * P:(tt + 1) * P], ws[k // 2][:, k % 2, :], k == 0, k == KT - 1)
                    last.then_inc(full(("mem", tt)), 1)
                for k in range(0, 8, 2):
                    spent_by[("mem", k)] = ("mem", 1)
                pe.wait_ge(sq_ready, 1)
                four(("kmT",), [memkv[:, n % 2, (n // 2) * P:(n // 2 + 1) * P] for n in range(4)])

            for c in range(2):
                outs = [bank(("dn", c, tt)) for tt in range(TT)]
                for tt in range(TT):
                    pe.wait_ge(*vacated(("dn", c, tt)))
                for k in range(FT):
                    if k % 2 == 0:
                        pe.wait_ge(*split((("dn", c), k)))
                    wh, wl = parts_at((("dn", c), k - k % 2), 512)
                    ah, al = act_parts[c][k % 2]
                    pe.wait_ge(*parts(("act", c, k)))
                    for tt in range(TT):
                        here = slice(tt * P, (tt + 1) * P)
                        last = three(outs[tt], ah[:, here], al[:, here], wh[:, k % 2, :], wl[:, k % 2, :],
                                     k == 0, k == FT - 1)
                        if k == FT - 1:
                            last.then_inc(full(("dn", c, tt)), 1)
                    if k == FT - 1:
                        spent_by[(("dn", c), k - 1)] = ("dn", c, TT - 1)
                    else:
                        last.then_inc(dn_spent, 1)
                        if k % 2:
                            spent_by[(("dn", c), k - 1)] = down_step(c, k)
                if c == 0:
                    memory()

            norm_tiles("h3", hs3, 2 * TT + 2, range(TT))
            for tt in range(TT):
                for half in range(2):
                    pe.wait_ge(*written(("h3", tt, half)))
            for c, (lo, n) in enumerate(IN2):
                token_rows(("in2", c), n, 8, h3T)
            pe.wait_ge(heads_ready, 3)
            for x in (0, 1, 2, 3, 6, 7):
                for half in range(2):
                    four(("dT", x, half), [pB[:, 4 * half + n, x * P:(x + 1) * P] for n in range(4)])
            end_phase(pe)
            pe.wait_ge(phase_done, 4 * 8)
            for k in range(3):
                for half in range(2):
                    four(("cqT", k, half), [pA[:, 4 * half + n, k * P:(k + 1) * P] for n in range(4)])
            pe.wait_ge(w_small_in, 32)
            for k in range(3):
                for half in range(2):
                    pe.wait_ge(*written(("cqT", k, half)))
            for tt in range(TT):
                here = slice(tt * P, (tt + 1) * P)
                out = bank(("uq", tt), 2)
                pe.wait_ge(*vacated(("uq", tt)))
                pe.wait_ge(*vacated(("uq", tt), 1))
                for lo, hi in chunks(768):
                    for k in range(2):
                        last = mm(out[:, lo:hi], cqT[:, k, here], wuq[:, k, lo:hi], k == 0, k == 1)
                last.then_inc(full(("uq", tt)), 1)
                out = bank(("ukv", tt), 2)
                pe.wait_ge(*vacated(("ukv", tt)))
                pe.wait_ge(*vacated(("ukv", tt), 1))
                for lo, hi in chunks(D):
                    last = mm(out[:, lo:hi], ckv2T[:, here], wukv[:, lo:hi])
                last.then_inc(full(("ukv", tt)), 1)
                for key, src, n in (("qTm", qtok, 2 * tt), ("kTm", ktok, 2 * tt + 1)):
                    pe.wait_ge(heads_ready, 4 + n)
                    for half in range(2):
                        out = bank((key, tt, half))
                        pe.wait_ge(*vacated((key, tt, half)))
                        for m in range(4):
                            h = 4 * half + m
                            last = tr(out[0:MQK, m * P:(m + 1) * P], src[:, h * MQK:(h + 1) * MQK])
                        last.then_inc(full((key, tt, half)), 1)
            end_phase(pe)
            pe.wait_ge(phase_done, 4 * 9)
            attend(units2, N1, None)
            end_phase(pe)
            pe.wait_ge(phase_done, 4 * 10)
            for tt in range(TT):
                for half in range(2):
                    four(("yT2", tt, half), [pZ[:, tt, (4 * half + n) * P:(4 * half + n + 1) * P] for n in range(4)])
            for tt in range(TT):
                for half in range(2):
                    pe.wait_ge(*written(("yT2", tt, half)))
            for c in range(2):
                token_rows(("o2", c), 512, 8, yT2)

        @block.sync
        def _(sp):
            def row_ap(name):
                a = t[name][0] if len(t[name].shape) > 1 else t[name]
                return a.rearrange("(k p) -> k p", p=P) if len(a.shape) == 1 else a.rearrange("j (k p) -> (j k) p", p=P)

            for name, m, r0, n in COLS:
                sp.dma_start(row_stage[r0:r0 + n, m, :], row_ap(name)).then_inc(consts_in, 16)
            taps = row_ap("conv_ffn_w")
            sp.dma_start(row_stage[0:88, 2, :], taps[0:88, :]).then_inc(consts_in, 16)
            sp.dma_start(row_stage[0:44, 3, :], taps[88:132, :]).then_inc(consts_in, 16)
            sp.dma_start(onehot[0:BUCKETS, :], t["buckets"]).then_inc(consts_in, 16)
            sp.dma_start(relb[0:BUCKETS, :], t["rel_bias"]).then_inc(consts_in, 16)
            for tt in range(TT):
                sp.dma_start(x_tok[:, tt, :], t["x"][0, tt * P:(tt + 1) * P, :]).then_inc(x_in[tt], 16)
            for name, dst in ROWS:
                src = t[name]
                n = src.shape[-1]
                sp.dma_start(dst, bass.AP(src.tensor, src.offset, [[0, P], [1, n]])).then_inc(rows_in, 16)

            def relative_bias():
                sp.wait_ge(*written("bias"))
                src = bias_row[0:HEADS, :].unsqueeze(1).broadcast_to([HEADS, P, 384])
                sp.dma_start(bias_d, src).then_inc(bias_out, 16)
                sp.wait_ge(bias_out, 16)
                src = bass.AP(bias_d.tensor, P - 1, [[384 - 1, P], [P * 384, HEADS], [1, 256]])
                sp.dma_start(biasT, src).then_inc(bias_in, 16)

            def gate_rows():
                sp.wait_ge(phase_done, 4 * 3)
                for c in range(TT):
                    if c >= 2:
                        sp.wait_ge(gated, c - 1)
                    sp.dma_start(zc[c % 2], z_d[c * P:(c + 1) * P, :]).then_inc(z_in[c % 2], 16)

            def branch_inputs():
                sp.dma_start(hTd.rearrange("p k s -> p (k s)"), hT_d).then_inc(back_in[0], 16)
                sp.dma_start(attTd.rearrange("p k s -> p (k s)"), attT_d).then_inc(back_in[1], 16)

            def residual():
                sp.wait_ge(phase_done, 4 * 5)
                sp.dma_start(x1, t["x"][0].rearrange("(a p) n -> p a n", p=P)).then_inc(x_again, 16)

            def mla_weights():
                sp.wait_ge(phase_done, 4 * 8)
                sp.dma_start(wuq, kp(t["w_uq_2"][0])).then_inc(w_small_in, 16)
                sp.dma_start(wukv, t["w_ukv_2"][0]).then_inc(w_small_in, 16)

            ahead = {"w_uk": relative_bias, ("so", 0, 0): gate_rows, ("gs", 0): branch_inputs,
                     ("up", 0, 0): residual, (("o2", 0), 0): mla_weights}
            for n, (name, slot, earlier, pieces, gate) in enumerate(order):
                if name in ahead:
                    ahead[name]()
                for tile in earlier:
                    last = spent_by[tile]
                    if isinstance(last, int):
                        sp.wait_ge(dn_spent, last)
                    else:
                        sp.wait_ge(*completed(last))
                if gate:
                    sp.wait_ge(phase_done, 4 * gate)
                for dst, src in pieces:
                    sp.dma_start(dst, src).then_inc(wslot_in[slot], 16)
                if n == len(order) - 1:
                    sp.dma_start(xo.rearrange("p a n -> p (a n)"), x3_d).then_inc(back_in[3], 16)
            for tt in range(TT):
                sp.wait_ge(*written(("o2", 1, tt)))
                sp.dma_start(t["out"][0, tt * P:(tt + 1) * P, :], xo[:, tt, :]).then_inc(out_done, 16)
            sp.wait_ge(out_done, 16 * TT)

        @block.gpsimd
        def _(pool):
            def power(*names):
                for name in names:
                    pool.wait_ge(mean_ready, stat_n[name])
                    v = stat_of(name)
                    pool.tensor_tensor(out=v, in0=v, in1=neghalf[:, 0:1].broadcast_to(list(v.shape)),
                                       op=ALU.pow).then_inc(rstd_ready, 1)

            def split_weights(*names):
                for name in names:
                    raw = weight_at(name, P)
                    high_part, low_part = parts_at(name, P)
                    pool.wait_ge(*loaded(name))
                    pool.tensor_copy(high_part, raw)
                    pool.drain()
                    pool.tensor_tensor(out=low_part, in0=raw, in1=high_part.bitcast(F32),
                                       op=ALU.subtract).then_inc(weights_split, 1)

            for m, value in ((ident, 0.0), (tri, 1.0), (after, 1.0), (ones, 1.0), (strip, 0.0), (future, 0.0),
                             (neghalf, -0.5)):
                pool.memset(m if m is future else m[:, :], value)
            pool.drain()
            pool.affine_select(out=ident[:, :], in_=ident[:, :], compare_op=ALU.not_equal, fill=1.0, base=0,
                               pattern=[[-1, P]], channel_multiplier=1)
            pool.affine_select(out=tri[:, :], in_=tri[:, :], compare_op=ALU.is_ge, fill=0.0, base=0,
                               pattern=[[1, P]], channel_multiplier=-1)
            pool.affine_select(out=after[:, :], in_=after[:, :], compare_op=ALU.is_gt, fill=0.0, base=0,
                               pattern=[[-1, P]], channel_multiplier=1)
            pool.affine_select(out=strip[:, S - P:S], in_=strip[:, S - P:S], compare_op=ALU.is_ge, fill=BIG, base=0,
                               pattern=[[-1, P]], channel_multiplier=1)
            pool.affine_select(out=future, in_=future, compare_op=ALU.is_ge, fill=LOW, base=0,
                               pattern=[[-1, P]], channel_multiplier=1)
            pool.drain()
            pool.sem_inc(consts_made, 1)
            power(*[("x", i) for i in range(TT)], "ckv")
            end_phase(pool)
            pool.wait_ge(phase_done, 4 * 1)
            end_phase(pool)
            pool.wait_ge(phase_done, 4 * 2)
            for u in uB:
                pool.memset(u[:, 0:CONV - 1], 0.0)
            pool.drain()
            pool.sem_inc(pads, 1)
            end_phase(pool)
            pool.wait_ge(phase_done, 4 * 3)
            NG = TT * GROUPS
            for n in range(NG + 4):
                c, g = n // GROUPS, n % GROUPS
                if n < NG:
                    if n >= 2:
                        pool.wait_ge(*completed(("sg", (n - 2) // GROUPS, (n - 2) % GROUPS)))
                    pool.tensor_tensor(out=step[n % 2].rearrange("p (h l) -> p h l", l=P),
                                       in0=bc(tri[:, :], HPG, 1), in1=bc(adt[:, c, HPG * g:HPG * (g + 1)], P),
                                       op=ALU.mult).then_inc(step_made, 1)
                if n >= 6 and (n - 6) % GROUPS == 0:
                    power(("ssd", (n - 6) // GROUPS))
            end_phase(pool)
            pool.wait_ge(phase_done, 4 * 4)
            end_phase(pool)
            pool.wait_ge(phase_done, 4 * 5)
            power(*[("h2", i) for i in range(TT)])
            end_phase(pool)
            pool.wait_ge(phase_done, 4 * 6)
            for j in range(FT):
                split_weights(("up", j, 0), ("up", j, 1))
            end_phase(pool)
            pool.wait_ge(phase_done, 4 * 7)
            for k in range(0, FT, 2):
                split_weights((("dn", 0), k))
                if k == 8:
                    power(("mem", 0), ("mem", 1))
            for k in range(0, 8, 2):
                split_weights((("dn", 1), k))
            power("memk")
            for k in range(8, FT, 2):
                split_weights((("dn", 1), k))
            for n in range(TT + 2):
                if n < TT:
                    power(("x3", n))
                if n >= 2:
                    power(("h3", n - 2))
            power("cc", "dd", "mqm")
            end_phase(pool)
            pool.wait_ge(phase_done, 4 * 8)
            for tt in range(TT):
                power(("mq", tt), ("mk", tt))
            end_phase(pool)
            pool.wait_ge(phase_done, 4 * 9)
            power("sub")
            end_phase(pool)
            pool.wait_ge(phase_done, 4 * 10)

        @block.scalar
        def _(act):
            def copy(out, name, src=None, func=ACT.Copy, scale=1.0):
                act.wait_ge(*completed(name))
                src = psum_of(name) if src is None else src
                act.activation(out, src, func, scale=scale).then_inc(empty(name), 1)

            def high_part(out, src):
                return act.activation(out, src, ACT.Copy).then_inc(high_made, 1)

            def square_sum(name, src, junk, k=None):
                act.drain()
                ins = act.activation(junk, src, ACT.Square, accum_out=stat_of(name, k))
                return ins

            def scale_tile(name, key, src, buf, tt, first=False):
                if not first and tt >= 2:
                    act.wait_ge(*completed((key, tt - 2, 1)))
                act.wait_ge(*rooted(name))
                r = stat_of(name)
                act.activation(buf[:, tt % 2, :], src, ACT.Copy, scale=r).then_inc(scaled, 1)

            junkA = at(18, D)
            for n in range(TT + 2):
                if n < TT:
                    act.wait_ge(x_in[n], 16)
                    square_sum(("x", n), x_tok[:, n, :], junkA).then_inc(squared, 1)
                if n >= 2:
                    scale_tile(("x", n - 2), "hx", x_tok[:, n - 2, :], hs, n - 2)
            act.wait_ge(*written("cols"))
            for tt in range(TT):
                for half in range(2):
                    act.wait_ge(*written(("hx", tt, half)))
            act.dma_start(hT_d, hT.rearrange("p k s -> p (k s)")).then_inc(hT_out, 16)
            act.drain()
            for half in range(2):
                copy(kiT[:, half * 512:half * 512 + 512], ("ki", half))
            for j in range(4):
                for half in range(2):
                    copy(qiT[:, j, half * 512:half * 512 + 512], ("qi", j, half))
            for tt in range(TT):
                copy(craw[:, tt, :], ("c", tt), psum_of(("c", tt))[:, 0:168])
            act.wait_ge(mean_ready, stat_n["ckv"])
            n = 0
            for i in range(2, TT):
                for h in range(IDXH):
                    if n >= 2:
                        act.wait_ge(relu_used, n - 1)
                    nk = (i + 1) * P
                    copy(rel[:, n % 2, 0:nk], ("ix", i, h), psum_of(("ix", i, h))[:, 0:nk], ACT.Relu)
                    n += 1
            for half in range(2):
                copy(ckvT[:, half * 512:half * 512 + 512], ("ckvT", half), scale=cols[:, 1, 43:44])
            for key, dst in (("ukT", ukT), ("uvT", uvT)):
                for half in range(2):
                    copy(dst[:, half * 512:half * 512 + 512], (key, half))
            for j in range(8):
                for half in range(2):
                    copy(qT[:, j, half * 512:half * 512 + 512], ("q", j, half), scale=-HD ** -0.5)
            act.wait_ge(bias_out, 16)
            n = 0
            for c in range(4):
                for tt in range(TT):
                    slot = n % 4
                    if n >= 4:
                        act.wait_ge(z_out[slot], 16 * (n // 4))
                    copy(zbuf[:, slot, :], ("z", c, tt), func=ACT.Silu)
                    act.wait_ge(*written(("z", c, tt)))
                    act.dma_start(z_d[tt * P:(tt + 1) * P, c * 512:(c + 1) * 512], zbuf[:, slot, :]).then_inc(z_out[slot], 16)
                    n += 1
            act.wait_ge(dt_steps, 1)
            act.activation(dtmp[1], dtmp[0], ACT.Exp, scale=-1.0)
            act.wait_ge(rows_in, 16 * len(ROWS))
            act.activation(r_alog, r_alog, ACT.Exp).then_inc(dt_steps, 1)
            act.wait_ge(dt_steps, 3)
            act.activation(dtmp[0], dtmp[2], ACT.Ln).then_inc(dt_steps, 1)
            for s in z_out:
                act.wait_ge(s, 16 * 8)
            act.wait_ge(hT_out, 16)
            end_phase(act)
            act.wait_ge(phase_done, 4 * 1)

            for j in range(8):
                for half in range(2):
                    copy(kT[:, j, half * 512:half * 512 + 512], ("kT", j, half))

            def attend(units, base):
                n = len(units)
                for s in range(n + 3):
                    if s < n:
                        u, g = units[s], base + s
                        scores_ring, probs_ring, _ = rings_of(g)
                        act.wait_ge(*written(("S", g)))
                        if s >= 3:
                            act.wait_ge(*completed(("T", g - 3, last_group(units[s - 3]))))
                        w = u["nk"] * P
                        act.activation(probs_ring[g % 3][:, 0:w], scores_ring[g % 2][:, 0:w], ACT.Exp, scale=-1.0,
                                       bias=negmax[:, g % 4:g % 4 + 1],
                                       accum_out=rsum[:, g % 8:g % 8 + 1]).then_inc(exp_ready, 1)
                    if 0 <= s - 3 and units[s - 3]["ph"] == "a" and units[s - 3]["h"] == HEADS - 1:
                        i = units[s - 3]["i"]
                        for half in range(2):
                            copy(attT[:, 4 * half:4 * half + 4, i * P:(i + 1) * P], ("aT", i, half),
                                 psum_of(("aT", i, half)).rearrange("p (a b) -> p a b", b=P))
                    if 0 <= s - 1 < n:
                        u, g = units[s - 1], base + s - 1
                        if s - 1 >= 3:
                            act.wait_ge(*completed(("O", g - 3)))
                        pT = rings_of(g)[2][g % 3]
                        for grp in range(last_group(u) + 1):
                            w = min(4, u["nk"] - 4 * grp) * P
                            copy(pT[:, grp * 512:grp * 512 + w], ("T", g, grp), psum_of(("T", g, grp))[:, 0:w])

            attend(units1, 0)
            act.wait_ge(*written(("aT", TT - 1, 1)))
            act.dma_start(attT_d, attT.rearrange("p k s -> p (k s)")).then_inc(attT_out, 16)
            act.wait_ge(attT_out, 16)
            end_phase(act)
            act.wait_ge(phase_done, 4 * 2)

            for j in range(XT + 1):
                if j < XT:
                    if j >= 2:
                        act.wait_ge(conv_ready, j - 1)
                    for half in range(2):
                        lo = CONV - 1 + half * 512
                        copy(uB[j % 2][:, lo:lo + 512], ("xc", j, half))
                if j >= 1:
                    act.wait_ge(conv_ready, j)
                    dst = xsT[:, j - 1, :] if j <= 16 else bT[:, j - 17, :] if j <= 20 else cT[:, j - 21, :]
                    act.activation(dst, accB[(j - 1) % 2], ACT.Silu).then_inc(conv_used, 1)
            end_phase(act)
            act.wait_ge(phase_done, 4 * 3)

            NG = TT * GROUPS
            for n in range(NG + 4):
                c, g = n // GROUPS, n % GROUPS
                if n < NG:
                    if g == 0:
                        copy(btok[c % 2], ("bt", c))
                        if c >= 3:
                            act.wait_ge(*written(("yo", c - 2, GROUPS - 1)))
                        if c >= 2:
                            act.wait_ge(*written(("st", c - 2, GROUPS - 1)))
                        copy(decay_out[:, c % 2, :], ("ea", c), psum_of(("ea", c))[:, 0:2 * SSMH], ACT.Exp)
                    if n >= 2:
                        act.wait_ge(*completed(("yd", (n - 2) // GROUPS, (n - 2) % GROUPS)))
                    copy(mix[n % 2], ("sg", c, g), func=ACT.Exp)
                if n >= 5 and (n - 5) % GROUPS == 0:
                    cc = (n - 5) // GROUPS
                    act.wait_ge(gated, cc + 1)
                    for gg in range(GROUPS):
                        ins = square_sum(("ssd", cc), yb[cc % 2][:, gg * 512:(gg + 1) * 512], junk, gg)
                    ins.then_inc(squared, 1)
                if n >= 7 and (n - 7) % GROUPS == 0:
                    cc = (n - 7) // GROUPS
                    for q in range(4):
                        act.wait_ge(*completed(("yt", cc, q)))
                        src = psum_of(("yt", cc, q))
                        for m in range(4):
                            ins = act.activation(yT[:, 4 * q + m, cc * P:(cc + 1) * P], src[:, m * P:(m + 1) * P], ACT.Copy,
                                                 scale=cols[:, 1, 4 * q + m:4 * q + m + 1])
                        ins.then_inc(empty(("yt", cc, q)), 1)
            end_phase(act)
            act.wait_ge(phase_done, 4 * 4)

            for j in range(KT):
                if j >= 1:
                    act.wait_ge(merged_ready, j)
                copy(gate_s, ("gs", j), func=ACT.Sigmoid)
                copy(mergedT[:, j, :], ("ga", j), func=ACT.Sigmoid)
            end_phase(act)
            act.wait_ge(phase_done, 4 * 5)

            for n in range(TT + 1):
                if n < TT:
                    act.wait_ge(*written(("o", 1, n)))
                    square_sum(("h2", n), x1[:, n, :], junkE).then_inc(squared, 1)
                if n >= 1:
                    scale_tile(("h2", n - 1), "h2", x1[:, n - 1, :], hsE, n - 1)
            act.dma_start(x1_d, x1.rearrange("p a n -> p (a n)")).then_inc(x1_out, 16)
            act.wait_ge(x1_out, 16)
            end_phase(act)
            act.wait_ge(phase_done, 4 * 6)

            for k in range(KT):
                high_part(h2hi[k], h2T[:, k, :])
            for j in range(FT):
                act.wait_ge(*written(("ug", j)))
                g = actT[:, j, :]
                act.activation(g, g, ACT.Silu).then_inc(silu_made, 1)
            end_phase(act)
            act.wait_ge(phase_done, 4 * 7)

            act.dma_start(memx, t["mem_2"][0].rearrange("(a p) n -> p a n", p=P)).then_inc(mem_in, 16)
            act.dma_start(x1.rearrange("p a n -> p (a n)"), x1_d).then_inc(back_in[2], 16)
            for k in range(FT):
                if k >= 2:
                    act.wait_ge(dn_spent, down_step(0, k - 2))
                high_part(act_parts[0][k % 2][0], actT[:, k, :])
                if k == 3:
                    act.wait_ge(mem_in, 16)
                    for tt in range(2):
                        square_sum(("mem", tt), memx[:, tt, :], hs3[:, tt, :]).then_inc(squared, 1)
                    act.drain()
                if k == 14:
                    for tt in range(2):
                        scale_tile(("mem", tt), "mx", memx[:, tt, :], hs3, tt)
            act.wait_ge(*completed(("dn", 0, TT - 1)))
            nf = t["norm_final"]
            act.dma_start(nfb, bass.AP(nf.tensor, nf.offset, [[0, P], [1, D]])).then_inc(nf_in, 16)
            lv = t["diff_lambda_2"]
            act.dma_start(lamv, bass.AP(lv.tensor, lv.offset, [[0, P], [32, 4], [1, 32]])).then_inc(pos_in, 16)
            act.dma_start(pos_i, t["positions_2"][0].rearrange("(a p) -> p a", p=P),
                          allow_slow_non_contiguous=True).then_inc(pos_in, 16)
            for tt in range(2):
                copy(memkv[:, tt, :], ("mem", tt))
            act.drain()
            for k in range(FT):
                if k >= 2:
                    act.wait_ge(dn_spent, down_step(1, k - 2))
                high_part(act_parts[1][k % 2][0], actT[:, k, :])
                if k == 1:
                    copy(kmT.rearrange("p a b -> p (a b)"), ("kmT",))
            act.wait_ge(*completed(("dn", 1, TT - 1)))
            for n in range(TT + 3):
                if n < TT:
                    act.wait_ge(*written(("dn", 1, n)))
                    square_sum(("x3", n), x1[:, n, :], junkG).then_inc(squared, 1)
                if 2 <= n < TT + 2:
                    act.wait_ge(resid, n - 1)
                    square_sum(("h3", n - 2), x1[:, n - 2, :], junkG).then_inc(squared, 1)
                if n >= 3:
                    if n < 5:
                        act.wait_ge(*completed(("mx", n - 3, 1)))
                    scale_tile(("h3", n - 3), "h3", x1[:, n - 3, :], hs3, n - 3)
            act.dma_start(x3_d, x1.rearrange("p a n -> p (a n)")).then_inc(x3_out, 16)
            act.drain()
            for c in range(len(IN2)):
                for tt in range(TT):
                    name = ("in2", c, tt)
                    if c == 0:
                        copy(pA[:, tt, :], name, psum_of(name)[:, 0:416])
                    elif c < 3:
                        copy(pB[:, tt, 512 * (c - 1):512 * c], name)
                    else:
                        copy(pZ[:, tt, 512 * (c - 3):512 * (c - 2)], name, func=ACT.Silu)
                if c == 0:
                    act.wait_ge(angle, 1)
                    act.activation(trigT[3], trigT[1], ACT.Sin)
                    act.activation(trigT[4], trigT[1], ACT.Sin, scale=0.5)
                    act.activation(lam[:, 2:4], lam[:, 0:2], ACT.Exp).then_inc(trig, 1)
            for x in (0, 1, 2, 3, 6, 7):
                for half in range(2):
                    name = ("dT", x, half)
                    scale = -DD ** -0.5 if x < 2 else 1.0 if x < 4 else -64 ** -0.5
                    copy(pB[:, 4 * half:4 * half + 4, x * P:(x + 1) * P], name,
                         psum_of(name).rearrange("p (a b) -> p a b", b=P), scale=scale)
            act.wait_ge(x3_out, 16)
            end_phase(act)
            act.wait_ge(phase_done, 4 * 8)
            for k in range(3):
                for half in range(2):
                    dst = cqT[:, k, :] if k < 2 else ckv2T
                    copy(dst[:, half * 512:half * 512 + 512], ("cqT", k, half), scale=cols[:, 1, 40 + k:41 + k])
            for tt in range(TT):
                if tt:
                    act.wait_ge(*completed(("qTm", tt - 1, 1)))
                copy(qtok, ("uq", tt), psum_of(("uq", tt))[:, 0:768])
                if tt:
                    act.wait_ge(*completed(("kTm", tt - 1, 1)))
                act.wait_ge(*completed(("ukv", tt)))
                src = psum_of(("ukv", tt)).rearrange("p (h c) -> p h c", c=128)
                kh = ktok.rearrange("p (h c) -> p h c", c=MQK)
                act.activation(vM[:, tt, :].rearrange("p (h c) -> p h c", c=64), src[:, :, 64:128], ACT.Copy)
                act.activation(kh[:, :, 64:96], bc(pA[:, tt, 384:416], MLAH, 1), ACT.Copy)
                copy(kh[:, :, 0:64], ("ukv", tt), src[:, :, 0:64])
                for key, dst, scale in (("qTm", qTm, -MQK ** -0.5), ("kTm", kTm, 1.0)):
                    for half in range(2):
                        name = (key, tt, half)
                        copy(dst[0:MQK, 4 * half:4 * half + 4, tt * P:(tt + 1) * P], name,
                             psum_of(name)[0:MQK, :].rearrange("p (a b) -> p a b", b=P), scale=scale)
            end_phase(act)
            act.wait_ge(phase_done, 4 * 9)
            attend(units2, N1)
            end_phase(act)
            act.wait_ge(phase_done, 4 * 10)
            for tt in range(TT):
                for half in range(2):
                    name = ("yT2", tt, half)
                    copy(yT2[:, 4 * half:4 * half + 4, tt * P:(tt + 1) * P], name,
                         psum_of(name).rearrange("p (a b) -> p a b", b=P))

        @block.vector
        def _(dve):
            def tt_(out, a, b, op):
                return dve.tensor_tensor(out=out, in0=a, in1=b, op=op)

            def stt(out, a, scalar, b, op0, op1):
                return dve.scalar_tensor_tensor(out=out, in0=a, scalar=scalar, in1=b, op0=op0, op1=op1)

            def mean(name, n):
                v = stat_of(name)
                dve.tensor_scalar(v, v, 1.0 / n, EPS, ALU.mult, ALU.add).then_inc(mean_ready, 1)

            def heads(ap, n):
                return ap.rearrange("p (h c) -> p h c", h=n)

            def with_gain(key, dst, m, col, tiles):
                for tt in tiles:
                    for half in range(2):
                        dve.wait_ge(*completed((key, tt, half)))
                        src = psum_of((key, tt, half)).rearrange("p (a b) -> p a b", b=P)
                        g = cols[:, m, col + 4 * half:col + 4 * half + 4]
                        tt_(dst[:, 4 * half:4 * half + 4, tt * P:(tt + 1) * P], src, bc(g, P), ALU.mult).then_inc(empty((key, tt, half)), 1)

            for b in range(8):
                dve.sem_inc(evacuated[b], 1)
            dve.wait_ge(*completed("cols"))
            src = psum_of("cols")
            for m, r in enumerate(COL_ROWS):
                ins = dve.tensor_copy(cols[:, m, 0:r], src[:, m * P:m * P + r])
            ins.then_inc(empty("cols"), 1)
            dve.wait_ge(*completed("bias"))
            dve.tensor_copy(bias_row[0:HEADS, :], psum_of("bias")[0:HEADS, 0:384]).then_inc(empty("bias"), 1)
            dve.drain()
            for n in range(TT):
                dve.wait_ge(squared, squared_n[("x", n)])
                mean(("x", n), D)
            with_gain("hx", hT, 0, 120, range(TT))

            dve.wait_ge(*written(("c", TT - 1)))
            c_lat = craw[:, :, 0:LAT]
            sq = rel[:, 0, :].rearrange("p (a b) -> p a b", b=LAT)
            tt_(sq, c_lat, c_lat, ALU.mult)
            dve.drain()
            dve.reduce_sum(stat_of("ckv"), sq, axis=AX.X)
            dve.drain()
            mean("ckv", LAT)
            dve.wait_ge(*rooted("ckv"))
            tt_(c_lat, c_lat, bc(stat_of("ckv"), LAT), ALU.mult).then_inc(heads_ready, 1)

            n = 0
            for i in range(2, TT):
                nk = (i + 1) * P
                sc = scores[:, score_off[i]:score_off[i] + nk]
                for h in range(IDXH):
                    dve.wait_ge(*written(("ix", i, h)))
                    w = craw[:, i, LAT + h:LAT + h + 1]
                    if h == 0:
                        dve.tensor_scalar(sc, rel[:, n % 2, 0:nk], w, None, ALU.mult).then_inc(relu_used, 1)
                    else:
                        stt(sc, rel[:, n % 2, 0:nk], w, sc, ALU.mult, ALU.add).then_inc(relu_used, 1)
                    dve.drain()
                    n += 1
                tt_(sc[:, nk - P:nk], sc[:, nk - P:nk], future, ALU.add)
                dve.drain()
            for i in range(2, TT):
                nk = (i + 1) * P
                sc = scores[:, score_off[i]:score_off[i] + nk]
                with dve.Fori(0, TOPK // 8):
                    dve.max(rinv[:, :], sc)
                    dve.drain()
                    dve.match_replace(sc, rinv[:, :], sc, TAKEN)
                    dve.drain()
                dve.tensor_scalar(negmask[:, score_off[i]:score_off[i] + nk], sc, SPLIT, BIG, ALU.is_gt, ALU.mult)
            dve.wait_ge(rows_in, 16 * len(ROWS))
            f0, f1, f2, f3 = dtmp
            tt_(dt, craw[:, :, LAT + IDXH:LAT + IDXH + SSMH], bc(r_dtb, TT, 1), ALU.add)
            dve.drain()
            v3 = lambda f: f.rearrange("p (a b) -> p a b", b=SSMH)
            stt(v3(f0), dt, -1.0, dt, ALU.mult, ALU.max)
            dve.tensor_scalar(dt, dt, 0.0, None, ALU.max)
            dve.drain()
            dve.sem_inc(dt_steps, 1)
            dve.wait_ge(dt_steps, 2)
            dve.tensor_scalar(f2, f1, 1.0, None, ALU.add)
            dve.drain()
            dve.tensor_scalar(f3, f2, 1.0, None, ALU.subtract).then_inc(dt_steps, 1)
            dve.wait_ge(dt_steps, 4)
            dve.drain()
            dve.tensor_scalar(f2, f3, 0.0, None, ALU.is_equal)
            dve.drain()
            tt_(f3, f3, f2, ALU.add)
            dve.drain()
            dve.reciprocal(f3, f3)
            dve.drain()
            tt_(f0, f0, f3, ALU.mult)
            dve.drain()
            tt_(f0, f0, f2, ALU.add)
            dve.drain()
            tt_(f0, f0, f1, ALU.mult)
            dve.drain()
            tt_(dt, dt, v3(f0), ALU.add)
            dve.drain()
            stt(adt, dt, -1.0, bc(r_alog, TT, 1), ALU.mult, ALU.mult)
            end_phase(dve)
            dve.wait_ge(phase_done, 4 * 1)

            for tt in range(TT):
                for half in range(2):
                    dve.wait_ge(*completed(("v", tt, half)))
                    dve.tensor_copy(v[:, tt, half * 512:half * 512 + 512], psum_of(("v", tt, half))).then_inc(empty(("v", tt, half)), 1)
            dve.wait_ge(bias_in, 16)

            def attend(units, base):
                n = len(units)
                for s in range(n + 3):
                    if s < n:
                        u, g = units[s], base + s
                        w = u["nk"] * P
                        dve.wait_ge(*completed(("S", g)))
                        out = psum_of(("S", g))
                        if u["ph"] == "a":
                            lo = max(0, w - 256)
                            tt_(out[:, lo:w], out[:, lo:w], biasT[:, u["h"], 256 - (w - lo):256], ALU.subtract)
                            dve.drain()
                        if g >= 2:
                            dve.wait_ge(exp_ready, g - 1)
                        dve.tensor_tensor_reduce(
                            out=rings_of(g)[0][g % 2][:, 0:w], in0=out[:, 0:w], in1=u["mask"], scale=1.0, scalar=3e38,
                            op0=ALU.add, op1=ALU.min, accum_out=negmax[:, g % 4:g % 4 + 1]).then_inc(empty(("S", g)), 1)
                    if s >= 3:
                        u, g = units[s - 3], base + s - 3
                        i, h = u["i"], u["h"]
                        dve.wait_ge(exp_ready, g + 1)
                        r = rinv[:, g % 8:g % 8 + 1]
                        dve.reciprocal(r, rsum[:, g % 8:g % 8 + 1])
                        dve.drain()
                        dve.wait_ge(*completed(("O", g)))
                        o = psum_of(("O", g))[:, 0:64]
                        if u["ph"] == "a":
                            if h == 0 and i:
                                dve.wait_ge(*completed(("aT", i - 1, 1)))
                            ins = dve.tensor_scalar(att[:, 0, h * 64:h * 64 + 64], o, r, None, ALU.mult)
                        elif u["ph"] == "m":
                            z = pZ[:, i, h * 64:h * 64 + 64]
                            ins = stt(z, o, r, z, ALU.mult, ALU.mult)
                        elif u["ph"] == "e":
                            z = pZ[:, i, 768 + h * 64:832 + h * 64]
                            ins = stt(z, o, r, z, ALU.mult, ALU.mult)
                        else:
                            d = od[:, i, (h // 2) * 64:(h // 2) * 64 + 64]
                            if h % 2 == 0:
                                ins = dve.tensor_scalar(d, o, r, None, ALU.mult)
                            else:
                                tt_(r, r, lam[:, 4:5], ALU.mult)
                                dve.drain()
                                ins = stt(d, o, r, d, ALU.mult, ALU.add)
                        ins.then_inc(empty(("O", g)), 1)

            attend(units1, 0)
            end_phase(dve)
            dve.wait_ge(phase_done, 4 * 2)

            dve.wait_ge(pads, 1)
            for j in range(XT):
                dve.wait_ge(*written(("xc", j, 0)))
                dve.wait_ge(*written(("xc", j, 1)))
                if j >= 2:
                    dve.wait_ge(conv_used, j - 1)
                a, u = accB[j % 2], uB[j % 2]
                dve.tensor_scalar(a, u[:, 3:3 + S], cols[:, 0, 3 * XT + j:3 * XT + j + 1],
                                  cols[:, 0, CONV * XT + j:CONV * XT + j + 1], ALU.mult, ALU.add)
                for m in (2, 1, 0):
                    dve.drain()
                    ins = stt(a, u[:, m:m + S], cols[:, 0, m * XT + j:m * XT + j + 1], a, ALU.mult, ALU.add)
                ins.then_inc(conv_ready, 1)
            end_phase(dve)
            dve.wait_ge(phase_done, 4 * 3)

            NG = TT * GROUPS
            tri4 = bc(tri[:, :], GROUPS, 1)

            def ssd_front(c):
                for g in range(GROUPS):
                    dve.wait_ge(*completed(("xt", c, g)))
                    src = heads(psum_of(("xt", c, g)), HPG)
                    span = slice(g * 512, (g + 1) * 512)
                    hs_ = slice(HPG * g, HPG * (g + 1))
                    if g == 0 and c >= 2:
                        dve.wait_ge(*completed(("yt", c - 2, 3)))
                    tt_(heads(yb[c % 2][:, span], HPG), src, bc(r_dskip[:, hs_], 64), ALU.mult)
                    tt_(heads(xdt[c % 2][:, span], HPG), src, bc(dt[:, c, hs_], 64), ALU.mult).then_inc(empty(("xt", c, g)), 1)
                dve.wait_ge(*completed(("cb", c)))
                tt_(heads(cbm[c % 2], GROUPS), heads(psum_of(("cb", c)), GROUPS), tri4, ALU.mult).then_inc(empty(("cb", c)), 1)
                dve.drain()

            def ssd_mix(n):
                c, g = n // GROUPS, n % GROUPS
                dve.wait_ge(*written(("sg", c, g)))
                m = heads(mix[n % 2], HPG)
                tail = m[:, :, P - 1:P].broadcast_to([P, HPG, 64])
                if c < TT - 1:
                    if n >= 2:
                        dve.wait_ge(*completed(("st", (n - 2) // GROUPS, (n - 2) % GROUPS)))
                    tt_(heads(xds[n % 2], HPG), heads(xdt[c % 2][:, g * 512:(g + 1) * 512], HPG), tail, ALU.mult)
                    dve.drain()
                tt_(m, m, bc(cbm[c % 2][:, g * P:(g + 1) * P], HPG, 1), ALU.mult).then_inc(mixed, 1)

            def ssd_tail(n):
                c, g = n // GROUPS, n % GROUPS
                span = slice(g * 512, (g + 1) * 512)
                hs_ = slice(HPG * g, HPG * (g + 1))
                y = yb[c % 2][:, span]
                dve.wait_ge(*completed(("yd", c, g)))
                tt_(y, y, psum_of(("yd", c, g)), ALU.add).then_inc(empty(("yd", c, g)), 1)
                dve.wait_ge(*written(("ea", c)))
                h = state[:, span]
                if c:
                    dve.wait_ge(*completed(("yo", c, g)))
                    tt_(heads(yoff, HPG), heads(psum_of(("yo", c, g)), HPG), bc(decay_out[:, c % 2, hs_], 64),
                             ALU.mult).then_inc(empty(("yo", c, g)), 1)
                    if c < TT - 1:
                        tt_(heads(h, HPG), heads(h, HPG), bc(decay_out[:, c % 2, SSMH + HPG * g:SSMH + HPG * (g + 1)], 64),
                            ALU.mult)
                    dve.drain()
                    tt_(y, y, yoff, ALU.add)
                if c < TT - 1:
                    dve.wait_ge(*completed(("st", c, g)))
                    src = psum_of(("st", c, g))
                    (tt_(h, h, src, ALU.add) if c else dve.tensor_copy(h, src)).then_inc(empty(("st", c, g)), 1)
                dve.drain()

            for n in range(NG + 3):
                c, g = n // GROUPS, n % GROUPS
                if n < NG:
                    if g == 0:
                        ssd_front(c)
                    ssd_mix(n)
                if 1 <= n <= NG:
                    ssd_tail(n - 1)
                if n >= 4 and (n - 4) % GROUPS == 0:
                    cc = (n - 4) // GROUPS
                    dve.wait_ge(z_in[cc % 2], 16 * (cc // 2 + 1))
                    tt_(yb[cc % 2], yb[cc % 2], zc[cc % 2], ALU.mult).then_inc(gated, 1)
                if n >= 6 and (n - 6) % GROUPS == 0:
                    cc = (n - 6) // GROUPS
                    dve.wait_ge(squared, squared_n[("ssd", cc)])
                    mean(("ssd", cc), INNER // GROUPS)
                    y = heads(yb[cc % 2], GROUPS)
                    dve.wait_ge(*rooted(("ssd", cc)))
                    tt_(y, y, bc(stat_of(("ssd", cc)), 512), ALU.mult).then_inc(ynorm, 1)
            end_phase(dve)
            dve.wait_ge(phase_done, 4 * 4)

            for j in range(KT):
                dve.wait_ge(*written(("gs", j)))
                dve.wait_ge(*completed(("so", j)))
                tt_(gate_s, gate_s, psum_of(("so", j)), ALU.mult).then_inc(empty(("so", j)), 1)
                dve.wait_ge(*written(("ga", j)))
                m = mergedT[:, j, :]
                dve.wait_ge(*completed(("ao", j)))
                tt_(m, m, psum_of(("ao", j)), ALU.mult).then_inc(empty(("ao", j)), 1)
                dve.drain()
                tt_(m, m, gate_s, ALU.add).then_inc(merged_ready, 1)
            end_phase(dve)
            dve.wait_ge(phase_done, 4 * 5)

            def add_to(x, key, c, tt):
                part = x[:, tt, c * 512:(c + 1) * 512]
                dve.wait_ge(*completed((key, c, tt)))
                tt_(part, part, psum_of((key, c, tt)), ALU.add).then_inc(empty((key, c, tt)), 1)

            dve.wait_ge(x_again, 16)
            for tt in range(TT):
                add_to(x1, "o", 0, tt)
            for n in range(TT + 2):
                if n < TT:
                    add_to(x1, "o", 1, n)
                    dve.wait_ge(squared, squared_n[("h2", n)])
                    mean(("h2", n), D)
                if n >= 2:
                    with_gain("h2", h2T, 1, 16, [n - 2])
            end_phase(dve)
            dve.wait_ge(phase_done, 4 * 6)

            def low_part(name, out, src, high_part):
                dve.wait_ge(*high(name))
                return tt_(out, src, high_part.bitcast(F32), ALU.subtract).then_inc(parts_made, 1)

            for k in range(KT):
                low_part(("h2", k), h2lo[k], h2T[:, k, :], h2hi[k])

            def gate_times_value(j):
                dve.wait_ge(silu_made, j + 1)
                tt_(actT[:, j, :], actT[:, j, :], accF[j % 2], ALU.mult)

            for j in range(FT):
                pair = [(actT[:, j, :], ("ug", j), j), (accF[j % 2], ("uv", j), FT + j)]
                for a, name, ch in pair:
                    dve.wait_ge(*completed(name))
                    u = psum_of(name)
                    dve.tensor_scalar(a, u, cols[:, 3, ch:ch + 1], cols[:, 1, 44 + ch:45 + ch], ALU.mult, ALU.add)
                    dve.drain()
                    if name[0] == "ug" and j >= 1:
                        gate_times_value(j - 1)
                    for m in (1, 0):
                        if m == 0:
                            dve.drain()
                        ins = stt(a[:, 2 - m:S], u[:, 0:S - 2 + m], cols[:, 2, 44 * m + ch:44 * m + ch + 1], a[:, 2 - m:S],
                                  ALU.mult, ALU.add)
                    ins.then_inc(empty(name), 1)
            dve.drain()
            gate_times_value(FT - 1)
            end_phase(dve)
            dve.wait_ge(phase_done, 4 * 7)

            for k in range(FT):
                hi, lo = act_parts[0][k % 2]
                low_part(("act", 0, k), lo, actT[:, k, :], hi)
                if k == 5:
                    for tt in range(2):
                        dve.wait_ge(squared, squared_n[("mem", tt)])
                        mean(("mem", tt), D)
            dve.wait_ge(back_in[2], 16)
            for tt in range(TT):
                add_to(x1, "dn", 0, tt)
            with_gain("mx", memT, 1, 32, range(2))
            dve.wait_ge(*written(("mem", 1)))
            km = memkv[:, :, 0:256].rearrange("p a (h c) -> p a h c", c=64)
            sq4 = dsq[:, 0:512].rearrange("p (a h c) -> p a h c", a=2, c=64)
            tt_(sq4, km, km, ALU.mult)
            dve.drain()
            dve.reduce_sum(stat_of("memk"), dsq[:, 0:512].rearrange("p (a c) -> p a c", c=64), axis=AX.X)
            dve.drain()
            mean("memk", 64)
            dve.wait_ge(*rooted("memk"))
            r = stat_of("memk").rearrange("p (a h) -> p a h", a=2)
            for tt in range(2):
                tt_(km[:, tt], km[:, tt], bc(r[:, tt], 64), ALU.mult)
            dve.drain()
            for tt in range(2):
                ins = tt_(km[:, tt], km[:, tt], bc(r_mkn, 4, 1), ALU.mult)
            ins.then_inc(sq_ready, 1)
            for k in range(FT):
                hi, lo = act_parts[1][k % 2]
                low_part(("act", 1, k), lo, actT[:, k, :], hi)
            for tt in range(TT):
                add_to(x1, "dn", 1, tt)
            dve.wait_ge(nf_in, 16)
            for n in range(TT + 2):
                if n < TT:
                    dve.wait_ge(squared, squared_n[("x3", n)])
                    mean(("x3", n), D)
                if 1 <= n < TT + 1:
                    dve.wait_ge(*rooted(("x3", n - 1)))
                    stt(x1[:, n - 1, :], x1[:, n - 1, :], stat_of(("x3", n - 1), 0), nfb, ALU.mult, ALU.mult)\
                        .then_inc(resid, 1)
                if n >= 2:
                    dve.wait_ge(squared, squared_n[("h3", n - 2)])
                    mean(("h3", n - 2), D)
            dve.wait_ge(pos_in, 32)
            freq = np.power(np.float32(THETA), -np.arange(0, ROPE, 2, dtype=np.float32) / np.float32(ROPE))
            for n in range(ROPE // 2):
                dve.memset(invf[:, n:n + 1], float(freq[n]))
            dve.tensor_copy(posf, pos_i)
            dve.drain()
            ang, red, turns = trigT[0], trigT[1], trigT[2]
            tt_(ang, bc(posf, 16), bc(invf, TT, 1), ALU.mult)
            dve.drain()
            magic = 1.5 * 2.0 ** 23
            dve.tensor_scalar(turns, ang, 1.0 / (2.0 * math.pi), magic, ALU.mult, ALU.add)
            dve.drain()
            dve.tensor_scalar(turns, turns, magic, None, ALU.subtract)
            dve.drain()
            c1, c2 = 6.28125, 0.0019350051879882812
            for k, (to, frm) in zip((c1, c2, 2.0 * math.pi - c1 - c2), ((red, ang), (red, red), (red, red))):
                stt(to, turns, -k, frm, ALU.mult, ALU.add)
                dve.drain()
            dve.tensor_scalar(red, red, 3.1415925, -3.1415925, ALU.min, ALU.max)
            for n in range(2):
                dve.tensor_tensor_reduce(out=dsq[:, 32 * n:32 * n + 32], in0=lamv[:, 2 * n, :], in1=lamv[:, 2 * n + 1, :],
                                         scale=1.0, scalar=0.0, op0=ALU.mult, op1=ALU.add, accum_out=lam[:, n:n + 1])
            dve.drain()
            dve.sem_inc(angle, 1)
            with_gain("h3", h3T, 1, 24, range(TT))
            dve.wait_ge(trig, 1)
            dve.tensor_copy(sinb, trigT[3])
            tt_(trigT[0], trigT[4], trigT[4], ALU.mult)
            tt_(lam[:, 4:5], lam[:, 3:4], lam[:, 2:3], ALU.subtract)
            dve.drain()
            dve.tensor_scalar(cosb, trigT[0], -2.0, 1.0, ALU.mult, ALU.add)
            dve.tensor_scalar(lam[:, 4:5], lam[:, 4:5], LAM0, None, ALU.subtract)
            dve.drain()

            for tt in range(TT):
                dve.wait_ge(*written(("in2", 0, tt)))
                for k, (lo, hi) in enumerate(((0, 256), (256, 384))):
                    dve.tensor_tensor_reduce(out=dsq[:, lo:hi], in0=pA[:, tt, lo:hi], in1=pA[:, tt, lo:hi], scale=1.0,
                                             scalar=0.0, op0=ALU.mult, op1=ALU.add, accum_out=stat_of("cc", TT * k + tt))
                dve.drain()
            cc = stat_of("cc")
            dve.tensor_scalar(cc[:, 0:TT], cc[:, 0:TT], 1.0 / 256, None, ALU.mult)
            dve.tensor_scalar(cc[:, TT:2 * TT], cc[:, TT:2 * TT], 1.0 / 128, None, ALU.mult)
            dve.drain()
            mean("cc", 1)
            dve.wait_ge(*rooted("cc"))
            tt_(pA[:, :, 0:256], pA[:, :, 0:256], bc(cc[:, 0:TT], 256), ALU.mult)
            tt_(pA[:, :, 256:384], pA[:, :, 256:384], bc(cc[:, TT:2 * TT], 128), ALU.mult).then_inc(heads_ready, 1)

            def rotate(x, tt, n, tmp):
                c = cosb[:, tt, :].unsqueeze(1).unsqueeze(1).broadcast_to([P, n, 2, 16])
                s = sinb[:, tt, :].unsqueeze(1).unsqueeze(1).broadcast_to([P, n, 2, 16])
                tm = tmp[:, 0:n * 32].rearrange("p (h a c) -> p h a c", a=2, c=16)
                tt_(tm, x, s, ALU.mult)
                tt_(x, x, c, ALU.mult)
                dve.drain()
                tt_(x[:, :, 0, :], x[:, :, 0, :], tm[:, :, 1, :], ALU.subtract)
                return tt_(x[:, :, 1, :], x[:, :, 1, :], tm[:, :, 0, :], ALU.add)

            for tt in range(TT):
                dve.wait_ge(*written(("in2", 1, tt)))
                d = pB[:, tt, 0:512]
                tt_(dsq[:, 0:512], d, d, ALU.mult)
                dve.drain()
                dve.reduce_sum(stat[:, 98 + 16 * tt:114 + 16 * tt], heads(dsq[:, 0:512], 16), axis=AX.X)
                dve.drain()
            mean_dd = stat_of("dd")
            mean("dd", DD)
            dve.wait_ge(*rooted("dd"))
            for tt in range(TT):
                d = heads(pB[:, tt, 0:512], 16)
                tt_(d, d, bc(mean_dd[:, 16 * tt:16 * tt + 16], DD), ALU.mult)
                dve.drain()
                tt_(d[:, 0:8], d[:, 0:8], bc(r_dqn, 8, 1), ALU.mult)
                tt_(d[:, 8:16], d[:, 8:16], bc(r_dkn, 8, 1), ALU.mult)
                dve.drain()
                rotate(pB[:, tt, 0:512].rearrange("p (h a c) -> p h a c", a=2, c=16), tt, 16, dsq)
                dve.drain()
            for tt in range(TT):
                dve.wait_ge(*written(("in2", 2, tt)))
                q = pB[:, tt, 768:1024]
                tt_(dsq[:, 0:256], q, q, ALU.mult)
                dve.drain()
                dve.reduce_sum(stat[:, 16 + 4 * tt:20 + 4 * tt], heads(dsq[:, 0:256], 4), axis=AX.X)
                dve.drain()
            dve.drain()
            mean("mqm", 64)
            dve.wait_ge(*rooted("mqm"))
            for tt in range(TT):
                q = heads(pB[:, tt, 768:1024], 4)
                tt_(q, q, bc(stat_of("mqm")[:, 4 * tt:4 * tt + 4], 64), ALU.mult)
            dve.drain()
            for tt in range(TT):
                q = heads(pB[:, tt, 768:1024], 4)
                ins = tt_(q, q, bc(r_mqn, 4, 1), ALU.mult)
            ins.then_inc(heads_ready, 1)
            dve.drain()
            end_phase(dve)
            dve.wait_ge(phase_done, 4 * 8)

            for tt in range(TT):
                sides = (("mq", qtok, r_qn, ("uq", tt)), ("mk", ktok, r_kn, ("ukv", tt)))
                for key, x, gain, name in sides:
                    dve.wait_ge(*written(name))
                    dve.drain()
                    tt_(htmp, x, x, ALU.mult)
                    dve.drain()
                    dve.reduce_sum(stat_of((key, tt)), heads(htmp, MLAH), axis=AX.X)
                    dve.drain()
                    mean((key, tt), MQK)
                for key, x, gain, name in sides:
                    xh = heads(x, MLAH)
                    dve.wait_ge(*rooted((key, tt)))
                    tt_(xh, xh, bc(stat_of((key, tt)), MQK), ALU.mult)
                    dve.drain()
                    tt_(xh, xh, bc(gain, MLAH, 1), ALU.mult)
                    dve.drain()
                    rotate(xh[:, :, 64:96].rearrange("p h (a c) -> p h a c", a=2), tt, MLAH, htmp).then_inc(heads_ready, 1)
            end_phase(dve)
            dve.wait_ge(phase_done, 4 * 9)
            attend(units2, N1)

            dve.drain()
            tt_(odsq, od, od, ALU.mult)
            dve.drain()
            dve.reduce_sum(stat_of("sub"), odsq.rearrange("p a (h c) -> p (a h) c", c=64), axis=AX.X)
            dve.drain()
            mean("sub", 64)
            o3 = od.rearrange("p a (h c) -> p (a h) c", c=64)
            dve.wait_ge(*rooted("sub"))
            tt_(o3, o3, bc(stat_of("sub"), 64), ALU.mult)
            dve.drain()
            tt_(o3, o3, bc(r_sub, 32, 1), ALU.mult)
            dve.drain()
            zd = pZ[:, :, 512:768]
            stt(zd, od, 1.0 - LAM0, zd, ALU.mult, ALU.mult)
            end_phase(dve)
            dve.wait_ge(phase_done, 4 * 10)

            dve.wait_ge(back_in[3], 16)
            for c in range(2):
                for tt in range(TT):
                    add_to(xo, "o2", c, tt)



_INS = ["x", "rel_bias", "norm_mix", "w_in", "kv_norm", "w_uk", "w_uv", "conv_ssm_w", "conv_ssm_b", "dt_bias",
        "a_log", "d_skip", "ssm_norm", "w_att_out", "w_ssm_out", "w_out", "norm_ffn", "w_ffn_up", "conv_ffn_w",
        "conv_ffn_b", "w_ffn_down", "norm_final", "mem_2", "positions_2", "norm_g_2", "w_in_2", "mla_q_norm_g_2",
        "mla_kv_norm_g_2", "w_uq_2", "w_ukv_2", "mla_qn_g_2", "mla_kn_g_2", "diff_qn_g_2", "diff_kn_g_2",
        "diff_lambda_2", "diff_subln_g_2", "mem_norm_g_2", "w_mem_kv_2", "mem_qn_g_2", "mem_kn_g_2", "w_out_2"]


def kernel(**inputs):
    import concourse.bacc as bacc
    from concourse.bass_utils import run_bass_kernel_spmd

    nc = bacc.Bacc("TRN2", target_bir_lowering=False, num_devices=1)
    arrays = {name: np.ascontiguousarray(inputs[name]) for name in _INS}
    arrays["buckets"] = bucket_table()
    t = {name: nc.dram_tensor(f"in_{name}", a.shape, mybir.dt.from_np(a.dtype), kind="ExternalInput").ap()
         for name, a in arrays.items()}
    t["out"] = nc.dram_tensor("out_0", (1, S, D), F32, kind="ExternalOutput").ap()
    hybrid_two_blocks(nc, t)
    r = run_bass_kernel_spmd(nc, [{f"in_{name}": a for name, a in arrays.items()}], core_ids=[0])
    return r.results[0]["out_0"]
```

```python
import math
from contextlib import ExitStack

import numpy as np
import concourse.bass as bass
from concourse import mybir

F32 = mybir.dt.float32
BF16 = mybir.dt.bfloat16
I32 = mybir.dt.int32
F32R = mybir.dt.float32r
ALU = mybir.AluOpType
ACT = mybir.ActivationFunctionType
AX = mybir.AxisListType

P = 128
S = 1024
D = 1024
TT = S // P
KT = D // P
EPS = 1e-6
HEADS, HD = 16, 64
LAT = 128
IDXH = 8
TOPK = 256
INNER = 2048
SSMH = 32
GROUPS = 4
HPG = SSMH // GROUPS
CONV = 4
FFN = 2816
FT = FFN // P
XT = (INNER + 2 * GROUPS * 128) // P
O_Q, O_C, O_QI, O_KI, O_WI, O_Z, O_X, O_DT, O_GA, O_GS = (
    0, 1024, 1152, 1664, 1728, 1736, 3784, 6856, 6888, 7912)
BUCKETS, REL_MAX = 32, 128
MEMT = 256
MLAH, NOPE, ROPE, MQK = 8, 64, 32, 96
DH, DD = 8, 32
MEMH = 4
LAM0 = 0.8 - 0.6 * math.exp(-0.3 * 0)
THETA = 10000.0
BIG = 1e30
LOW, TAKEN, SPLIT = -3e38, -3.4e38, -3.2e38
Kf = 1024
W_SLOTS = 8
EXTRA_SLOTS = (10, 11, 14, 15)


def bucket_table():
    n = np.maximum(255 - np.arange(384), 0)
    exact = BUCKETS // 2
    large = exact + (np.log(np.maximum(n, 1).astype(np.float32) / exact)
                     / math.log(REL_MAX / exact) * (BUCKETS - exact)).astype(np.int32)
    b = np.where(n < exact, n, np.minimum(large, BUCKETS - 1))
    out = (b[None, :] == np.arange(BUCKETS)[:, None]).astype(np.float32)
    out[BUCKETS - 1] -= 1.0
    return out


def hybrid_two_blocks(nc, t):
    ctx = ExitStack()
    with ctx:
        def sb(name, shape, dt=F32):
            return ctx.enter_context(nc.sbuf_tensor(name, shape, dt))

        def sem(name):
            return ctx.enter_context(nc.semaphore(name))

        arena_at = -(-nc.sbuf_base // 32) * 32
        arena = sb("arena", [P, 49 * Kf])
        rounded_tiles = {}

        def rounded(off):
            if off not in rounded_tiles:
                rounded_tiles[off] = nc.alloc_sbuf_tensor_at(f"rounded{off}", [P, Kf], F32R,
                                                             offset=arena_at + int(off * Kf) * 4)
            return rounded_tiles[off][:, :]

        def at(off, *shape):
            o, n = int(off * Kf), int(np.prod(shape))
            v = arena[:, o:o + n]
            if len(shape) == 2:
                v = v.rearrange("p (a b) -> p a b", b=shape[1])
            if len(shape) == 3:
                v = v.rearrange("p (a b c) -> p a b c", b=shape[1], c=shape[2])
            return v

        ident = sb("ident", [P, P])
        scan = sb("scan", [P, 4, P])
        tri = scan[:, 0, :]
        after = scan[:, 1, :]
        ones = scan[:, 2, :]
        strip = sb("strip", [P, S], BF16)
        future = scan[:, 3, :]
        decay_out = future.rearrange("p (a b) -> p a b", a=2)
        cols = sb("cols", [P, 4, P])
        rows = sb("rows", [P, 544])
        dtbuf = sb("dtbuf", [P, TT, 2, SSMH])
        dt, adt = dtbuf[:, :, 0, :], dtbuf[:, :, 1, :]
        cosb = dtbuf[:, :, 0, 0:16]
        sinb = dtbuf[:, :, 0, 16:32]
        stat = sb("stat", [P, 256])
        neghalf = sb("neghalf", [P, 1])
        negmax = sb("negmax", [P, 4])
        rsum = sb("rsum", [P, 8])
        rinv = sb("rinv", [P, 8])
        lam = sb("lam", [P, 8])
        head_gain = sb("head_gain", [P, 2])

        r_dtb, r_alog, r_dskip = rows[:, 0:32], rows[:, 32:64], rows[:, 64:96]
        r_qn, r_kn = rows[:, 96:192], rows[:, 192:288]
        r_dqn, r_dkn, r_sub = rows[:, 288:320], rows[:, 320:352], rows[:, 352:416]
        r_mqn, r_mkn = rows[:, 416:480], rows[:, 480:544]
        ROWS = [("dt_bias", r_dtb), ("a_log", r_alog), ("d_skip", r_dskip),
                ("mla_qn_g_2", r_qn), ("mla_kn_g_2", r_kn), ("diff_qn_g_2", r_dqn),
                ("diff_kn_g_2", r_dkn), ("diff_subln_g_2", r_sub), ("mem_qn_g_2", r_mqn),
                ("mem_kn_g_2", r_mkn)]
        COLS = [("conv_ssm_w", 0, 0, CONV * XT), ("conv_ssm_b", 0, 96, XT), ("norm_mix", 0, 120, KT),
                ("ssm_norm", 1, 0, 16), ("norm_ffn", 1, 16, KT), ("norm_g_2", 1, 24, KT),
                ("mem_norm_g_2", 1, 32, KT), ("mla_q_norm_g_2", 1, 40, 2), ("mla_kv_norm_g_2", 1, 42, 1),
                ("kv_norm", 1, 43, 1), ("conv_ffn_b", 1, 44, 2 * FT)]
        COL_ROWS = [128, 88, 88, 44]
        N_CONSTS = len(COLS) + 4

        def dram(name, shape):
            return nc.dram_tensor(name, shape, F32, kind="Internal").ap()

        hT_d = dram("hT_d", [P, KT * S])
        attT_d = dram("attT_d", [P, KT * S])
        z_d = dram("z_d", [S, INNER])
        gate_d = dram("gate_d", [2, KT, P, S])
        bias_d = dram("bias_d", [HEADS, P, 384])
        x1_d = dram("x1_d", [P, TT * D])
        x3_d = dram("x3_d", [P, TT * D])

        psum = ctx.enter_context(nc.psum_tensor("psum", [P, 8, 512], F32))
        filled = [sem(f"filled{b}") for b in range(8)]
        evacuated = [sem(f"evacuated{b}") for b in range(8)]
        used = [0] * 8
        owner = [(b, 0) for b in range(8)]
        turn = [0]
        tile_of, before = {}, {}

        def bank(name, n=1):
            b = turn[0] if turn[0] + n <= 8 else 0
            turn[0] = (b + n) % 8
            before[name] = owner[b:b + n]
            used[b] += 1
            owner[b:b + n] = [(b, used[b])] * n
            tile_of[name] = (b, used[b], n)
            return psum_of(name)

        def psum_of(name):
            b, _, n = tile_of[name]
            return psum[:, b, :] if n == 1 else psum[:, b:b + n, :].rearrange("p a b -> p (a b)")

        def full(name):
            return filled[tile_of[name][0]]

        def completed(name):
            return filled[tile_of[name][0]], tile_of[name][1]

        def empty(name):
            return evacuated[tile_of[name][0]]

        def written(name):
            return evacuated[tile_of[name][0]], tile_of[name][1] + 1

        def vacated(name, k=0):
            b, count = before[name][k]
            return evacuated[b], count + 1

        wslot_in = [sem(f"wslot_in{i}") for i in range(W_SLOTS + len(EXTRA_SLOTS))]
        weights_split = sem("weights_split")
        weights, slot_count = {}, [0] * len(wslot_in)
        slot_user, next_slot = [None] * len(wslot_in), [0]
        order = []
        split_order = []
        spent_by = {}

        def slot_at(i):
            return 41 + i if i < W_SLOTS else EXTRA_SLOTS[i - W_SLOTS]

        def weight(name, pieces, gate=0, split=False, extra=None):
            n = 2 if split else 1
            i = next_slot[0]
            i = (i + i % n) % W_SLOTS if extra is None else W_SLOTS + extra
            if extra is None:
                next_slot[0] = (i + n) % W_SLOTS
            earlier = [u for u in dict.fromkeys(slot_user[i:i + n]) if u is not None]
            slot_user[i:i + n] = [name] * n
            base = at(slot_at(i), Kf)
            slot_count[i] += 16 * len(pieces)
            weights[name] = (i, slot_count[i])
            order.append((name, i, earlier, [(base[:, 0:f * g].rearrange("p (a b) -> p a b", b=g)[:, :, lo:hi], src)
                                             for f, g, lo, hi, src in pieces], gate))
            if split:
                split_order.append(name)

        def loaded(name):
            i, count = weights[name]
            return wslot_in[i], count

        def weight_at(name, n):
            base = at(slot_at(weights[name][0]), Kf)
            return base[:, 0:(Kf // n) * n].rearrange("p (a b) -> p a b", b=n)

        def split(name):
            return weights_split, split_order.index(name) + 1

        def parts_at(name, n):
            i = weights[name][0]
            return [rounded(slot_at(s))[:, 0:(Kf // n) * n].rearrange("p (a b) -> p a b", b=n) for s in (i + 1, i)]

        def kp(ap):
            return ap.rearrange("(k p) n -> p k n", p=P)

        w_in = kp(t["w_in"][0])
        w_in2 = kp(t["w_in_2"][0])

        def w_cols(name, w, k0, kn, lo, n, gate=0, split=False):
            weight(name, [(kn, n, 0, n, w[:, k0:k0 + kn, lo:lo + n])], gate, split)

        def w_wide(name, w, kn, lo, n, gate=0, split=False):
            for k in range(0, kn, 2):
                w_cols((name, k), w, k, 2, lo, n, gate, split)

        weight("ki", [(8, 128, 0, 64, w_in[:, :, O_KI:O_KI + 64]), (8, 128, 64, 128, w_in[:, :, O_KI:O_KI + 64])])
        for j in range(4):
            w_cols(("qi", j), w_in, 0, 8, O_QI + P * j, P)
        C_N = LAT + IDXH + SSMH
        for k in (0, 4):
            weight(("c", k), [(4, C_N, 0, LAT, w_in[:, k:k + 4, O_C:O_C + LAT]),
                              (4, C_N, LAT, LAT + IDXH, w_in[:, k:k + 4, O_WI:O_WI + IDXH]),
                              (4, C_N, LAT + IDXH, C_N, w_in[:, k:k + 4, O_DT:O_DT + SSMH])])
        for n in ("w_uk", "w_uv"):
            w_cols(n, t[n][0].rearrange("h d c -> (h d) c").rearrange("(k p) n -> p k n", p=P), 0, 8, 0, LAT)
        for j in range(8):
            w_cols(("q", j), w_in, 0, 8, O_Q + P * j, P, split=True)
        for c in range(4):
            w_wide(("z", c), w_in, 8, O_Z + 512 * c, 512, split=True)
        for g, o in enumerate((O_GS, O_GA)):
            for j in range(KT):
                w_cols(("gate", g, j), w_in, 0, 8, o + P * j, P, split=True)
        PH_SSM, PH_MERGE, PH_OUT2 = 2, 4, 10
        LAST_MLA = TT * (HEADS + MLAH) - 1
        for j in range(XT):
            w_cols(("x", j), w_in, 0, 8, O_X + P * j, P, PH_SSM, True)
        w_so, w_ao, w_o = kp(t["w_ssm_out"][0]), kp(t["w_att_out"][0]), kp(t["w_out"][0])
        next_slot[0] = 6
        for half in range(2):
            for j in range(KT):
                w_cols(("so", half, j), w_so, 8 * half, 8, P * j, P, PH_MERGE if (half, j) != (0, 0) else 3, True)
        for j in range(KT):
            w_cols(("ao", j), w_ao, 0, 8, P * j, P, PH_MERGE, True)
        for c in range(2):
            w_wide(("o", c), w_o, 8, 512 * c, 512, split=True)
        w_up, w_dn = kp(t["w_ffn_up"][0]), kp(t["w_ffn_down"][0])
        for j in range(FT):
            w_cols(("up", j, 0), w_up, 0, 8, P * j, P, split=True)
            w_cols(("up", j, 1), w_up, 0, 8, FFN + P * j, P, split=True)
        w_mem = kp(t["w_mem_kv_2"][0])
        w_wide(("dn", 0), w_dn, FT, 0, 512, split=True)
        w_wide("mem", w_mem, 8, 0, 512)
        w_wide(("dn", 1), w_dn, FT, 512, 512, split=True)
        IN2 = [(0, 416), (416, 512), (928, 512), (1440, 512), (1952, 512)]
        for c, (lo, n) in enumerate(IN2):
            w_wide(("in2", c), w_in2, 8, lo, n, split=True)
        w_o2 = kp(t["w_out_2"][0])
        for c in range(2):
            for k in range(0, 8, 2):
                first = c == 0 and k < 4
                weight((("o2", c), k), [(2, 512, 0, 512, w_o2[:, k:k + 2, 512 * c:512 * c + 512])],
                       ("O", LAST_MLA) if first else PH_OUT2, True, k if first else None)

        x_in = [sem(f"x_in{i}") for i in range(TT)]
        consts_in = sem("consts_in")
        rows_in = sem("rows_in")
        consts_made = sem("consts_made")
        squared = sem("squared")
        mean_ready = sem("mean_ready")
        rstd_ready = sem("rstd_ready")
        scaled = sem("scaled")
        relu_used = sem("relu_used")
        exp_ready = sem("exp_ready")
        phase_done = sem("phase_done")
        z_out = [sem(f"z_out{i}") for i in range(4)]
        hT_out = sem("hT_out")
        attT_out = sem("attT_out")
        bias_out = sem("bias_out")
        bias_in = sem("bias_in")
        dt_steps = sem("dt_steps")
        z_in = sem("z_in")
        step_made = sem("step_made")
        mixed = sem("mixed")
        y_summed = sem("y_summed")
        state_decayed = sem("state_decayed")
        gated = sem("gated")
        ynorm = sem("ynorm")
        back_in = [sem(f"back_in{i}") for i in range(6)]
        x_again = sem("x_again")
        gate_out = [sem(f"gate_out{i}") for i in range(2)]
        gate_in = sem("gate_in")
        merged_ready = sem("merged_ready")
        rows_spent = sem("rows_spent")
        resid = sem("resid")
        x1_out = sem("x1_out")
        silu_made = sem("silu_made")
        high_made = sem("high_made")
        parts_made = sem("parts_made")
        mem_in = sem("mem_in")
        nf_in = sem("nf_in")
        x3_out = sem("x3_out")
        pos_in = sem("pos_in")
        dn_spent = sem("dn_spent")
        angle = sem("angle")
        trig = sem("trig")
        w_small_in = sem("w_small_in")
        heads_ready = sem("heads_ready")
        sq_ready = sem("sq_ready")
        sq_made = sem("sq_made")
        out_done = sem("out_done")

        hT = at(0, KT, S)
        x_tok = at(8, TT, D)
        hs = at(16, 2, D)
        qT = at(8, KT, S)
        attT = qT
        zbuf = at(37.5, 4, 512)
        qiT, kiT = at(18, 4, S), at(22, S)
        ckvT = at(24, LAT * TT)
        score_off = {}
        o = 0
        for i in range(2, TT):
            score_off[i] = o
            o += (i + 1) * P
        scores = at(25, o)
        negmask = arena[:, int(29.25 * Kf):int(29.25 * Kf) + o // 2].bitcast(BF16)
        biasT = at(31.5, HEADS, 256)
        ukT, uvT = at(35.5, D), at(36.5, D)
        row_stage = at(37.5, 4, P)
        onehot, relb = at(38, 384), at(38.5, HEADS)
        bias_row = at(38.75, 384 // 2 * 2)
        craw = at(39.5, TT, 168)
        top8 = at(40.875, TT - 2, 8)
        rel = at(16, 2, S)
        kT, v = at(16, KT, S), at(41, TT, D)
        hAhi, hAlo = [[rounded(off + k) for k in range(KT)] for off in (16, 0)]
        gate_stage = at(37.5, 2, S)
        dtmp = [at(25 + 0.25 * n, TT * SSMH) for n in range(4)]
        def rings(l_off, p_offs, pt_off):
            return ([at(l_off + n, S) for n in range(2)], [at(q, S) for q in p_offs],
                    [at(pt_off + n, S) for n in range(3)])
        A1 = rings(25, (27, 28, 38.5), 35.5)
        att = at(39.5, 1, D)
        hBhi, hBlo = [[rounded(off + k) for k in range(KT)] for off in (8, 0)]
        xsT, bT, cT = at(16, 16, S), at(32, 4, S), at(36, 4, S)
        yT = xsT

        def xbc_at(j):
            return xsT[:, j, :] if j < 16 else bT[:, j - 16, :] if j < 20 else cT[:, j - 20, :]

        xdt = [at(0 + 2 * n, INNER) for n in range(2)]
        yb = [at(4 + 2 * n, INNER) for n in range(2)]
        state = at(8, INNER)
        zc = at(10, INNER)
        mix = [at(14 + n, S) for n in range(2)]
        step = [[rounded(off + n) for off in (40, 12)] for n in range(2)]
        adt_parts = [rounded(46)[:, lo:lo + TT * SSMH].rearrange("p (t h) -> p t h", h=SSMH) for lo in (0, TT * SSMH)]
        after_r = rounded(46)[:, 2 * TT * SSMH:2 * TT * SSMH + P]
        xds = [at(42 + 0.5 * n, 512) for n in range(2)]
        btok = [at(43 + 0.5 * n, 512) for n in range(2)]
        cbm = [at(44 + 0.5 * n, 512) for n in range(2)]
        yoff = at(45, 512)
        junk = at(45.5, 512)
        yhi, ylo = [[rounded(off + k) for k in range(2 * KT)] for off in (0, 16)]
        attTd = at(0, KT, S)
        ahi, alo = [[rounded(off + k) for k in range(KT)] for off in (16, 0)]
        mergedT = at(32, KT, S)
        mhi, mlo = [[rounded(off + k) for k in range(KT)] for off in (24, 32)]
        gate = at(40, S)
        x1, x1E = at(0, TT, D), at(16, TT, D)
        hsE, junkE = at(24, 2, D), at(40, D)
        h2T = at(8, KT, S)
        h2hi, h2lo = [[rounded(off + k) for k in range(KT)] for off in (0, 8)]
        accF = [at(38 + n, S) for n in range(2)]
        actT = at(16, FT, S)
        act_parts = [[[rounded(off + n) for n in range(2)] for off in offs]
                     for offs in ((12, 14), (8, 38))]
        memx, memT, memkv, kmT = (at(8, 2, D), at(10, KT, MEMT), at(40, 2, 512),
                                   scan[:, :, :].rearrange("p (a c) b -> p a (c b)", a=2))
        nfb = at(12, D)
        h3T = at(16, KT, S)
        h3hi, h3lo = [[rounded(off + k) for k in range(KT)] for off in (0, 16)]
        hs3, junkG = at(38, 2, D), at(24, D)
        pA, pB, pZ = at(8, TT, 416), at(24, TT, 1024), at(32, TT, 1024)
        trigT = [at(13 + 0.125 * n, TT, 16) for n in range(5)]
        invf, posf, pos_i = at(13.75, 16), at(13.8125, TT), at(13.875, TT).bitcast(I32)
        lamv = at(14, 4, 32)
        dsq = at(14.5, 768)
        vM = at(12, TT, 512)
        qTm, kTm = at(0, MLAH, S), at(16, MLAH, S)
        cqT, ckv2T = at(41, 2, S), at(43, S)
        wuq, wukv = at(44, 2, 768), at(45.5, D)
        qtok, ktok = [at(46.5, 768), at(48, 768)], [at(47.25, 768), at(11.25, 768)]
        htmp = at(48.75, 256)
        A2 = rings(41, (43, 44, 45), 46)
        od, odsq = at(8, TT, 256), at(12, TT, 256)
        yT2, xo = at(0, KT, S), at(16, TT, D)
        y2hi, y2lo = [[rounded(off + k) for k in range(KT)] for off in (24, 0)]

        def rings_of(g):
            return A1 if g < N1 else A2

        stat_col, stat_n, stat_at = {}, {}, {}
        squared_n = {}

        def chain(name, col, width, by_act=False):
            stat_n[name] = len(stat_n) + 1
            stat_at[name] = (col, width)

        for i in range(TT):
            chain(("x", i), i, 1)
        chain("ckv", 8, TT)
        for c in range(TT):
            chain(("ssd", c), 16 + 4 * c, 4)
        for i in range(TT):
            chain(("h2", i), 48 + i, 1)
        for i in range(2):
            chain(("mem", i), 72 + i, 1)
        chain("memk", 74, 8)
        for n in range(TT + 2):
            if n < TT:
                chain(("x3", n), 56 + n, 1)
            if n >= 2:
                chain(("h3", n - 2), 64 + n - 2, 1)
        chain("cc", 82, 16)
        chain("dd", 98, 128)
        chain("mqm", 16, 32)
        for i in range(TT):
            chain(("mq", i), 16 * (i % 2), 8)
            chain(("mk", i), 16 * (i % 2) + 8, 8)
        chain("sub", 48, 32)
        sq_order = ([("x", i) for i in range(TT)] + [("ssd", c) for c in range(TT)] + [("h2", i) for i in range(TT)]
                    + [("mem", i) for i in range(2)])
        for n in range(TT + 2):
            sq_order += ([("x3", n)] if n < TT else []) + ([("h3", n - 2)] if n >= 2 else [])
        squared_n = {name: n + 1 for n, name in enumerate(sq_order)}

        part_order = [(key, k) for key, n in (("hA", KT), ("hB", KT), ("adt", 1), ("y", 2 * KT), ("att", KT), ("m", KT), ("h2", KT))
                      for k in range(n)]
        part_order += [("act", c, k) for c in range(2) for k in range(FT)]
        part_order += [(key, k) for key in ("h3", "y2") for k in range(KT)]

        def high(name):
            return high_made, part_order.index(name) + 1

        def parts(name):
            return parts_made, part_order.index(name) + 1

        def down_step(c, k):
            return c * (FT - 1) + k + 1

        def stat_of(name, k=None):
            col, width = stat_at[name]
            return stat[:, col:col + width] if k is None else stat[:, col + k:col + k + 1]

        def rooted(name):
            return rstd_ready, stat_n[name]

        def bc(ap, n, axis=2):
            shape = list(ap.shape)
            return ap.unsqueeze(axis).broadcast_to(shape[:axis] + [n] + shape[axis:])

        block = ctx.enter_context(nc.Block())

        def chunks(n):
            return [(lo, min(n, lo + 512)) for lo in range(0, n, 512)]

        def unit(ph, i, nk, q, k, v, **more):
            return dict(ph=ph, i=i, nk=nk, q=q, k=k, v=v, **more)

        units1 = []
        for i in range(TT):
            for h in range(HEADS):
                r, j = 64 * (h % 2), h // 2
                units1.append(unit(
                    "a", i, i + 1, qT[r:r + 64, j, i * P:(i + 1) * P],
                    lambda lo, hi, r=r, j=j: kT[r:r + 64, j, lo:hi],
                    lambda b, h=h: v[:, b, h * 64:h * 64 + 64], h=h,
                    mask=strip[:, (7 - i) * P:S] if i < 2 else negmask[:, score_off[i]:score_off[i] + (i + 1) * P]))
        units2 = []
        for i in range(TT):
            for h in range(MLAH):
                units2.append(unit(
                    "m", i, i + 1, qTm[0:MQK, h, i * P:(i + 1) * P],
                    lambda lo, hi, h=h: kTm[0:MQK, h, lo:hi],
                    lambda b, h=h: vM[:, b, h * 64:h * 64 + 64], h=h, mask=strip[:, (7 - i) * P:S]))
        for i in range(TT):
            for m in range(2 * DH // 2):
                r, j = 32 * (m % 4), m // 4
                units2.append(unit(
                    "d", i, i + 1, pB[r:r + 32, i, j * P:(j + 1) * P],
                    lambda lo, hi, r=r, j=j: pB[r:r + 32, lo // P:hi // P, 256 + j * P:256 + (j + 1) * P],
                    lambda b, m=m: pB[:, b, 512 + 64 * (m // 2):576 + 64 * (m // 2)], h=m,
                    mask=strip[:, (7 - i) * P:S]))
        for i in range(TT):
            for h in range(MEMH):
                r, j = 64 * (h % 2), h // 2
                units2.append(unit(
                    "e", i, 2, pB[r:r + 64, i, 768 + j * P:768 + (j + 1) * P],
                    lambda lo, hi, r=r, j=j: kmT[r:r + 64, j, lo:hi],
                    lambda b, h=h: memkv[:, b, 256 + h * 64:320 + h * 64], h=h, mask=strip[:, 0:256]))
        N1 = len(units1)

        def last_group(u):
            return (u["nk"] - 1) // 4

        def end_phase(eng):
            eng.drain()
            eng.sem_inc(phase_done, 1)

        @block.tensor
        def _(pe):
            def mm(out, lhsT, rhs, start=True, stop=True):
                return pe.matmul(out, lhsT, rhs, start=start, stop=stop)

            def tr(out, src):
                n = src.shape[0]
                return pe.transpose(out, src, ident[0:n, 0:n])

            def four(name, blocks):
                out = bank(name)
                pe.wait_ge(*vacated(name))
                for n, src in enumerate(blocks):
                    last = tr(out[:, n * P:(n + 1) * P], src)
                last.then_inc(full(name), 1)

            def stationary_weights(name, wnames, xT, both=False):
                for wn in wnames:
                    pe.wait_ge(*loaded(wn))
                if both:
                    out2 = bank(name, 2)
                    pe.wait_ge(*vacated(name))
                    pe.wait_ge(*vacated(name, 1))
                for half in range(2):
                    if both:
                        out = out2[:, half * 512:half * 512 + 512]
                    else:
                        out = bank((*name, half))
                        pe.wait_ge(*vacated((*name, half)))
                    n = 0
                    for wn in wnames:
                        w = weight_at(wn, P)
                        for k in range(8):
                            last = mm(out, w[:, k, :], xT[:, n, half * 512:half * 512 + 512],
                                      n == 0, n == 8 * len(wnames) - 1)
                            n += 1
                    if not both:
                        last.then_inc(full((*name, half)), 1)
                if both:
                    last.then_inc(full(name), 1)
                for wn in wnames:
                    spent_by[wn] = completed(name if both else (*name, 1))

            def three(out, whigh, wlow, xhigh, xlow, first, last):
                mm(out, whigh, xlow, first, False)
                mm(out, whigh, xhigh, False, False)
                return mm(out, wlow, xhigh, False, last)

            def stationary_parts(name, wnames, xhigh, xlow, key=None, n0=0):
                for wn in wnames:
                    pe.wait_ge(*split(wn))
                out2 = bank(name, 2)
                pe.wait_ge(*vacated(name))
                pe.wait_ge(*vacated(name, 1))
                n = 0
                for wn in wnames:
                    wh, wl = parts_at(wn, P)
                    for k in range(8):
                        if key is not None:
                            pe.wait_ge(*parts((key, n0 + n)))
                        for lo in (0, 512):
                            last = three(out2[:, lo:lo + 512], wh[:, k, :], wl[:, k, :], xhigh[n0 + n][:, lo:lo + 512],
                                         xlow[n0 + n][:, lo:lo + 512], n == 0, n == 8 * len(wnames) - 1)
                        n += 1
                last.then_inc(full(name), 1)
                for wn in wnames:
                    spent_by[wn] = completed(name)

            rows_step = [0]

            def token_rows_parts(name, n, kn, xhigh, xlow, key=None):
                outs = [bank((*name, tt)) for tt in range(TT)]
                for tt in range(TT):
                    pe.wait_ge(*vacated((*name, tt)))
                for k in range(kn):
                    if k % 2 == 0:
                        pe.wait_ge(*split((name, k)))
                    wh, wl = parts_at((name, k - k % 2), n)
                    if key is not None:
                        pe.wait_ge(*parts((key, k)))
                    for tt in range(TT):
                        here = slice(tt * P, (tt + 1) * P)
                        last = three(outs[tt][:, 0:n], xhigh[k][:, here], xlow[k][:, here], wh[:, k % 2, :], wl[:, k % 2, :],
                                     k == 0, k == kn - 1)
                        if k == kn - 1:
                            last.then_inc(full((*name, tt)), 1)
                    if k == kn - 1:
                        spent_by[(name, k - 1)] = completed((*name, TT - 1))
                    elif k % 2:
                        last.then_inc(rows_spent, 1)
                        rows_step[0] += 1
                        spent_by[(name, k - 1)] = rows_spent, rows_step[0]

            def attend(units, base, after_block):
                n = len(units)
                pending = None
                for s in range(n + 4):
                    if s < n:
                        u = units[s]
                        out = bank(("S", base + s), 1 if u["nk"] <= 4 else 2)
                        pe.wait_ge(*vacated(("S", base + s)))
                        pe.wait_ge(*vacated(("S", base + s), -1))
                        for lo, hi in chunks(u["nk"] * P):
                            last = mm(out[:, lo:hi], u["q"], u["k"](lo, hi))
                        last.then_inc(full(("S", base + s)), 1)
                    if pending is not None:
                        after_block(pending)
                        pending = None
                    if 0 <= s - 2 < n:
                        u, g = units[s - 2], base + s - 2
                        probs = rings_of(g)[1][g % 3]
                        pe.wait_ge(exp_ready, g + 1)
                        for grp in range(last_group(u) + 1):
                            out = bank(("T", g, grp))
                            pe.wait_ge(*vacated(("T", g, grp)))
                            for b in range(4 * grp, min(4 * grp + 4, u["nk"])):
                                last = tr(out[:, (b - 4 * grp) * P:(b - 4 * grp + 1) * P], probs[:, b * P:(b + 1) * P])
                            last.then_inc(full(("T", g, grp)), 1)
                    if 0 <= s - 3 < n:
                        u, g = units[s - 3], base + s - 3
                        pT = rings_of(g)[2][g % 3]
                        pe.wait_ge(*written(("T", g, last_group(u))))
                        out = bank(("O", g))
                        pe.wait_ge(*vacated(("O", g)))
                        for b in range(u["nk"]):
                            last = mm(out[:, 0:64], pT[:, b * P:(b + 1) * P], u["v"](b), b == 0, b == u["nk"] - 1)
                        last.then_inc(full(("O", g)), 1)
                        if u["ph"] == "a" and u["h"] == HEADS - 1:
                            pending = u["i"]

            pe.wait_ge(consts_made, 1)
            pe.wait_ge(consts_in, 16 * N_CONSTS)
            out = bank("cols")
            pe.wait_ge(*vacated("cols"))
            for m, r in enumerate(COL_ROWS):
                last = tr(out[:, m * P:m * P + r], row_stage[0:r, m, :])
            last.then_inc(full("cols"), 1)
            out = bank("bias")
            pe.wait_ge(*vacated("bias"))
            mm(out[0:HEADS, 0:384], relb[0:BUCKETS, :], onehot[0:BUCKETS, :]).then_inc(full("bias"), 1)

            def norm_tiles(key, src, n0, tiles, before=None):
                for tt in tiles:
                    pe.wait_ge(scaled, n0 + tt + 1)
                    for half in range(2):
                        four((key, tt, half), [src[:, tt % 2, (4 * half + n) * P:(4 * half + n + 1) * P] for n in range(4)])

            norm_tiles("hx", hs, 0, range(TT))
            for tt in range(TT):
                for half in range(2):
                    pe.wait_ge(*written(("hx", tt, half)))
            stationary_weights(("ki",), ["ki"], hT)
            for j in range(4):
                stationary_weights(("qi", j), [("qi", j)], hT)
            for k in (0, 4):
                pe.wait_ge(*loaded(("c", k)))
            wc = [weight_at(("c", k - k % 4), C_N)[:, k % 4, :] for k in range(KT)]
            for tt in range(TT):
                out = bank(("c", tt))
                pe.wait_ge(*vacated(("c", tt)))
                for k in range(KT):
                    last = mm(out[:, 0:C_N], hT[:, k, tt * P:(tt + 1) * P], wc[k], k == 0, k == KT - 1)
                last.then_inc(full(("c", tt)), 1)
            for k in (0, 4):
                spent_by[("c", k)] = completed(("c", TT - 1))
            for half in range(2):
                pe.wait_ge(*written(("ki", half)))
            for j in range(4):
                pe.wait_ge(*written(("qi", j, 1)))
            for i in range(2, TT):
                for h in range(IDXH):
                    r, nk = 64 * (h % 2), (i + 1) * P
                    out = bank(("ix", i, h), 1 if nk <= 512 else 2)
                    pe.wait_ge(*vacated(("ix", i, h)))
                    pe.wait_ge(*vacated(("ix", i, h), -1))
                    for lo, hi in chunks(nk):
                        last = mm(out[:, lo:hi], qiT[r:r + 64, h // 2, i * P:(i + 1) * P], kiT[r:r + 64, lo:hi])
                    last.then_inc(full(("ix", i, h)), 1)
            pe.wait_ge(heads_ready, 1)
            for half in range(2):
                four(("ckvT", half), [craw[:, 4 * half + n, 0:LAT] for n in range(4)])
            for wn, key in (("w_uk", "ukT"), ("w_uv", "uvT")):
                pe.wait_ge(*loaded(wn))
                w = weight_at(wn, P)
                for half in range(2):
                    four((key, half), [w[:, 4 * half + n, :] for n in range(4)])
                spent_by[wn] = completed((key, 1))
            for j in range(8):
                stationary_parts(("q", j), [("q", j)], hAhi, hAlo, "hA" if j == 0 else None)
            for c in range(4):
                token_rows_parts(("z", c), 512, 8, hAhi, hAlo)
            for g in range(2):
                for j in range(KT):
                    stationary_parts(("gate", g, j), [("gate", g, j)], hAhi, hAlo)
            end_phase(pe)
            pe.wait_ge(phase_done, 4 * 1)

            for j in range(8):
                for half in range(2):
                    out = bank(("kT", j, half))
                    pe.wait_ge(*vacated(("kT", j, half)))
                    mm(out, ukT[:, j * P:(j + 1) * P], ckvT[:, half * 512:half * 512 + 512]).then_inc(full(("kT", j, half)), 1)
            for tt in range(TT):
                for half in range(2):
                    out = bank(("v", tt, half))
                    pe.wait_ge(*vacated(("v", tt, half)))
                    mm(out, ckvT[:, tt * P:(tt + 1) * P], uvT[:, half * 512:half * 512 + 512]).then_inc(full(("v", tt, half)), 1)
            for j in range(8):
                pe.wait_ge(*written(("kT", j, 1)))
            for tt in range(TT):
                pe.wait_ge(*written(("v", tt, 1)))

            def att_transposed(i):
                pe.wait_ge(*written(("O", HEADS * i + HEADS - 1)))
                for half in range(2):
                    four(("aT", i, half), [att[:, 0, (4 * half + n) * P:(4 * half + n + 1) * P] for n in range(4)])

            attend(units1, 0, att_transposed)
            end_phase(pe)
            pe.wait_ge(phase_done, 4 * 2)

            for j in range(XT):
                stationary_parts(("xc", j), [("x", j)], hBhi, hBlo, "hB" if j == 0 else None)
            end_phase(pe)
            pe.wait_ge(phase_done, 4 * 3)

            def ssd_front(c):
                here = slice(c * P, (c + 1) * P)
                for g in range(GROUPS):
                    four(("xt", c, g), [xsT[:, 4 * g + n, here] for n in range(4)])
                four(("bt", c), [bT[:, n, here] for n in range(GROUPS)])
                out = bank(("cb", c))
                pe.wait_ge(*vacated(("cb", c)))
                for g in range(GROUPS):
                    last = mm(out[:, g * P:(g + 1) * P], bT[:, g, here], cT[:, g, here])
                last.then_inc(full(("cb", c)), 1)
                out = bank(("ea", c))
                pe.wait_ge(*vacated(("ea", c)))
                mm(out[:, 0:SSMH], tri[:, :], adt[:, c, :])
                mm(out[:, SSMH:2 * SSMH], ones[:, :], adt[:, c, :]).then_inc(full(("ea", c)), 1)

            def ssd_tail(n):
                c, g = n // GROUPS, n % GROUPS
                here = slice(c * P, (c + 1) * P)
                pe.wait_ge(mixed, n + 1)
                out = bank(("yd", c, g))
                pe.wait_ge(*vacated(("yd", c, g)))
                for h in range(HPG):
                    lo = (HPG * g + h) * 64
                    last = mm(out[:, h * 64:h * 64 + 64], mix[n % 2][:, h * P:(h + 1) * P], xdt[c % 2][:, lo:lo + 64])
                last.then_inc(full(("yd", c, g)), 1)
                if c:
                    pe.wait_ge(*written(("st", c - 1, g)))
                    out = bank(("yo", c, g))
                    pe.wait_ge(*vacated(("yo", c, g)))
                    mm(out, cT[:, g, here], state[:, g * 512:(g + 1) * 512]).then_inc(full(("yo", c, g)), 1)
                if c < TT - 1:
                    pe.wait_ge(*written(("bt", c)))
                    out = bank(("st", c, g))
                    pe.wait_ge(*vacated(("st", c, g)))
                    mm(out, btok[c % 2][:, g * P:(g + 1) * P], xds[n % 2]).then_inc(full(("st", c, g)), 1)

            NG = TT * GROUPS
            for n in range(NG + 4):
                c, g = n // GROUPS, n % GROUPS
                if n < NG:
                    if g == 0:
                        ssd_front(c)
                    pe.wait_ge(step_made, n + 1)
                    out = bank(("sg", c, g), 2)
                    pe.wait_ge(*vacated(("sg", c, g)))
                    pe.wait_ge(*vacated(("sg", c, g), 1))
                    for lo, hi in chunks(S):
                        mm(out[:, lo:hi], after_r, step[n % 2][0][:, lo:hi], True, False)
                        last = mm(out[:, lo:hi], after_r, step[n % 2][1][:, lo:hi], False, True)
                    last.then_inc(full(("sg", c, g)), 1)
                if 1 <= n <= NG:
                    ssd_tail(n - 1)
                if n >= 4 and (n - 4) % GROUPS == 3:
                    cc = (n - 4) // GROUPS
                    pe.wait_ge(ynorm, cc + 1)
                    for q in range(4):
                        four(("yt", cc, q), [yb[cc % 2][:, (4 * q + m) * P:(4 * q + m + 1) * P] for m in range(4)])
            end_phase(pe)
            pe.wait_ge(phase_done, 4 * 4)

            for half in range(2):
                for j in range(KT):
                    stationary_parts(("so", half, j), [("so", half, j)], yhi, ylo, "y" if j == 0 else None, 8 * half)
            for j in range(KT):
                stationary_parts(("ao", j), [("ao", j)], ahi, alo, "att" if j == 0 else None)
            end_phase(pe)

            for c in range(2):
                token_rows_parts(("o", c), 512, 8, mhi, mlo, "m" if c == 0 else None)
            norm_tiles("h2", hsE, TT, range(TT))
            for tt in range(TT):
                for half in range(2):
                    pe.wait_ge(*written(("h2", tt, half)))
            end_phase(pe)
            for j in range(FT):
                stationary_parts(("ug", j), [("up", j, 0)], h2hi, h2lo, "h2" if j == 0 else None)
                stationary_parts(("uv", j), [("up", j, 1)], h2hi, h2lo)
            end_phase(pe)
            def memory():
                norm_tiles("mx", hs3, 2 * TT, range(2))
                for tt in range(2):
                    for half in range(2):
                        pe.wait_ge(*written(("mx", tt, half)))
                for k in range(0, 8, 2):
                    pe.wait_ge(*loaded(("mem", k)))
                ws = [weight_at(("mem", k), 512) for k in range(0, 8, 2)]
                for tt in range(2):
                    out = bank(("mem", tt))
                    pe.wait_ge(*vacated(("mem", tt)))
                    for k in range(KT):
                        last = mm(out, memT[:, k, tt * P:(tt + 1) * P], ws[k // 2][:, k % 2, :], k == 0, k == KT - 1)
                    last.then_inc(full(("mem", tt)), 1)
                for k in range(0, 8, 2):
                    spent_by[("mem", k)] = completed(("mem", 1))

            for c in range(2):
                outs = [bank(("dn", c, tt)) for tt in range(TT)]
                for tt in range(TT):
                    pe.wait_ge(*vacated(("dn", c, tt)))
                for k in range(FT):
                    if k % 2 == 0:
                        pe.wait_ge(*split((("dn", c), k)))
                    wh, wl = parts_at((("dn", c), k - k % 2), 512)
                    ah, al = act_parts[c][k % 2]
                    pe.wait_ge(*parts(("act", c, k)))
                    for tt in range(TT):
                        here = slice(tt * P, (tt + 1) * P)
                        last = three(outs[tt], ah[:, here], al[:, here], wh[:, k % 2, :], wl[:, k % 2, :],
                                     k == 0, k == FT - 1)
                        if k == FT - 1:
                            last.then_inc(full(("dn", c, tt)), 1)
                    if k == FT - 1:
                        spent_by[(("dn", c), k - 1)] = completed(("dn", c, TT - 1))
                    else:
                        last.then_inc(dn_spent, 1)
                        if k % 2:
                            spent_by[(("dn", c), k - 1)] = dn_spent, down_step(c, k)
                if c == 0:
                    memory()

            pe.wait_ge(sq_ready, 1)
            four(("kmT",), [memkv[:, n % 2, (n // 2) * P:(n // 2 + 1) * P] for n in range(4)])
            norm_tiles("h3", hs3, 2 * TT + 2, range(TT))
            for tt in range(TT):
                for half in range(2):
                    pe.wait_ge(*written(("h3", tt, half)))
            for c, (lo, n) in enumerate(IN2):
                token_rows_parts(("in2", c), n, 8, h3hi, h3lo, "h3" if c == 0 else None)
            pe.wait_ge(heads_ready, 3)
            for x in (0, 1, 2, 3, 6, 7):
                for half in range(2):
                    four(("dT", x, half), [pB[:, 4 * half + n, x * P:(x + 1) * P] for n in range(4)])
            end_phase(pe)
            for k in range(3):
                for half in range(2):
                    four(("cqT", k, half), [pA[:, 4 * half + n, k * P:(k + 1) * P] for n in range(4)])
            pe.wait_ge(w_small_in, 32)
            for k in range(3):
                for half in range(2):
                    pe.wait_ge(*written(("cqT", k, half)))
            for tt in range(TT + 1):
                if tt < TT:
                    here = slice(tt * P, (tt + 1) * P)
                    out = bank(("uq", tt), 2)
                    pe.wait_ge(*vacated(("uq", tt)))
                    pe.wait_ge(*vacated(("uq", tt), 1))
                    for lo, hi in chunks(768):
                        for k in range(2):
                            last = mm(out[:, lo:hi], cqT[:, k, here], wuq[:, k, lo:hi], k == 0, k == 1)
                    last.then_inc(full(("uq", tt)), 1)
                    out = bank(("ukv", tt), 2)
                    pe.wait_ge(*vacated(("ukv", tt)))
                    pe.wait_ge(*vacated(("ukv", tt), 1))
                    for lo, hi in chunks(D):
                        last = mm(out[:, lo:hi], ckv2T[:, here], wukv[:, lo:hi])
                    last.then_inc(full(("ukv", tt)), 1)
                if tt == 0:
                    continue
                for key, src, n in (("qTm", qtok, 2 * tt - 2), ("kTm", ktok, 2 * tt - 1)):
                    pe.wait_ge(heads_ready, 4 + n)
                    for half in range(2):
                        out = bank((key, tt - 1, half))
                        pe.wait_ge(*vacated((key, tt - 1, half)))
                        for m in range(4):
                            h = 4 * half + m
                            last = tr(out[0:MQK, m * P:(m + 1) * P], src[(tt - 1) % 2][:, h * MQK:(h + 1) * MQK])
                        last.then_inc(full((key, tt - 1, half)), 1)
            end_phase(pe)
            pe.wait_ge(phase_done, 4 * 9)
            attend(units2, N1, None)
            end_phase(pe)
            pe.wait_ge(phase_done, 4 * 10)
            for tt in range(TT):
                for half in range(2):
                    four(("yT2", tt, half), [pZ[:, tt, (4 * half + n) * P:(4 * half + n + 1) * P] for n in range(4)])
            for tt in range(TT):
                for half in range(2):
                    pe.wait_ge(*written(("yT2", tt, half)))
            for c in range(2):
                token_rows_parts(("o2", c), 512, 8, y2hi, y2lo, "y2" if c == 0 else None)

        @block.sync
        def _(sp):
            def row_ap(name):
                a = t[name][0] if len(t[name].shape) > 1 else t[name]
                return a.rearrange("(k p) -> k p", p=P) if len(a.shape) == 1 else a.rearrange("j (k p) -> (j k) p", p=P)

            for name, m, r0, n in COLS:
                sp.dma_start(row_stage[r0:r0 + n, m, :], row_ap(name)).then_inc(consts_in, 16)
            taps = row_ap("conv_ffn_w")
            sp.dma_start(row_stage[0:88, 2, :], taps[0:88, :]).then_inc(consts_in, 16)
            sp.dma_start(row_stage[0:44, 3, :], taps[88:132, :]).then_inc(consts_in, 16)
            sp.dma_start(onehot[0:BUCKETS, :], t["buckets"]).then_inc(consts_in, 16)
            sp.dma_start(relb[0:BUCKETS, :], t["rel_bias"]).then_inc(consts_in, 16)
            for tt in range(TT):
                sp.dma_start(x_tok[:, tt, :], t["x"][0, tt * P:(tt + 1) * P, :]).then_inc(x_in[tt], 16)
            for name, dst in ROWS:
                src = t[name]
                n = src.shape[-1]
                sp.dma_start(dst, bass.AP(src.tensor, src.offset, [[0, P], [1, n]])).then_inc(rows_in, 16)

            def relative_bias():
                sp.wait_ge(*written("bias"))
                src = bias_row[0:HEADS, :].unsqueeze(1).broadcast_to([HEADS, P, 384])
                sp.dma_start(bias_d, src).then_inc(bias_out, 16)
                sp.wait_ge(bias_out, 16)
                src = bass.AP(bias_d.tensor, P - 1, [[384 - 1, P], [P * 384, HEADS], [1, 256]])
                sp.dma_start(biasT, src).then_inc(bias_in, 16)

            def gate_rows():
                sp.wait_ge(phase_done, 4 * 3)
                for c in range(TT):
                    if c:
                        sp.wait_ge(gated, GROUPS * c)
                    sp.dma_start(zc, z_d[c * P:(c + 1) * P, :]).then_inc(z_in, 16)

            def branch_inputs():
                sp.wait_ge(*completed(("so", 0, KT - 1)))
                sp.dma_start(attTd.rearrange("p k s -> p (k s)"), attT_d).then_inc(back_in[1], 16)

            def tokens_again():
                sp.wait_ge(phase_done, 4 * 1)
                sp.dma_start(hT.rearrange("p k s -> p (k s)"), hT_d).then_inc(back_in[0], 16)

            def residual():
                sp.wait_ge(*completed(("ao", KT - 1)))
                sp.dma_start(x1E, t["x"][0].rearrange("(a p) n -> p a n", p=P)).then_inc(x_again, 16)

            def mla_weights():
                sp.wait_ge(phase_done, 4 * 8)
                sp.dma_start(wuq, kp(t["w_uq_2"][0])).then_inc(w_small_in, 16)
                sp.dma_start(wukv, t["w_ukv_2"][0]).then_inc(w_small_in, 16)

            ahead = {"w_uk": relative_bias, ("x", 0): tokens_again, ("so", 0, 1): gate_rows,
                     ("so", 1, 4): branch_inputs, (("o", 1), 0): residual, (("o2", 0), 0): mla_weights}
            for n, (name, slot, earlier, pieces, gate) in enumerate(order):
                if name in ahead:
                    ahead[name]()
                for tile in earlier:
                    sp.wait_ge(*spent_by[tile])
                if isinstance(gate, tuple):
                    sp.wait_ge(*completed(gate))
                elif gate:
                    sp.wait_ge(phase_done, 4 * gate)
                for dst, src in pieces:
                    sp.dma_start(dst, src).then_inc(wslot_in[slot], 16)
            for tt in range(TT):
                sp.wait_ge(*written(("o2", 1, tt)))
                sp.dma_start(t["out"][0, tt * P:(tt + 1) * P, :], xo[:, tt, :]).then_inc(out_done, 16)
            sp.wait_ge(out_done, 16 * TT)

        @block.gpsimd
        def _(pool):
            def power(*names):
                for name in names:
                    pool.wait_ge(mean_ready, stat_n[name])
                    v = stat_of(name)
                    pool.tensor_tensor(out=v, in0=v, in1=neghalf[:, 0:1].broadcast_to(list(v.shape)),
                                       op=ALU.pow).then_inc(rstd_ready, 1)

            def split_weights(*names):
                for name in names:
                    n = 416 if name[0] == ("in2", 0) else P
                    raw = weight_at(name, n)
                    high_part, low_part = parts_at(name, n)
                    pool.wait_ge(*loaded(name))
                    pool.tensor_copy(high_part, raw)
                    pool.drain()
                    pool.tensor_tensor(out=low_part, in0=raw, in1=high_part.bitcast(F32),
                                       op=ALU.subtract).then_inc(weights_split, 1)

            for m, value in ((head_gain, 1.0), (ident, 0.0), (tri, 1.0), (after, 1.0), (ones, 1.0), (strip, 0.0), (future, 0.0),
                             (neghalf, -0.5)):
                pool.memset(m if m is future else m[:, :], value)
            pool.drain()
            pool.affine_select(out=ident[:, :], in_=ident[:, :], compare_op=ALU.not_equal, fill=1.0, base=0,
                               pattern=[[-1, P]], channel_multiplier=1)
            pool.affine_select(out=tri[:, :], in_=tri[:, :], compare_op=ALU.is_ge, fill=0.0, base=0,
                               pattern=[[1, P]], channel_multiplier=-1)
            pool.affine_select(out=after[:, :], in_=after[:, :], compare_op=ALU.is_gt, fill=0.0, base=0,
                               pattern=[[-1, P]], channel_multiplier=1)
            pool.affine_select(out=strip[:, S - P:S], in_=strip[:, S - P:S], compare_op=ALU.is_ge, fill=BIG, base=0,
                               pattern=[[-1, P]], channel_multiplier=1)
            pool.affine_select(out=future, in_=future, compare_op=ALU.is_ge, fill=LOW, base=0,
                               pattern=[[-1, P]], channel_multiplier=1)
            pool.drain()
            pool.sem_inc(consts_made, 1)
            power(*[("x", i) for i in range(TT)], "ckv")
            split_weights(*[("q", j) for j in range(8)])
            split_weights(*[(("z", c), k) for c in range(4) for k in range(0, 8, 2)])
            split_weights(*[("gate", g, j) for g in range(2) for j in range(KT)])
            end_phase(pool)
            pool.wait_ge(phase_done, 4 * 1)
            end_phase(pool)
            pool.wait_ge(phase_done, 4 * 2)
            split_weights(*[("x", j) for j in range(XT)])
            end_phase(pool)
            pool.wait_ge(phase_done, 4 * 3)
            NG = TT * GROUPS
            for n in range(NG + 5):
                c, g = n // GROUPS, n % GROUPS
                if n < NG:
                    if n >= 2:
                        pool.wait_ge(*completed(("sg", (n - 2) // GROUPS, (n - 2) % GROUPS)))
                    if n == 0:
                        pool.tensor_copy(after_r, after)
                        pool.wait_ge(*parts(("adt", 0)))
                    for part, out in zip(adt_parts, step[n % 2]):
                        ins = pool.tensor_tensor(out=out.rearrange("p (h l) -> p h l", l=P), in0=bc(tri[:, :], HPG, 1),
                                                 in1=bc(part[:, c, HPG * g:HPG * (g + 1)].bitcast(F32), P), op=ALU.mult)
                    ins.then_inc(step_made, 1)
                m = n - 2
                if GROUPS <= m < NG - GROUPS:
                    c, g = m // GROUPS, m % GROUPS
                    h = state[:, g * 512:(g + 1) * 512].rearrange("p (h c) -> p h c", h=HPG)
                    pool.wait_ge(*completed(("yo", c, g)))
                    pool.wait_ge(*written(("ea", c)))
                    pool.tensor_tensor(out=h, in0=h, in1=bc(decay_out[:, c % 2, SSMH + HPG * g:SSMH + HPG * (g + 1)], 64),
                                       op=ALU.mult).then_inc(state_decayed, 1)
                if 0 <= m < NG:
                    c, g = m // GROUPS, m % GROUPS
                    if c:
                        pool.wait_ge(y_summed, m - GROUPS + 1)
                    else:
                        pool.wait_ge(*written(("yd", 0, g)))
                    pool.wait_ge(z_in, 16 * (c + 1))
                    y = yb[c % 2][:, g * 512:(g + 1) * 512]
                    pool.tensor_tensor(out=y, in0=y, in1=zc[:, g * 512:(g + 1) * 512], op=ALU.mult).then_inc(gated, 1)
                if n >= 6 and (n - 6) % GROUPS == 0:
                    power(("ssd", (n - 6) // GROUPS))
            split_weights(("so", 0, 0))
            end_phase(pool)
            pool.wait_ge(phase_done, 4 * 4)
            split_weights(*[("so", half, j) for half in range(2) for j in range(KT) if half or j])
            split_weights(*[("ao", j) for j in range(KT)])
            end_phase(pool)
            split_weights(*[(("o", c), k) for c in range(2) for k in range(0, 8, 2)])
            power(*[("h2", i) for i in range(TT)])
            end_phase(pool)
            for j in range(FT):
                split_weights(("up", j, 0), ("up", j, 1))
            end_phase(pool)
            for k in range(0, FT, 2):
                split_weights((("dn", 0), k))
                if k == 8:
                    power(("mem", 0), ("mem", 1))
            for k in range(0, 4, 2):
                split_weights((("dn", 1), k))
            power("memk")
            for k in range(4, FT, 2):
                split_weights((("dn", 1), k))
            split_weights(*[(("in2", 0), k) for k in (0, 2, 4)])
            for n in range(TT + 2):
                if n < TT:
                    power(("x3", n))
                if n >= 2:
                    power(("h3", n - 2))
            split_weights((("in2", 0), 6))
            split_weights(*[(("in2", 1), k) for k in range(0, 8, 2)])
            power("cc")
            split_weights(*[(("in2", c), k) for c in (2, 3) for k in range(0, 8, 2)])
            power("dd")
            split_weights(*[(("in2", 4), k) for k in range(0, 8, 2)])
            power("mqm")
            end_phase(pool)
            for tt in range(TT):
                power(("mq", tt), ("mk", tt))
            end_phase(pool)
            pool.wait_ge(phase_done, 4 * 9)
            split_weights(*[(("o2", 0), k) for k in (0, 2)])
            power("sub")
            end_phase(pool)
            pool.wait_ge(phase_done, 4 * 10)
            split_weights(*[(("o2", 0), k) for k in (4, 6)])
            split_weights(*[(("o2", 1), k) for k in range(0, 8, 2)])

        @block.scalar
        def _(act):
            def copy(out, name, src=None, func=ACT.Copy, scale=1.0):
                act.wait_ge(*completed(name))
                src = psum_of(name) if src is None else src
                act.activation(out, src, func, scale=scale).then_inc(empty(name), 1)

            def high_part(out, src):
                return act.activation(out, src, ACT.Copy).then_inc(high_made, 1)

            def square_sum(name, src, junk, k=None):
                act.drain()
                ins = act.activation(junk, src, ACT.Square, accum_out=stat_of(name, k))
                return ins

            def scale_tile(name, key, src, buf, tt, first=False):
                if not first and tt >= 2:
                    act.wait_ge(*completed((key, tt - 2, 1)))
                act.wait_ge(*rooted(name))
                r = stat_of(name)
                act.activation(buf[:, tt % 2, :], src, ACT.Copy, scale=r).then_inc(scaled, 1)

            junkA = at(18, D)
            for n in range(TT + 2):
                if n < TT:
                    act.wait_ge(x_in[n], 16)
                    square_sum(("x", n), x_tok[:, n, :], junkA).then_inc(squared, 1)
                if n >= 2:
                    scale_tile(("x", n - 2), "hx", x_tok[:, n - 2, :], hs, n - 2)
            act.wait_ge(*written("cols"))
            for tt in range(TT):
                for half in range(2):
                    act.wait_ge(*written(("hx", tt, half)))
            act.dma_start(hT_d, hT.rearrange("p k s -> p (k s)")).then_inc(hT_out, 16)
            act.drain()
            for half in range(2):
                copy(kiT[:, half * 512:half * 512 + 512], ("ki", half))
            for j in range(4):
                for half in range(2):
                    copy(qiT[:, j, half * 512:half * 512 + 512], ("qi", j, half))
            for tt in range(TT):
                copy(craw[:, tt, :], ("c", tt), psum_of(("c", tt))[:, 0:168])
            act.wait_ge(mean_ready, stat_n["ckv"])
            n = 0
            for i in range(2, TT):
                for h in range(IDXH):
                    if n >= 2:
                        act.wait_ge(relu_used, n - 1)
                    nk = (i + 1) * P
                    copy(rel[:, n % 2, 0:nk], ("ix", i, h), psum_of(("ix", i, h))[:, 0:nk], ACT.Relu)
                    n += 1
            act.wait_ge(relu_used, n)
            for k in range(KT):
                high_part(hAhi[k], hT[:, k, :])
            for half in range(2):
                copy(ckvT[:, half * 512:half * 512 + 512], ("ckvT", half), scale=cols[:, 1, 43:44])
            for key, dst in (("ukT", ukT), ("uvT", uvT)):
                for half in range(2):
                    copy(dst[:, half * 512:half * 512 + 512], (key, half))
            for j in range(8):
                copy(qT[:, j, :], ("q", j), scale=-HD ** -0.5)
            act.wait_ge(bias_out, 16)
            for n in range(4 * TT + 1):
                if n < 4 * TT:
                    if n >= 4:
                        act.wait_ge(z_out[n % 4], 16 * (n // 4))
                    copy(zbuf[:, n % 4, :], ("z", n // TT, n % TT), func=ACT.Silu)
                if n >= 1:
                    c, tt = (n - 1) // TT, (n - 1) % TT
                    act.wait_ge(*written(("z", c, tt)))
                    act.dma_start(z_d[tt * P:(tt + 1) * P, c * 512:(c + 1) * 512],
                                  zbuf[:, (n - 1) % 4, :]).then_inc(z_out[(n - 1) % 4], 16)
            for s in z_out:
                act.wait_ge(s, 16 * 8)
            for n in range(2 * KT):
                g, j, slot = n // KT, n % KT, n % 2
                if n >= 2:
                    act.wait_ge(gate_out[slot], 16 * (n // 2))
                copy(gate_stage[:, slot, :], ("gate", g, j), func=ACT.Sigmoid)
                act.wait_ge(*written(("gate", g, j)))
                act.dma_start(gate_d[g, j], gate_stage[:, slot, :]).then_inc(gate_out[slot], 16)
                if n == 11:
                    act.wait_ge(dt_steps, 1)
                    act.activation(dtmp[1], dtmp[0], ACT.Exp, scale=-1.0)
                    act.wait_ge(rows_in, 16 * len(ROWS))
                    act.activation(r_alog, r_alog, ACT.Exp).then_inc(dt_steps, 1)
                    act.wait_ge(dt_steps, 3)
                    act.activation(dtmp[0], dtmp[2], ACT.Ln).then_inc(dt_steps, 1)
            for s in gate_out:
                act.wait_ge(s, 16 * KT)
            end_phase(act)
            act.wait_ge(phase_done, 4 * 1)

            for j in range(8):
                for half in range(2):
                    copy(kT[:, j, half * 512:half * 512 + 512], ("kT", j, half))

            def attend(units, base):
                n = len(units)
                for s in range(n + 3):
                    if s < n:
                        u, g = units[s], base + s
                        scores_ring, probs_ring, _ = rings_of(g)
                        act.wait_ge(*written(("S", g)))
                        if s >= 3:
                            act.wait_ge(*completed(("T", g - 3, last_group(units[s - 3]))))
                        w = u["nk"] * P
                        act.activation(probs_ring[g % 3][:, 0:w], scores_ring[g % 2][:, 0:w], ACT.Exp, scale=-1.0,
                                       bias=negmax[:, g % 4:g % 4 + 1],
                                       accum_out=rsum[:, g % 8:g % 8 + 1]).then_inc(exp_ready, 1)
                    if 0 <= s - 3 and units[s - 3]["ph"] == "a" and units[s - 3]["h"] == HEADS - 1:
                        i = units[s - 3]["i"]
                        for half in range(2):
                            copy(attT[:, 4 * half:4 * half + 4, i * P:(i + 1) * P], ("aT", i, half),
                                 psum_of(("aT", i, half)).rearrange("p (a b) -> p a b", b=P))
                        act.wait_ge(*written(("aT", i, 1)))
                        act.dma_start(attT_d.rearrange("p (k s) -> p k s", k=KT)[:, :, i * P:(i + 1) * P],
                                      attT[:, :, i * P:(i + 1) * P]).then_inc(attT_out, 16)
                    if 0 <= s - 1 < n:
                        u, g = units[s - 1], base + s - 1
                        if s - 1 >= 3:
                            act.wait_ge(*completed(("O", g - 3)))
                        pT = rings_of(g)[2][g % 3]
                        for grp in range(last_group(u) + 1):
                            w = min(4, u["nk"] - 4 * grp) * P
                            copy(pT[:, grp * 512:grp * 512 + w], ("T", g, grp), psum_of(("T", g, grp))[:, 0:w])

            attend(units1, 0)
            act.wait_ge(attT_out, 16 * TT)
            end_phase(act)
            act.wait_ge(phase_done, 4 * 2)

            act.wait_ge(back_in[0], 16)
            for k in range(KT):
                high_part(hBhi[k], hT[:, k, :])
            for j in range(XT):
                act.wait_ge(*written(("xc", j)))
                act.activation(xbc_at(j), xbc_at(j), ACT.Silu)
            end_phase(act)
            act.wait_ge(phase_done, 4 * 3)

            high_part(adt_parts[0], adt)
            NG = TT * GROUPS
            for n in range(NG + 4):
                c, g = n // GROUPS, n % GROUPS
                if n < NG:
                    if g == 0:
                        copy(btok[c % 2], ("bt", c))
                        if c >= 3:
                            act.wait_ge(*written(("yo", c - 2, GROUPS - 1)))
                        if c >= 2:
                            act.wait_ge(*written(("st", c - 2, GROUPS - 1)))
                        copy(decay_out[:, c % 2, :], ("ea", c), psum_of(("ea", c))[:, 0:2 * SSMH], ACT.Exp)
                    if n >= 2:
                        act.wait_ge(*completed(("yd", (n - 2) // GROUPS, (n - 2) % GROUPS)))
                    copy(mix[n % 2], ("sg", c, g), func=ACT.Exp)
                m = n - 2
                if 0 <= m < NG:
                    cc, gg = m // GROUPS, m % GROUPS
                    act.wait_ge(gated, m + 1)
                    ins = square_sum(("ssd", cc), yb[cc % 2][:, gg * 512:(gg + 1) * 512], junk, gg)
                    if gg == GROUPS - 1:
                        ins.then_inc(squared, 1)
                if n >= 6 and (n - 6) % GROUPS == 0:
                    cc = (n - 6) // GROUPS
                    act.wait_ge(*rooted(("ssd", cc)))
                    for gg in range(GROUPS):
                        y = yb[cc % 2][:, gg * 512:(gg + 1) * 512]
                        ins = act.activation(y, y, ACT.Copy, scale=stat_of(("ssd", cc), gg))
                    ins.then_inc(ynorm, 1)
                if n >= 7 and (n - 7) % GROUPS == 0:
                    cc = (n - 7) // GROUPS
                    for q in range(4):
                        act.wait_ge(*completed(("yt", cc, q)))
                        src = psum_of(("yt", cc, q))
                        for m in range(4):
                            ins = act.activation(yT[:, 4 * q + m, cc * P:(cc + 1) * P], src[:, m * P:(m + 1) * P], ACT.Copy,
                                                 scale=cols[:, 1, 4 * q + m:4 * q + m + 1])
                        ins.then_inc(empty(("yt", cc, q)), 1)
            end_phase(act)
            act.wait_ge(phase_done, 4 * 4)

            def gate_again(n):
                act.dma_start(gate, gate_d[n // KT, n % KT]).then_inc(gate_in, 16)

            gate_again(0)
            for k in range(2 * KT):
                high_part(yhi[k], yT[:, k, :])
            for j in range(KT):
                copy(mergedT[:, j, :], ("so", 0, j))
            for n in range(1, 2 * KT + 1):
                act.wait_ge(merged_ready, n)
                if n < 2 * KT:
                    gate_again(n)
                if n in (4, 5):
                    act.wait_ge(back_in[1], 16)
                    for k in range(4 * (n - 4), 4 * (n - 4) + 4):
                        high_part(ahi[k], attTd[:, k, :])
                if n > KT:
                    high_part(mhi[n - KT - 1], mergedT[:, n - KT - 1, :])
            end_phase(act)

            for n in range(TT + 1):
                if n < TT:
                    act.wait_ge(*written(("o", 1, n)))
                    square_sum(("h2", n), x1E[:, n, :], junkE).then_inc(squared, 1)
                    act.dma_start(x1_d[:, n * D:(n + 1) * D], x1E[:, n, :]).then_inc(x1_out, 16)
                if n >= 1:
                    scale_tile(("h2", n - 1), "h2", x1E[:, n - 1, :], hsE, n - 1)
            act.wait_ge(x1_out, 16 * TT)
            end_phase(act)

            act.wait_ge(*written(("h2", TT - 1, 1)))
            for k in range(KT):
                high_part(h2hi[k], h2T[:, k, :])
            for j in range(FT):
                act.wait_ge(*written(("ug", j)))
                g = actT[:, j, :]
                act.activation(g, g, ACT.Silu).then_inc(silu_made, 1)
            end_phase(act)
            act.wait_ge(phase_done, 4 * 7)

            act.dma_start(memx, t["mem_2"][0].rearrange("(a p) n -> p a n", p=P)).then_inc(mem_in, 16)
            act.dma_start(x1.rearrange("p a n -> p (a n)"), x1_d).then_inc(back_in[2], 16)
            for k in range(FT):
                if k >= 2:
                    act.wait_ge(dn_spent, down_step(0, k - 2))
                high_part(act_parts[0][k % 2][0], actT[:, k, :])
                if k == 3:
                    act.wait_ge(mem_in, 16)
                    for tt in range(2):
                        square_sum(("mem", tt), memx[:, tt, :], hs3[:, tt, :]).then_inc(squared, 1)
                    act.drain()
                if k == 14:
                    for tt in range(2):
                        scale_tile(("mem", tt), "mx", memx[:, tt, :], hs3, tt)
            act.wait_ge(*completed(("dn", 0, TT - 1)))
            nf = t["norm_final"]
            act.dma_start(nfb, bass.AP(nf.tensor, nf.offset, [[0, P], [1, D]])).then_inc(nf_in, 16)
            lv = t["diff_lambda_2"]
            act.dma_start(lamv, bass.AP(lv.tensor, lv.offset, [[0, P], [32, 4], [1, 32]])).then_inc(pos_in, 16)
            for n, name in enumerate(("mla_qn_g_2", "mla_kn_g_2")):
                act.dma_start(head_gain[0:NOPE, n:n + 1], t[name][0, 0:NOPE].rearrange("(p o) -> p o", o=1),
                              allow_slow_non_contiguous=True).then_inc(pos_in, 16)
            act.dma_start(pos_i, t["positions_2"][0].rearrange("(a p) -> p a", p=P),
                          allow_slow_non_contiguous=True).then_inc(pos_in, 16)
            act.wait_ge(*completed(("mx", 1, 1)))
            act.drain()
            for k in range(FT):
                if k >= 2:
                    act.wait_ge(dn_spent, down_step(1, k - 2))
                high_part(act_parts[1][k % 2][0], actT[:, k, :])
                if k == 1:
                    for tt in range(2):
                        copy(memkv[:, tt, :], ("mem", tt))
                if k == 12:
                    act.wait_ge(angle, 1)
                    act.activation(trigT[3], trigT[1], ACT.Sin)
                    act.activation(trigT[4], trigT[1], ACT.Sin, scale=0.5)
                    act.activation(lam[:, 2:4], lam[:, 0:2], ACT.Exp).then_inc(trig, 1)
            copy(kmT.rearrange("p a b -> p (a b)"), ("kmT",))
            act.wait_ge(*completed(("dn", 1, TT - 1)))
            for n in range(TT + 3):
                if n < TT:
                    act.wait_ge(*written(("dn", 1, n)))
                    square_sum(("x3", n), x1[:, n, :], junkG).then_inc(squared, 1)
                if 2 <= n < TT + 2:
                    act.wait_ge(resid, n - 1)
                    act.dma_start(x3_d[:, (n - 2) * D:(n - 1) * D], x1[:, n - 2, :]).then_inc(x3_out, 16)
                    square_sum(("h3", n - 2), x1[:, n - 2, :], junkG).then_inc(squared, 1)
                if n >= 3:
                    if n < 5:
                        act.wait_ge(*completed(("mx", n - 3, 1)))
                    scale_tile(("h3", n - 3), "h3", x1[:, n - 3, :], hs3, n - 3)
            act.drain()
            act.wait_ge(x3_out, 16 * TT)
            act.wait_ge(*written(("h3", TT - 1, 1)))
            for k in range(KT):
                high_part(h3hi[k], h3T[:, k, :])
            for c in range(len(IN2)):
                for tt in range(TT):
                    name = ("in2", c, tt)
                    if c == 0:
                        copy(pA[:, tt, :], name, psum_of(name)[:, 0:416])
                    elif c < 3:
                        copy(pB[:, tt, 512 * (c - 1):512 * c], name)
                    else:
                        copy(pZ[:, tt, 512 * (c - 3):512 * (c - 2)], name, func=ACT.Silu)
            for x in (0, 1, 2, 3, 6, 7):
                for half in range(2):
                    name = ("dT", x, half)
                    scale = -DD ** -0.5 if x < 2 else 1.0 if x < 4 else -64 ** -0.5
                    copy(pB[:, 4 * half:4 * half + 4, x * P:(x + 1) * P], name,
                         psum_of(name).rearrange("p (a b) -> p a b", b=P), scale=scale)
            end_phase(act)
            act.wait_ge(phase_done, 4 * 8)
            for k in range(3):
                for half in range(2):
                    dst = cqT[:, k, :] if k < 2 else ckv2T
                    copy(dst[:, half * 512:half * 512 + 512], ("cqT", k, half), scale=cols[:, 1, 40 + k:41 + k])
            for tt in range(TT + 1):
                if tt < TT:
                    if tt >= 2:
                        act.wait_ge(*completed(("qTm", tt - 2, 1)))
                    act.wait_ge(*completed(("uq", tt)))
                    src = psum_of(("uq", tt))[:, 0:768]
                    act.activation(qtok[tt % 2], src, ACT.Copy)
                    act.drain()
                    act.activation(src, src, ACT.Square).then_inc(sq_made, 1)
                    if tt >= 2:
                        act.wait_ge(*completed(("kTm", tt - 2, 1)))
                    act.wait_ge(*completed(("ukv", tt)))
                    src = psum_of(("ukv", tt)).rearrange("p (h c) -> p h c", c=128)
                    kh = ktok[tt % 2].rearrange("p (h c) -> p h c", c=MQK)
                    act.activation(vM[:, tt, :].rearrange("p (h c) -> p h c", c=64), src[:, :, 64:128], ACT.Copy)
                    act.activation(kh[:, :, 64:96], bc(pA[:, tt, 384:416], MLAH, 1), ACT.Copy)
                    act.activation(kh[:, :, 0:64], src[:, :, 0:64], ACT.Copy)
                    act.drain()
                    act.activation(src[:, :, 0:96], kh, ACT.Square).then_inc(sq_made, 1)
                if tt == 0:
                    continue
                for n, (key, dst) in enumerate((("qTm", qTm), ("kTm", kTm))):
                    for half in range(2):
                        name = (key, tt - 1, half)
                        copy(dst[0:MQK, 4 * half:4 * half + 4, (tt - 1) * P:tt * P], name,
                             psum_of(name)[0:MQK, :].rearrange("p (a b) -> p a b", b=P), scale=head_gain[0:MQK, n:n + 1])
            end_phase(act)
            act.wait_ge(phase_done, 4 * 9)
            attend(units2, N1)
            end_phase(act)
            act.wait_ge(phase_done, 4 * 10)
            act.dma_start(xo.rearrange("p a n -> p (a n)"), x3_d).then_inc(back_in[3], 16)
            for tt in range(TT):
                for half in range(2):
                    name = ("yT2", tt, half)
                    copy(yT2[:, 4 * half:4 * half + 4, tt * P:(tt + 1) * P], name,
                         psum_of(name).rearrange("p (a b) -> p a b", b=P))
            act.drain()
            for k in range(KT):
                high_part(y2hi[k], yT2[:, k, :])

        @block.vector
        def _(dve):
            def tt_(out, a, b, op):
                return dve.tensor_tensor(out=out, in0=a, in1=b, op=op)

            def stt(out, a, scalar, b, op0, op1):
                return dve.scalar_tensor_tensor(out=out, in0=a, scalar=scalar, in1=b, op0=op0, op1=op1)

            def mean(name, n):
                v = stat_of(name)
                dve.tensor_scalar(v, v, 1.0 / n, EPS, ALU.mult, ALU.add).then_inc(mean_ready, 1)

            def heads(ap, n):
                return ap.rearrange("p (h c) -> p h c", h=n)

            def with_gain(key, dst, m, col, tiles):
                for tt in tiles:
                    for half in range(2):
                        dve.wait_ge(*completed((key, tt, half)))
                        src = psum_of((key, tt, half)).rearrange("p (a b) -> p a b", b=P)
                        g = cols[:, m, col + 4 * half:col + 4 * half + 4]
                        tt_(dst[:, 4 * half:4 * half + 4, tt * P:(tt + 1) * P], src, bc(g, P), ALU.mult).then_inc(empty((key, tt, half)), 1)

            def low_part(name, out, src, high_part):
                dve.wait_ge(*high(name))
                return tt_(out, src, high_part.bitcast(F32), ALU.subtract).then_inc(parts_made, 1)

            for b in range(8):
                dve.sem_inc(evacuated[b], 1)
            dve.wait_ge(*completed("cols"))
            src = psum_of("cols")
            for m, r in enumerate(COL_ROWS):
                ins = dve.tensor_copy(cols[:, m, 0:r], src[:, m * P:m * P + r])
            ins.then_inc(empty("cols"), 1)
            dve.wait_ge(*completed("bias"))
            dve.tensor_copy(bias_row[0:HEADS, :], psum_of("bias")[0:HEADS, 0:384]).then_inc(empty("bias"), 1)
            dve.drain()
            for n in range(TT):
                dve.wait_ge(squared, squared_n[("x", n)])
                mean(("x", n), D)
            with_gain("hx", hT, 0, 120, range(TT))

            dve.wait_ge(*written(("c", TT - 1)))
            c_lat = craw[:, :, 0:LAT]
            sq = rel[:, 0, :].rearrange("p (a b) -> p a b", b=LAT)
            tt_(sq, c_lat, c_lat, ALU.mult)
            dve.drain()
            dve.reduce_sum(stat_of("ckv"), sq, axis=AX.X)
            dve.drain()
            mean("ckv", LAT)
            dve.wait_ge(*rooted("ckv"))
            tt_(c_lat, c_lat, bc(stat_of("ckv"), LAT), ALU.mult).then_inc(heads_ready, 1)

            n = 0
            for i in range(2, TT):
                nk = (i + 1) * P
                sc = scores[:, score_off[i]:score_off[i] + nk]
                for h in range(IDXH):
                    dve.wait_ge(*written(("ix", i, h)))
                    w = craw[:, i, LAT + h:LAT + h + 1]
                    if h == 0:
                        dve.tensor_scalar(sc, rel[:, n % 2, 0:nk], w, None, ALU.mult).then_inc(relu_used, 1)
                    else:
                        stt(sc, rel[:, n % 2, 0:nk], w, sc, ALU.mult, ALU.add).then_inc(relu_used, 1)
                    dve.drain()
                    n += 1
                tt_(sc[:, nk - P:nk], sc[:, nk - P:nk], future, ALU.add)
                dve.drain()
            dve.wait_ge(hT_out, 16)
            for k in range(KT):
                low_part(("hA", k), hAlo[k], hT[:, k, :], hAhi[k])
            score_rows = [scores[:, score_off[i]:score_off[i] + (i + 1) * P] for i in range(2, TT)]
            with dve.Fori(0, TOPK // 8):
                for n, sc in enumerate(score_rows):
                    dve.max(top8[:, n, :], sc)
                dve.drain()
                for n, sc in enumerate(score_rows):
                    dve.match_replace(sc, top8[:, n, :], sc, TAKEN)
                dve.drain()
            for i, sc in enumerate(score_rows, 2):
                dve.tensor_scalar(negmask[:, score_off[i]:score_off[i] + (i + 1) * P], sc, SPLIT, BIG, ALU.is_gt, ALU.mult)
            dve.wait_ge(rows_in, 16 * len(ROWS))
            f0, f1, f2, f3 = dtmp
            tt_(dt, craw[:, :, LAT + IDXH:LAT + IDXH + SSMH], bc(r_dtb, TT, 1), ALU.add)
            dve.drain()
            v3 = lambda f: f.rearrange("p (a b) -> p a b", b=SSMH)
            stt(v3(f0), dt, -1.0, dt, ALU.mult, ALU.max)
            dve.tensor_scalar(dt, dt, 0.0, None, ALU.max)
            dve.drain()
            dve.sem_inc(dt_steps, 1)
            dve.wait_ge(dt_steps, 2)
            dve.tensor_scalar(f2, f1, 1.0, None, ALU.add)
            dve.drain()
            dve.tensor_scalar(f3, f2, 1.0, None, ALU.subtract).then_inc(dt_steps, 1)
            dve.wait_ge(dt_steps, 4)
            dve.drain()
            dve.tensor_scalar(f2, f3, 0.0, None, ALU.is_equal)
            dve.drain()
            tt_(f3, f3, f2, ALU.add)
            dve.drain()
            dve.reciprocal(f3, f3)
            dve.drain()
            tt_(f0, f0, f3, ALU.mult)
            dve.drain()
            tt_(f0, f0, f2, ALU.add)
            dve.drain()
            tt_(f0, f0, f1, ALU.mult)
            dve.drain()
            tt_(dt, dt, v3(f0), ALU.add)
            dve.drain()
            stt(adt, dt, -1.0, bc(r_alog, TT, 1), ALU.mult, ALU.mult)
            end_phase(dve)
            dve.wait_ge(phase_done, 4 * 1)

            for tt in range(TT):
                for half in range(2):
                    dve.wait_ge(*completed(("v", tt, half)))
                    dve.tensor_copy(v[:, tt, half * 512:half * 512 + 512], psum_of(("v", tt, half))).then_inc(empty(("v", tt, half)), 1)
            dve.wait_ge(bias_in, 16)

            def attend(units, base, between={}):
                n = len(units)
                for s in range(n + 3):
                    if s in between:
                        between[s]()
                    if s < n:
                        u, g = units[s], base + s
                        w = u["nk"] * P
                        dve.wait_ge(*completed(("S", g)))
                        out = psum_of(("S", g))
                        if u["ph"] == "a":
                            lo = max(0, w - 256)
                            tt_(out[:, lo:w], out[:, lo:w], biasT[:, u["h"], 256 - (w - lo):256], ALU.subtract)
                            dve.drain()
                        if g >= 2:
                            dve.wait_ge(exp_ready, g - 1)
                        dve.tensor_tensor_reduce(
                            out=rings_of(g)[0][g % 2][:, 0:w], in0=out[:, 0:w], in1=u["mask"], scale=1.0, scalar=3e38,
                            op0=ALU.add, op1=ALU.min, accum_out=negmax[:, g % 4:g % 4 + 1]).then_inc(empty(("S", g)), 1)
                    if s >= 3:
                        u, g = units[s - 3], base + s - 3
                        i, h = u["i"], u["h"]
                        dve.wait_ge(exp_ready, g + 1)
                        r = rinv[:, g % 8:g % 8 + 1]
                        dve.reciprocal(r, rsum[:, g % 8:g % 8 + 1])
                        dve.drain()
                        dve.wait_ge(*completed(("O", g)))
                        o = psum_of(("O", g))[:, 0:64]
                        if u["ph"] == "a":
                            if h == 0 and i:
                                dve.wait_ge(*completed(("aT", i - 1, 1)))
                            ins = dve.tensor_scalar(att[:, 0, h * 64:h * 64 + 64], o, r, None, ALU.mult)
                        elif u["ph"] == "m":
                            z = pZ[:, i, h * 64:h * 64 + 64]
                            ins = stt(z, o, r, z, ALU.mult, ALU.mult)
                        elif u["ph"] == "e":
                            z = pZ[:, i, 768 + h * 64:832 + h * 64]
                            ins = stt(z, o, r, z, ALU.mult, ALU.mult)
                        else:
                            d = od[:, i, (h // 2) * 64:(h // 2) * 64 + 64]
                            if h % 2 == 0:
                                ins = dve.tensor_scalar(d, o, r, None, ALU.mult)
                            else:
                                tt_(r, r, lam[:, 4:5], ALU.mult)
                                dve.drain()
                                ins = stt(d, o, r, d, ALU.mult, ALU.add)
                        ins.then_inc(empty(("O", g)), 1)

            attend(units1, 0)
            end_phase(dve)
            dve.wait_ge(phase_done, 4 * 2)

            for k in range(KT):
                low_part(("hB", k), hBlo[k], hT[:, k, :], hBhi[k])
            for j in range(XT):
                dve.wait_ge(*completed(("xc", j)))
                a, u = xbc_at(j), psum_of(("xc", j))
                dve.tensor_scalar(a, u, cols[:, 0, 3 * XT + j:3 * XT + j + 1],
                                  cols[:, 0, CONV * XT + j:CONV * XT + j + 1], ALU.mult, ALU.add)
                for m in (2, 1, 0):
                    dve.drain()
                    ins = stt(a[:, 3 - m:S], u[:, 0:S - 3 + m], cols[:, 0, m * XT + j:m * XT + j + 1], a[:, 3 - m:S],
                              ALU.mult, ALU.add)
                ins.then_inc(empty(("xc", j)), 1)
            end_phase(dve)
            dve.wait_ge(phase_done, 4 * 3)

            low_part(("adt", 0), adt_parts[1], adt, adt_parts[0])
            NG = TT * GROUPS
            tri4 = bc(tri[:, :], GROUPS, 1)

            def ssd_front(c):
                for g in range(GROUPS):
                    dve.wait_ge(*completed(("xt", c, g)))
                    src = heads(psum_of(("xt", c, g)), HPG)
                    span = slice(g * 512, (g + 1) * 512)
                    hs_ = slice(HPG * g, HPG * (g + 1))
                    if g == 0 and c >= 2:
                        dve.wait_ge(*completed(("yt", c - 2, 3)))
                    tt_(heads(yb[c % 2][:, span], HPG), src, bc(r_dskip[:, hs_], 64), ALU.mult)
                    tt_(heads(xdt[c % 2][:, span], HPG), src, bc(dt[:, c, hs_], 64), ALU.mult).then_inc(empty(("xt", c, g)), 1)
                dve.wait_ge(*completed(("cb", c)))
                tt_(heads(cbm[c % 2], GROUPS), heads(psum_of(("cb", c)), GROUPS), tri4, ALU.mult).then_inc(empty(("cb", c)), 1)
                dve.drain()

            def ssd_mix(n):
                c, g = n // GROUPS, n % GROUPS
                dve.wait_ge(*written(("sg", c, g)))
                m = heads(mix[n % 2], HPG)
                tail = m[:, :, P - 1:P].broadcast_to([P, HPG, 64])
                if c < TT - 1:
                    if n >= 2:
                        dve.wait_ge(*completed(("st", (n - 2) // GROUPS, (n - 2) % GROUPS)))
                    tt_(heads(xds[n % 2], HPG), heads(xdt[c % 2][:, g * 512:(g + 1) * 512], HPG), tail, ALU.mult)
                    dve.drain()
                tt_(m, m, bc(cbm[c % 2][:, g * P:(g + 1) * P], HPG, 1), ALU.mult).then_inc(mixed, 1)

            def ssd_tail(n):
                c, g = n // GROUPS, n % GROUPS
                span = slice(g * 512, (g + 1) * 512)
                hs_ = slice(HPG * g, HPG * (g + 1))
                y = yb[c % 2][:, span]
                dve.wait_ge(*completed(("yd", c, g)))
                tt_(y, y, psum_of(("yd", c, g)), ALU.add).then_inc(empty(("yd", c, g)), 1)
                dve.wait_ge(*written(("ea", c)))
                h = state[:, span]
                if c:
                    dve.wait_ge(*completed(("yo", c, g)))
                    tt_(heads(yoff, HPG), heads(psum_of(("yo", c, g)), HPG), bc(decay_out[:, c % 2, hs_], 64),
                             ALU.mult).then_inc(empty(("yo", c, g)), 1)
                    dve.drain()
                    tt_(y, y, yoff, ALU.add).then_inc(y_summed, 1)
                if c < TT - 1:
                    dve.wait_ge(*completed(("st", c, g)))
                    if c:
                        dve.wait_ge(state_decayed, n - GROUPS + 1)
                    src = psum_of(("st", c, g))
                    (tt_(h, h, src, ALU.add) if c else dve.tensor_copy(h, src)).then_inc(empty(("st", c, g)), 1)
                dve.drain()

            for n in range(NG + 3):
                c, g = n // GROUPS, n % GROUPS
                if n >= 6 and (n - 6) % GROUPS == 0:
                    cc = (n - 6) // GROUPS
                    dve.wait_ge(squared, squared_n[("ssd", cc)])
                    mean(("ssd", cc), INNER // GROUPS)
                if n < NG:
                    if g == 0:
                        ssd_front(c)
                    ssd_mix(n)
                if 1 <= n <= NG:
                    ssd_tail(n - 1)
            end_phase(dve)
            dve.wait_ge(phase_done, 4 * 4)

            for k in range(2 * KT):
                low_part(("y", k), ylo[k], yT[:, k, :], yhi[k])
            for j in range(KT):
                m = mergedT[:, j, :]
                dve.wait_ge(*written(("so", 0, j)))
                dve.wait_ge(*completed(("so", 1, j)))
                tt_(m, m, psum_of(("so", 1, j)), ALU.add).then_inc(empty(("so", 1, j)), 1)
                dve.drain()
                dve.wait_ge(gate_in, 16 * (j + 1))
                tt_(m, m, gate, ALU.mult).then_inc(merged_ready, 1)
                if j in (4, 5):
                    for k in range(4 * (j - 4), 4 * (j - 4) + 4):
                        low_part(("att", k), alo[k], attTd[:, k, :], ahi[k])
            for j in range(KT + 1):
                if j < KT:
                    m = mergedT[:, j, :]
                    dve.wait_ge(gate_in, 16 * (KT + j + 1))
                    dve.wait_ge(*completed(("ao", j)))
                    tt_(gate, gate, psum_of(("ao", j)), ALU.mult).then_inc(empty(("ao", j)), 1)
                    dve.drain()
                    tt_(m, m, gate, ALU.add).then_inc(merged_ready, 1)
                if j >= 1:
                    low_part(("m", j - 1), mlo[j - 1], mergedT[:, j - 1, :], mhi[j - 1])
            end_phase(dve)

            def add_to(x, key, c, tt):
                part = x[:, tt, c * 512:(c + 1) * 512]
                dve.wait_ge(*completed((key, c, tt)))
                tt_(part, part, psum_of((key, c, tt)), ALU.add).then_inc(empty((key, c, tt)), 1)

            dve.wait_ge(x_again, 16)
            for tt in range(TT):
                add_to(x1E, "o", 0, tt)
            for n in range(TT + 5):
                if n < TT:
                    add_to(x1E, "o", 1, n)
                if 1 <= n <= TT:
                    dve.wait_ge(squared, squared_n[("h2", n - 1)])
                    mean(("h2", n - 1), D)
                if n >= 5:
                    with_gain("h2", h2T, 1, 16, [n - 5])
            end_phase(dve)

            for k in range(KT):
                low_part(("h2", k), h2lo[k], h2T[:, k, :], h2hi[k])
            dve.wait_ge(phase_done, 4 * 6)

            def gate_times_value(j):
                dve.wait_ge(silu_made, j + 1)
                tt_(actT[:, j, :], actT[:, j, :], accF[j % 2], ALU.mult)

            for j in range(FT):
                pair = [(actT[:, j, :], ("ug", j), j), (accF[j % 2], ("uv", j), FT + j)]
                for a, name, ch in pair:
                    dve.wait_ge(*completed(name))
                    u = psum_of(name)
                    dve.tensor_scalar(a, u, cols[:, 3, ch:ch + 1], cols[:, 1, 44 + ch:45 + ch], ALU.mult, ALU.add)
                    dve.drain()
                    if name[0] == "ug" and j >= 1:
                        gate_times_value(j - 1)
                    for m in (1, 0):
                        if m == 0:
                            dve.drain()
                        ins = stt(a[:, 2 - m:S], u[:, 0:S - 2 + m], cols[:, 2, 44 * m + ch:44 * m + ch + 1], a[:, 2 - m:S],
                                  ALU.mult, ALU.add)
                    ins.then_inc(empty(name), 1)
            dve.drain()
            gate_times_value(FT - 1)
            end_phase(dve)

            for k in range(FT):
                hi, lo = act_parts[0][k % 2]
                low_part(("act", 0, k), lo, actT[:, k, :], hi)
                if k == 5:
                    for tt in range(2):
                        dve.wait_ge(squared, squared_n[("mem", tt)])
                        mean(("mem", tt), D)
            dve.wait_ge(back_in[2], 16)
            for tt in range(TT):
                add_to(x1, "dn", 0, tt)
            with_gain("mx", memT, 1, 32, range(2))
            for k in range(2):
                hi, lo = act_parts[1][k % 2]
                low_part(("act", 1, k), lo, actT[:, k, :], hi)
            dve.wait_ge(*written(("mem", 1)))
            km = memkv[:, :, 0:256].rearrange("p a (h c) -> p a h c", c=64)
            sq4 = dsq[:, 0:512].rearrange("p (a h c) -> p a h c", a=2, c=64)
            tt_(sq4, km, km, ALU.mult)
            dve.drain()
            dve.reduce_sum(stat_of("memk"), dsq[:, 0:512].rearrange("p (a c) -> p a c", c=64), axis=AX.X)
            dve.drain()
            mean("memk", 64)
            dve.wait_ge(*rooted("memk"))
            r = stat_of("memk").rearrange("p (a h) -> p a h", a=2)
            for tt in range(2):
                tt_(km[:, tt], km[:, tt], bc(r[:, tt], 64), ALU.mult)
            dve.drain()
            for tt in range(2):
                ins = tt_(km[:, tt], km[:, tt], bc(r_mkn, 4, 1), ALU.mult)
            ins.then_inc(sq_ready, 1)
            dve.wait_ge(pos_in, 64)
            dve.tensor_scalar(head_gain[:, 0:1], head_gain[:, 0:1], -MQK ** -0.5, None, ALU.mult)
            freq = np.power(np.float32(THETA), -np.arange(0, ROPE, 2, dtype=np.float32) / np.float32(ROPE))
            for n in range(ROPE // 2):
                dve.memset(invf[:, n:n + 1], float(freq[n]))
            dve.tensor_copy(posf, pos_i)
            dve.drain()
            ang, red, turns = trigT[0], trigT[1], trigT[2]
            tt_(ang, bc(posf, 16), bc(invf, TT, 1), ALU.mult)
            dve.drain()
            magic = 1.5 * 2.0 ** 23
            dve.tensor_scalar(turns, ang, 1.0 / (2.0 * math.pi), magic, ALU.mult, ALU.add)
            dve.drain()
            dve.tensor_scalar(turns, turns, magic, None, ALU.subtract)
            dve.drain()
            c1, c2 = 6.28125, 0.0019350051879882812
            for k, (to, frm) in zip((c1, c2, 2.0 * math.pi - c1 - c2), ((red, ang), (red, red), (red, red))):
                stt(to, turns, -k, frm, ALU.mult, ALU.add)
                dve.drain()
            dve.tensor_scalar(red, red, 3.1415925, -3.1415925, ALU.min, ALU.max)
            for n in range(2):
                dve.tensor_tensor_reduce(out=dsq[:, 32 * n:32 * n + 32], in0=lamv[:, 2 * n, :], in1=lamv[:, 2 * n + 1, :],
                                         scale=1.0, scalar=0.0, op0=ALU.mult, op1=ALU.add, accum_out=lam[:, n:n + 1])
            dve.drain()
            dve.sem_inc(angle, 1)
            for k in range(2, FT):
                hi, lo = act_parts[1][k % 2]
                low_part(("act", 1, k), lo, actT[:, k, :], hi)
                if k == 18:
                    dve.wait_ge(trig, 1)
                    dve.tensor_copy(sinb, trigT[3])
                    tt_(trigT[0], trigT[4], trigT[4], ALU.mult)
                    tt_(lam[:, 4:5], lam[:, 3:4], lam[:, 2:3], ALU.subtract)
                    dve.drain()
                    dve.tensor_scalar(cosb, trigT[0], -2.0, 1.0, ALU.mult, ALU.add)
                    dve.tensor_scalar(lam[:, 4:5], lam[:, 4:5], LAM0, None, ALU.subtract)
                    dve.drain()
            for tt in range(TT):
                add_to(x1, "dn", 1, tt)
            dve.wait_ge(nf_in, 16)
            for n in range(TT + 5):
                if n < TT:
                    dve.wait_ge(squared, squared_n[("x3", n)])
                    mean(("x3", n), D)
                if 1 <= n < TT + 1:
                    dve.wait_ge(*rooted(("x3", n - 1)))
                    stt(x1[:, n - 1, :], x1[:, n - 1, :], stat_of(("x3", n - 1), 0), nfb, ALU.mult, ALU.mult)\
                        .then_inc(resid, 1)
                if 2 <= n < TT + 2:
                    dve.wait_ge(squared, squared_n[("h3", n - 2)])
                    mean(("h3", n - 2), D)
                if n >= 5:
                    with_gain("h3", h3T, 1, 24, [n - 5])
            for k in range(KT):
                low_part(("h3", k), h3lo[k], h3T[:, k, :], h3hi[k])
            for tt in range(TT):
                dve.wait_ge(*written(("in2", 0, tt)))
                for k, (lo, hi) in enumerate(((0, 256), (256, 384))):
                    dve.tensor_tensor_reduce(out=dsq[:, lo:hi], in0=pA[:, tt, lo:hi], in1=pA[:, tt, lo:hi], scale=1.0,
                                             scalar=0.0, op0=ALU.mult, op1=ALU.add, accum_out=stat_of("cc", TT * k + tt))
                dve.drain()
            cc = stat_of("cc")
            dve.tensor_scalar(cc[:, 0:TT], cc[:, 0:TT], 1.0 / 256, None, ALU.mult)
            dve.tensor_scalar(cc[:, TT:2 * TT], cc[:, TT:2 * TT], 1.0 / 128, None, ALU.mult)
            dve.drain()
            mean("cc", 1)
            dve.wait_ge(*rooted("cc"))
            tt_(pA[:, :, 0:256], pA[:, :, 0:256], bc(cc[:, 0:TT], 256), ALU.mult)
            tt_(pA[:, :, 256:384], pA[:, :, 256:384], bc(cc[:, TT:2 * TT], 128), ALU.mult).then_inc(heads_ready, 1)

            def rotate(x, tt, n, tmp):
                c = cosb[:, tt, :].unsqueeze(1).unsqueeze(1).broadcast_to([P, n, 2, 16])
                s = sinb[:, tt, :].unsqueeze(1).unsqueeze(1).broadcast_to([P, n, 2, 16])
                tm = tmp[:, 0:n * 32].rearrange("p (h a c) -> p h a c", a=2, c=16)
                tt_(tm, x, s, ALU.mult)
                tt_(x, x, c, ALU.mult)
                dve.drain()
                tt_(x[:, :, 0, :], x[:, :, 0, :], tm[:, :, 1, :], ALU.subtract)
                return tt_(x[:, :, 1, :], x[:, :, 1, :], tm[:, :, 0, :], ALU.add)

            for tt in range(TT):
                dve.wait_ge(*written(("in2", 1, tt)))
                d = pB[:, tt, 0:512]
                tt_(dsq[:, 0:512], d, d, ALU.mult)
                dve.drain()
                dve.reduce_sum(stat[:, 98 + 16 * tt:114 + 16 * tt], heads(dsq[:, 0:512], 16), axis=AX.X)
                dve.drain()
            mean_dd = stat_of("dd")
            mean("dd", DD)
            dve.wait_ge(*rooted("dd"))
            for tt in range(TT):
                d = heads(pB[:, tt, 0:512], 16)
                tt_(d, d, bc(mean_dd[:, 16 * tt:16 * tt + 16], DD), ALU.mult)
                dve.drain()
                tt_(d[:, 0:8], d[:, 0:8], bc(r_dqn, 8, 1), ALU.mult)
                tt_(d[:, 8:16], d[:, 8:16], bc(r_dkn, 8, 1), ALU.mult)
                dve.drain()
                rotate(pB[:, tt, 0:512].rearrange("p (h a c) -> p h a c", a=2, c=16), tt, 16, dsq)
                dve.drain()
            for tt in range(TT):
                dve.wait_ge(*written(("in2", 2, tt)))
                q = pB[:, tt, 768:1024]
                tt_(dsq[:, 0:256], q, q, ALU.mult)
                dve.drain()
                dve.reduce_sum(stat[:, 16 + 4 * tt:20 + 4 * tt], heads(dsq[:, 0:256], 4), axis=AX.X)
                dve.drain()
            dve.drain()
            mean("mqm", 64)
            dve.wait_ge(*rooted("mqm"))
            for tt in range(TT):
                q = heads(pB[:, tt, 768:1024], 4)
                tt_(q, q, bc(stat_of("mqm")[:, 4 * tt:4 * tt + 4], 64), ALU.mult)
            dve.drain()
            for tt in range(TT):
                q = heads(pB[:, tt, 768:1024], 4)
                ins = tt_(q, q, bc(r_mqn, 4, 1), ALU.mult)
            ins.then_inc(heads_ready, 1)
            dve.drain()
            end_phase(dve)

            def head_squares(tt):
                for n, (key, name, w) in enumerate((("mq", ("uq", tt), MQK), ("mk", ("ukv", tt), 128))):
                    squares = psum_of(name)[:, 0:MLAH * w].rearrange("p (h c) -> p h c", c=w)[:, :, 0:MQK]
                    dve.wait_ge(sq_made, 2 * tt + n + 1)
                    dve.reduce_sum(stat_of((key, tt)), squares, axis=AX.X).then_inc(empty(name), 1)
                    dve.drain()
                    mean((key, tt), MQK)

            head_squares(0)
            for tt in range(TT):
                sides = (("mq", qtok[tt % 2], r_qn), ("mk", ktok[tt % 2], r_kn))
                for key, x, gain in sides:
                    xh = heads(x, MLAH)
                    dve.wait_ge(*rooted((key, tt)))
                    tt_(xh, xh, bc(stat_of((key, tt)), MQK), ALU.mult)
                    dve.drain()
                    tt_(xh[:, :, NOPE:MQK], xh[:, :, NOPE:MQK], bc(gain[:, NOPE:MQK], MLAH, 1), ALU.mult)
                    dve.drain()
                    rotate(xh[:, :, 64:96].rearrange("p h (a c) -> p h a c", a=2), tt, MLAH, htmp).then_inc(heads_ready, 1)
                    dve.drain()
                if tt < TT - 1:
                    head_squares(tt + 1)
            end_phase(dve)
            dve.wait_ge(phase_done, 4 * 9)

            def by_head(x, a):
                return x[:, 2 * a:2 * a + 2, :].rearrange("p a (h c) -> p (a h) c", c=64)

            def sub_squares(a):
                dve.drain()
                tt_(odsq[:, 2 * a:2 * a + 2, :], od[:, 2 * a:2 * a + 2, :], od[:, 2 * a:2 * a + 2, :], ALU.mult)
                dve.drain()
                dve.reduce_sum(stat_of("sub")[:, 8 * a:8 * a + 8], by_head(odsq, a), axis=AX.X)
                if a == TT // 2 - 1:
                    dve.drain()
                    mean("sub", 64)

            def sub_scale(a):
                o3, zd = by_head(od, a), pZ[:, 2 * a:2 * a + 2, 512:768]
                dve.wait_ge(*rooted("sub"))
                tt_(o3, o3, bc(stat_of("sub")[:, 8 * a:8 * a + 8], 64), ALU.mult)
                dve.drain()
                tt_(o3, o3, bc(r_sub, 8, 1), ALU.mult)
                dve.drain()
                stt(zd, od[:, 2 * a:2 * a + 2, :], 1.0 - LAM0, zd, ALU.mult, ALU.mult)

            after_diff = TT * (MLAH + DH) + 3
            between = {after_diff + a: lambda a=a: sub_squares(a) for a in range(TT // 2)}
            between.update({after_diff + 10 + a: lambda a=a: sub_scale(a) for a in range(TT // 2)})
            attend(units2, N1, between)
            end_phase(dve)
            dve.wait_ge(phase_done, 4 * 10)

            for k in range(KT):
                low_part(("y2", k), y2lo[k], yT2[:, k, :], y2hi[k])
            dve.wait_ge(back_in[3], 16)
            for c in range(2):
                for tt in range(TT):
                    add_to(xo, "o2", c, tt)



_INS = ["x", "rel_bias", "norm_mix", "w_in", "kv_norm", "w_uk", "w_uv", "conv_ssm_w", "conv_ssm_b", "dt_bias",
        "a_log", "d_skip", "ssm_norm", "w_att_out", "w_ssm_out", "w_out", "norm_ffn", "w_ffn_up", "conv_ffn_w",
        "conv_ffn_b", "w_ffn_down", "norm_final", "mem_2", "positions_2", "norm_g_2", "w_in_2", "mla_q_norm_g_2",
        "mla_kv_norm_g_2", "w_uq_2", "w_ukv_2", "mla_qn_g_2", "mla_kn_g_2", "diff_qn_g_2", "diff_kn_g_2",
        "diff_lambda_2", "diff_subln_g_2", "mem_norm_g_2", "w_mem_kv_2", "mem_qn_g_2", "mem_kn_g_2", "w_out_2"]


def kernel(**inputs):
    import concourse.bacc as bacc
    from concourse.bass_utils import run_bass_kernel_spmd

    nc = bacc.Bacc("TRN2", target_bir_lowering=False, num_devices=1)
    arrays = {name: np.ascontiguousarray(inputs[name]) for name in _INS}
    arrays["buckets"] = bucket_table()
    t = {name: nc.dram_tensor(f"in_{name}", a.shape, mybir.dt.from_np(a.dtype), kind="ExternalInput").ap()
         for name, a in arrays.items()}
    t["out"] = nc.dram_tensor("out_0", (1, S, D), F32, kind="ExternalOutput").ap()
    hybrid_two_blocks(nc, t)
    r = run_bass_kernel_spmd(nc, [{f"in_{name}": a for name, a in arrays.items()}], core_ids=[0])
    return r.results[0]["out_0"]
```
